# Optimizing a Trainium2 kernel written in Bass

```python
import math
import jax, jax.numpy as jnp
from jax import lax
import numpy as np

D_MODEL = 1024
BATCH = 1
SEQ = 512
DEPTH = 1

HEAD_DIM = 64
N_ATT_HEADS = 12
ATT_WIDTH = N_ATT_HEADS * HEAD_DIM
DILATED_PATTERNS = ((128, 1), (512, 4), (2048, 16))
ATT_BLOCK = 128
SSM_EXPAND = 2
SSM_INNER = SSM_EXPAND * D_MODEL
SSM_HEAD_DIM = 64
SSM_HEADS = SSM_INNER // SSM_HEAD_DIM
SSM_GROUPS = 8
SSM_STATE = 128
SSM_CONV = 4
SSM_CHUNK = 128
CONV_DIM = SSM_INNER + 2 * SSM_GROUPS * SSM_STATE
FFN_HIDDEN = 4 * D_MODEL
N_BRANCHES = 2
IN_SPLITS = (ATT_WIDTH, ATT_WIDTH, ATT_WIDTH, SSM_INNER, CONV_DIM, SSM_HEADS, N_BRANCHES * D_MODEL)
IN_PROJ_WIDTH = sum(IN_SPLITS)
RMS_EPS = 1e-6


def rmsnorm(x, w):
    x32 = x.astype(jnp.float32)
    y = x32 * lax.rsqrt(jnp.mean(x32 * x32, axis=-1, keepdims=True) + RMS_EPS)
    return (y * w.astype(jnp.float32)).astype(x.dtype)

def alibi_slopes(n):
    def pow2(m):
        start = 2.0 ** (-8.0 / m)
        return [start ** (i + 1) for i in range(m)]
    if (n & (n - 1)) == 0:
        s = pow2(n)
    else:
        c = 2 ** int(math.floor(math.log2(n)))
        s = pow2(c) + pow2(2 * c)[0::2][: n - c]
    return jnp.asarray(np.array(s, dtype=np.float32))

def dilated_window_attention(q, k, v, slopes, window, dilation):
    b, s, h, dh = q.shape
    band = window // dilation
    blk = ATT_BLOCK
    span = dilation * blk
    s_pad = -(-s // span) * span
    pad = ((0, 0), (0, s_pad - s), (0, 0), (0, 0))
    q, k, v = [jnp.pad(t, pad) for t in (q, k, v)]
    nb = s_pad // span
    qb = q.reshape(b, nb, blk, dilation, h, dh)
    kb = k.reshape(b, nb, blk, dilation, h, dh)
    vb = v.reshape(b, nb, blk, dilation, h, dh)

    def with_prev(t):
        prev = jnp.concatenate([jnp.zeros_like(t[:, :1]), t[:, :-1]], axis=1)
        return jnp.concatenate([prev, t], axis=2)

    kk, vv = with_prev(kb), with_prev(vb)
    scores = jnp.einsum('bnirhd,bnjrhd->bnrhij', qb, kk,
                        preferred_element_type=jnp.float32) * (dh ** -0.5)
    i_idx = jnp.arange(blk)[:, None]
    j_idx = jnp.arange(2 * blk)[None, :]
    dist = blk + i_idx - j_idx
    n_idx = jnp.arange(nb)[:, None, None]
    valid = (dist >= 0) & (dist <= band) & ((n_idx > 0) | (j_idx >= blk))
    bias = -slopes[:, None, None] * (dist * dilation).astype(jnp.float32)
    scores = scores + bias[None, None, None]
    scores = jnp.where(valid[None, :, None, None], scores, -jnp.inf)
    m = jnp.max(scores, axis=-1, keepdims=True)
    p = jnp.exp(scores - m)
    l = jnp.sum(p, axis=-1)
    o = jnp.einsum('bnrhij,bnjrhd->bnirhd', p, vv.astype(jnp.float32))
    l_t = jnp.transpose(l, (0, 1, 4, 2, 3))
    m_t = jnp.transpose(m[..., 0], (0, 1, 4, 2, 3))
    o = o / l_t[..., None]
    o = o.reshape(b, s_pad, h, dh)[:, :s]
    return o, m_t.reshape(b, s_pad, h)[:, :s], l_t.reshape(b, s_pad, h)[:, :s]

def ssd_chunked(x, dt, a, bmat, cmat):
    b, s, g, hg, p = x.shape
    n = bmat.shape[-1]
    ch = SSM_CHUNK
    s_pad = -(-s // ch) * ch
    padlen = s_pad - s
    x = jnp.pad(x.astype(jnp.float32), ((0, 0), (0, padlen), (0, 0), (0, 0), (0, 0)))
    dt = jnp.pad(dt, ((0, 0), (0, padlen), (0, 0), (0, 0)))
    bmat = jnp.pad(bmat.astype(jnp.float32), ((0, 0), (0, padlen), (0, 0), (0, 0)))
    cmat = jnp.pad(cmat.astype(jnp.float32), ((0, 0), (0, padlen), (0, 0), (0, 0)))
    c = s_pad // ch
    xd = (x * dt[..., None]).reshape(b, c, ch, g, hg, p)
    la = jnp.moveaxis((dt * a).reshape(b, c, ch, g, hg), 2, -1)
    bc = bmat.reshape(b, c, ch, g, n)
    cc = cmat.reshape(b, c, ch, g, n)
    a_cs = jnp.cumsum(la, axis=-1)
    tril = jnp.tril(jnp.ones((ch, ch), dtype=bool))
    decay = jnp.exp(jnp.where(tril, a_cs[..., :, None] - a_cs[..., None, :], -jnp.inf))
    cb = jnp.einsum('bclgn,bcsgn->bcgls', cc, bc)
    y_diag = jnp.einsum('bcghls,bcsghp->bclghp', cb[:, :, :, None] * decay, xd)
    decay_states = jnp.exp(a_cs[..., -1:] - a_cs)
    states = jnp.einsum('bclgn,bcghl,bclghp->bcghpn', bc, decay_states, xd)
    chunk_decay = jnp.exp(a_cs[..., -1])

    def step(hstate, inp):
        st, dec = inp
        return hstate * dec[..., None, None] + st, hstate

    init = jnp.zeros((b, g, hg, p, n), jnp.float32)
    _, prev = lax.scan(step, init, (jnp.moveaxis(states, 1, 0), jnp.moveaxis(chunk_decay, 1, 0)))
    prev = jnp.moveaxis(prev, 0, 1)
    y_off = jnp.einsum('bclgn,bcghpn,bcghl->bclghp', cc, prev, jnp.exp(a_cs))
    return (y_diag + y_off).reshape(b, s_pad, g, hg, p)[:, :s]

def mamba2_mixer(z, xbc, dt_raw, conv_w, conv_b, dt_bias, a_log, d_skip, norm_w):
    b, s, _ = z.shape
    hg = SSM_HEADS // SSM_GROUPS
    xbc = lax.conv_general_dilated(xbc, conv_w[:, None, :], window_strides=(1,),
                                   padding=[(SSM_CONV - 1, 0)],
                                   dimension_numbers=('NWC', 'WIO', 'NWC'),
                                   feature_group_count=CONV_DIM) + conv_b
    xbc = jax.nn.silu(xbc)
    xs, bm, cm = jnp.split(xbc, [SSM_INNER, SSM_INNER + SSM_GROUPS * SSM_STATE], axis=-1)
    xh = xs.reshape(b, s, SSM_GROUPS, hg, SSM_HEAD_DIM)
    bm = bm.reshape(b, s, SSM_GROUPS, SSM_STATE)
    cm = cm.reshape(b, s, SSM_GROUPS, SSM_STATE)
    dt = jax.nn.softplus((dt_raw + dt_bias).astype(jnp.float32)).reshape(b, s, SSM_GROUPS, hg)
    a = -jnp.exp(a_log.astype(jnp.float32)).reshape(SSM_GROUPS, hg)
    y = ssd_chunked(xh, dt, a, bm, cm)
    y = y + d_skip.astype(jnp.float32).reshape(SSM_GROUPS, hg)[:, :, None] * xh.astype(jnp.float32)
    y = y.reshape(b, s, SSM_INNER) * jax.nn.silu(z.astype(jnp.float32))
    yg = y.reshape(b, s, SSM_GROUPS, SSM_INNER // SSM_GROUPS)
    yg = yg * lax.rsqrt(jnp.mean(yg * yg, axis=-1, keepdims=True) + RMS_EPS)
    y = yg.reshape(b, s, SSM_INNER) * norm_w.astype(jnp.float32)
    return y.astype(z.dtype)

def first_inputs(seed: int = 0) -> dict:
    key = jax.random.key(seed)
    ks = jax.random.split(key, 20)
    f32 = jnp.float32

    def nrm(k, shape, scale):
        return jax.random.normal(k, shape, f32) * scale

    def gain(k, width):
        return 1.0 + 0.05 * jax.random.normal(k, (DEPTH, width), f32)

    dt0 = jnp.exp(jax.random.uniform(ks[7], (DEPTH, SSM_HEADS), f32,
                                     math.log(1e-3), math.log(1e-1)))
    return {
        "x": jax.random.normal(ks[0], (BATCH, SEQ, D_MODEL), f32),
        "norm_mix_pre_w": gain(ks[1], D_MODEL),
        "w_in": nrm(ks[2], (DEPTH, D_MODEL, IN_PROJ_WIDTH), D_MODEL ** -0.5),
        "b_gate": nrm(ks[3], (DEPTH, N_BRANCHES * D_MODEL), 0.02),
        "conv_w": nrm(ks[4], (DEPTH, SSM_CONV, CONV_DIM), SSM_CONV ** -0.5),
        "conv_b": nrm(ks[5], (DEPTH, CONV_DIM), 0.02),
        "dt_bias": dt0 + jnp.log(-jnp.expm1(-dt0)),
        "a_log": jnp.log(jax.random.uniform(ks[8], (DEPTH, SSM_HEADS), f32, 1.0, 16.0)),
        "d_skip": 1.0 + 0.1 * jax.random.normal(ks[9], (DEPTH, SSM_HEADS), f32),
        "ssm_norm_w": gain(ks[10], SSM_INNER),
        "w_att_proj": nrm(ks[11], (DEPTH, ATT_WIDTH, D_MODEL), ATT_WIDTH ** -0.5),
        "w_ssm_proj": nrm(ks[12], (DEPTH, SSM_INNER, D_MODEL), SSM_INNER ** -0.5),
        "w_out": nrm(ks[13], (DEPTH, D_MODEL, D_MODEL), D_MODEL ** -0.5),
        "norm_mix_post_w": gain(ks[14], D_MODEL),
        "norm_ffn_pre_w": gain(ks[15], D_MODEL),
        "w_up": nrm(ks[16], (DEPTH, D_MODEL, FFN_HIDDEN), D_MODEL ** -0.5),
        "w_down": nrm(ks[17], (DEPTH, FFN_HIDDEN, D_MODEL), FFN_HIDDEN ** -0.5),
        "norm_ffn_post_w": gain(ks[18], D_MODEL),
    }

def first_block(x, norm_mix_pre_w, w_in, b_gate, conv_w, conv_b, dt_bias, a_log, d_skip,
              ssm_norm_w, w_att_proj, w_ssm_proj, w_out, norm_mix_post_w, norm_ffn_pre_w,
              w_up, w_down, norm_ffn_post_w):
    b, s, _ = x.shape
    slopes = alibi_slopes(N_ATT_HEADS)
    offsets = [int(o) for o in np.cumsum(IN_SPLITS)[:-1]]
    h = x
    for layer in range(DEPTH):
        u = rmsnorm(h, norm_mix_pre_w[layer])
        proj = u @ w_in[layer]
        q, k, v, z, xbc, dt_raw, gate_logits = jnp.split(proj, offsets, axis=-1)
        q = q.reshape(b, s, N_ATT_HEADS, HEAD_DIM)
        k = k.reshape(b, s, N_ATT_HEADS, HEAD_DIM)
        v = v.reshape(b, s, N_ATT_HEADS, HEAD_DIM)
        outs, maxes, dens = [], [], []
        for window, dilation in DILATED_PATTERNS:
            o_g, m_g, l_g = dilated_window_attention(q, k, v, slopes, window, dilation)
            outs.append(o_g)
            maxes.append(m_g)
            dens.append(l_g)
        m_all = jnp.stack(maxes)
        wts = jnp.exp(m_all - jnp.max(m_all, axis=0, keepdims=True)) * jnp.stack(dens)
        att = jnp.sum(wts[..., None] * jnp.stack(outs), axis=0) / jnp.sum(wts, axis=0)[..., None]
        att = att.reshape(b, s, ATT_WIDTH).astype(x.dtype) @ w_att_proj[layer]
        ssm = mamba2_mixer(z, xbc, dt_raw, conv_w[layer], conv_b[layer], dt_bias[layer],
                           a_log[layer], d_skip[layer], ssm_norm_w[layer])
        ssm = ssm @ w_ssm_proj[layer]
        gates = jax.nn.sigmoid(gate_logits + b_gate[layer])
        g_att, g_ssm = jnp.split(gates, 2, axis=-1)
        mixed = (g_att * att + g_ssm * ssm) @ w_out[layer]
        h = h + rmsnorm(mixed, norm_mix_post_w[layer])
        f = rmsnorm(h, norm_ffn_pre_w[layer])
        f = jnp.square(jax.nn.relu(f @ w_up[layer])) @ w_down[layer]
        h = h + rmsnorm(f, norm_ffn_post_w[layer])
    return h


D_MIX = D_MODEL
D_CONV = D_MIX // 2
D_RET = D_MIX - D_CONV
N_RET_HEADS = 4
RET_HEAD_DIM = D_RET // N_RET_HEADS
CONV_WIDTH = 31
CHUNK = 128
D_FF = ((8 * D_MODEL // 3 + 255) // 256) * 256
D_PLE = 256
ROPE_BASE = 10000.0
EPS = 1e-6
D_IN = 2 * D_CONV + 4 * D_RET


def rmsnorm_2(x, w):
    xf = x.astype(jnp.float32)
    y = xf * lax.rsqrt(jnp.mean(xf * xf, axis=-1, keepdims=True) + EPS)
    return (y * w.astype(jnp.float32)).astype(x.dtype)

def layernorm(x, w, b):
    xf = x.astype(jnp.float32)
    mu = jnp.mean(xf, axis=-1, keepdims=True)
    var = jnp.mean(jnp.square(xf - mu), axis=-1, keepdims=True)
    y = (xf - mu) * lax.rsqrt(var + EPS)
    return (y * w.astype(jnp.float32) + b.astype(jnp.float32)).astype(x.dtype)

def rotary(t, pos):
    half = t.shape[-1] // 2
    freqs = ROPE_BASE ** (-jnp.arange(half, dtype=jnp.float32) / half)
    ang = pos[:, None] * freqs[None, :]
    cos = jnp.cos(ang)[None, :, None, :]
    sin = jnp.sin(ang)[None, :, None, :]
    t1, t2 = t[..., :half], t[..., half:]
    return jnp.concatenate([t1 * cos - t2 * sin, t1 * sin + t2 * cos], axis=-1)

def conformer_conv(u_a, u_b, dw_w, dw_b, ln_w, ln_b):
    u = u_a * jax.nn.sigmoid(u_b)
    y = lax.conv_general_dilated(
        u, dw_w[:, None, :].astype(u.dtype), window_strides=(1,),
        padding=[(CONV_WIDTH - 1, 0)],
        dimension_numbers=("NWC", "WIO", "NWC"),
        feature_group_count=D_CONV)
    y = y + dw_b
    y = layernorm(y, ln_w, ln_b)
    return jax.nn.silu(y)

def chunkwise_retention(q, k, v):
    b, s, h, dh = q.shape
    nc = s // CHUNK
    log_g = jnp.log(1.0 - 2.0 ** (-5.0 - jnp.arange(h, dtype=jnp.float32)))
    idx = jnp.arange(CHUNK, dtype=jnp.float32)
    rel = idx[:, None] - idx[None, :]
    decay_in = jnp.where(rel >= 0, jnp.exp(log_g[:, None, None] * jnp.maximum(rel, 0.0)), 0.0)
    q_decay = jnp.exp(log_g[:, None] * (idx + 1.0))[None, :, :, None]
    k_decay = jnp.exp(log_g[:, None] * (CHUNK - 1.0 - idx))[None, :, :, None]
    chunk_decay = jnp.exp(log_g * CHUNK)[None, :, None, None]

    def to_chunks(t):
        return t.reshape(b, nc, CHUNK, h, dh).transpose(1, 0, 3, 2, 4)

    def step(state, qkv):
        qc, kc, vc = qkv
        scores = jnp.einsum("bhid,bhjd->bhij", qc, kc) * decay_in[None]
        inner = jnp.einsum("bhij,bhjd->bhid", scores, vc)
        cross = jnp.einsum("bhid,bhde->bhie", qc, state) * q_decay
        new_state = state * chunk_decay + jnp.einsum("bhjd,bhje->bhde", kc * k_decay, vc)
        return new_state, inner + cross

    state0 = jnp.zeros((b, h, dh, dh), jnp.float32)
    _, out = lax.scan(step, state0, (to_chunks(q), to_chunks(k), to_chunks(v)))
    return out.transpose(1, 0, 3, 2, 4).reshape(b, s, h, dh)

def retention_group(hq, hk, hv, hg):
    b, s, _ = hq.shape
    shp = (b, s, N_RET_HEADS, RET_HEAD_DIM)
    pos = jnp.arange(s, dtype=jnp.float32)
    q = rotary(hq.reshape(shp).astype(jnp.float32), pos)
    k = rotary(hk.reshape(shp).astype(jnp.float32), pos) * (RET_HEAD_DIM ** -0.5)
    v = hv.reshape(shp).astype(jnp.float32)
    o = chunkwise_retention(q, k, v)
    o = o * lax.rsqrt(jnp.mean(o * o, axis=-1, keepdims=True) + EPS)
    o = o.reshape(b, s, D_RET).astype(hg.dtype)
    return jax.nn.silu(hg) * o

def second_inputs(seed: int = 0) -> dict:
    key = jax.random.key(seed)
    ks = jax.random.split(key, 20)
    f32 = jnp.float32

    def nrm(k, shape, scale):
        return jax.random.normal(k, shape, f32) * scale

    def gain(k, shape):
        return 1.0 + 0.01 * jax.random.normal(k, shape, f32)

    L = DEPTH
    return {
        "x": nrm(ks[0], (BATCH, SEQ, D_MODEL), 1.0),
        "p": nrm(ks[1], (DEPTH, BATCH, SEQ, D_PLE), 1.0),
        "mix_pre_norm": gain(ks[2], (L, D_MODEL)),
        "w_in": nrm(ks[3], (L, D_MODEL, D_IN), D_MODEL ** -0.5),
        "conv_dw_w": nrm(ks[4], (L, CONV_WIDTH, D_CONV), CONV_WIDTH ** -0.5),
        "conv_dw_b": nrm(ks[5], (L, D_CONV), 0.01),
        "conv_ln_w": gain(ks[6], (L, D_CONV)),
        "conv_ln_b": nrm(ks[7], (L, D_CONV), 0.01),
        "w_out": nrm(ks[8], (L, D_MIX, D_MODEL), D_MIX ** -0.5),
        "mix_post_norm": gain(ks[9], (L, D_MODEL)),
        "ffn_pre_norm": gain(ks[10], (L, D_MODEL)),
        "w_ffn_gate": nrm(ks[11], (L, D_MODEL, D_FF), D_MODEL ** -0.5),
        "w_ffn_up": nrm(ks[12], (L, D_MODEL, D_FF), D_MODEL ** -0.5),
        "w_ffn_down": nrm(ks[13], (L, D_FF, D_MODEL), D_FF ** -0.5),
        "ffn_post_norm": gain(ks[14], (L, D_MODEL)),
        "w_ple_gate": nrm(ks[15], (L, D_MODEL, D_MODEL), D_MODEL ** -0.5),
        "w_ple_proj": nrm(ks[16], (L, D_PLE, D_MODEL), D_PLE ** -0.5),
        "ple_post_norm": gain(ks[17], (L, D_MODEL)),
    }

def second_block(x, p, mix_pre_norm, w_in, conv_dw_w, conv_dw_b, conv_ln_w, conv_ln_b,
              w_out, mix_post_norm, ffn_pre_norm, w_ffn_gate, w_ffn_up, w_ffn_down,
              ffn_post_norm, w_ple_gate, w_ple_proj, ple_post_norm):
    for i in range(DEPTH):
        h = rmsnorm_2(x, mix_pre_norm[i])
        u = h @ w_in[i]
        c0, c1 = D_CONV, 2 * D_CONV
        u_a, u_b = u[..., :c0], u[..., c0:c1]
        hq = u[..., c1:c1 + D_RET]
        hk = u[..., c1 + D_RET:c1 + 2 * D_RET]
        hv = u[..., c1 + 2 * D_RET:c1 + 3 * D_RET]
        hg = u[..., c1 + 3 * D_RET:]
        y_conv = conformer_conv(u_a, u_b, conv_dw_w[i], conv_dw_b[i], conv_ln_w[i], conv_ln_b[i])
        y_ret = retention_group(hq, hk, hv, hg)
        y = jnp.concatenate([y_conv, y_ret], axis=-1) @ w_out[i]
        x = x + rmsnorm_2(y, mix_post_norm[i])
        h = rmsnorm_2(x, ffn_pre_norm[i])
        f = (jax.nn.silu(h @ w_ffn_gate[i]) * (h @ w_ffn_up[i])) @ w_ffn_down[i]
        x = x + rmsnorm_2(f, ffn_post_norm[i])
        e = jax.nn.sigmoid(x @ w_ple_gate[i]) * (p[i].astype(x.dtype) @ w_ple_proj[i])
        x = x + rmsnorm_2(e, ple_post_norm[i])
    return x


def setup_inputs(seed=0):
    out = dict(first_inputs(seed))
    for name, value in second_inputs(seed + 1).items():
        if name != "x":
            out[name + "_2"] = value
    return out


def reference(
    x, norm_mix_pre_w, w_in, b_gate, conv_w, conv_b, dt_bias, a_log, d_skip, ssm_norm_w,
    w_att_proj, w_ssm_proj, w_out, norm_mix_post_w, norm_ffn_pre_w, w_up, w_down,
    norm_ffn_post_w, p_2, mix_pre_norm_2, w_in_2, conv_dw_w_2, conv_dw_b_2, conv_ln_w_2,
    conv_ln_b_2, w_out_2, mix_post_norm_2, ffn_pre_norm_2, w_ffn_gate_2, w_ffn_up_2,
    w_ffn_down_2, ffn_post_norm_2, w_ple_gate_2, w_ple_proj_2, ple_post_norm_2,
):
    x = first_block(
        x, norm_mix_pre_w, w_in, b_gate, conv_w, conv_b, dt_bias, a_log, d_skip, ssm_norm_w,
        w_att_proj, w_ssm_proj, w_out, norm_mix_post_w, norm_ffn_pre_w, w_up, w_down,
        norm_ffn_post_w,
    )
    return second_block(
        x, p_2, mix_pre_norm_2, w_in_2, conv_dw_w_2, conv_dw_b_2, conv_ln_w_2, conv_ln_b_2,
        w_out_2, mix_post_norm_2, ffn_pre_norm_2, w_ffn_gate_2, w_ffn_up_2, w_ffn_down_2,
        ffn_post_norm_2, w_ple_gate_2, w_ple_proj_2, ple_post_norm_2,
    )


_drawn_inputs = setup_inputs


def setup_inputs(seed=0):
    import zlib

    import numpy as np

    out = dict(_drawn_inputs(seed))
    spreads = {}
    factors = {'b_gate': 8.0,
     'mix_pre_norm_2': 6.559,
     'conv_dw_b_2': 22.25,
     'conv_ln_w_2': 46.185,
     'conv_ln_b_2': 46.036,
     'mix_post_norm_2': 33.197,
     'ffn_pre_norm_2': 41.984,
     'ffn_post_norm_2': 174.815,
     'ple_post_norm_2': 200.0}
    for name, (base, spread) in spreads.items():
        noise = np.random.default_rng([zlib.crc32(name.encode()), seed]).standard_normal(out[name].shape)
        drawn = base * np.exp(spread * noise) if base else spread * noise
        out[name] = __import__('jax').numpy.asarray(drawn.astype(out[name].dtype))
    for name, factor in factors.items():
        out[name] = (out[name] * factor).astype(out[name].dtype)
    return out
```

```python
import numpy as np

import concourse.bass as bass
from concourse import mybir

F32 = mybir.dt.float32
F32R = mybir.dt.float32r
ALU = mybir.AluOpType
ACT = mybir.ActivationFunctionType

P = 128
T = 512
D = 1024
C8 = D // P
QB = T // P
EPS = 1e-6
RING = 4
TILES = 8

N_HEADS, HEAD = 12, 64
ATT_W = N_HEADS * HEAD
PAIRS = N_HEADS // 2
S_HEADS, GROUPS, S_INNER, S_STATE = 32, 8, 2048, 128
HPG = S_HEADS // GROUPS
CONV4 = 4
FFN1 = 4096
D_CONV, CONV31, R_HEADS = 512, 31, 4
FFN2 = 2816
H2 = FFN2 // P
D_PLE = 256
MASKED = 1e30

PHASES = {
    "attend": (PAIRS, 4, 6, 5),
    "ssm": (GROUPS, 8, 7, 7),
    "gates": (4, 4, 2, 2),
    "mix_out": (2, 4, 2, 2),
    "ffn": (4, 16, 8, 8),
    "glu": (1, 8, 4, 4),
    "retain": (R_HEADS, 4, 2, 2),
    "mix2_out": (2, 4, 2, 2),
    "swiglu": (H2 // 2, 4, 2, 2),
    "down2": (2, 12, 2, 2),
    "ple_proj": (1, 4, 4, 4),
    "ple_gate": (2, 4, 2, 2),
}
def by_output(n):
    return [(j % 2, j // 2) for j in range(n)]


ENDS = {
    "attend": [(0, 0), (1, 0), (0, 1), (1, 4)],
    "ssm": [*by_output(6), (1, 4), (1, 6)],
    "gates": by_output(4), "mix_out": by_output(4), "ffn": by_output(16), "glu": by_output(8),
    "retain": by_output(4), "mix2_out": by_output(4), "swiglu": by_output(4),
    "down2": [None, None, (0, 0), None, None, (1, 0), None, None, (0, 1), None, None, (1, 1)],
    "ple_proj": [(1, 1), (1, 3), (1, 3), (1, 3)], "ple_gate": by_output(4),
}
UNIT0, OUT0 = {}, {}
_u, _a, _b = 0, 0, 0
for _name, (_t, _n, _p, _q) in PHASES.items():
    UNIT0[_name], OUT0[_name] = _u, (_a, _b)
    _u, _a, _b = _u + _t * _n, _a + _t * _p, _b + _t * _q
SLOTS = _u

VEC = {}
_at = 0
for _name, _n in (("pre1", 8), ("post1", 8), ("fpre1", 8), ("fpost1", 8), ("gate_b", 16), ("ssm_norm", 16),
                  ("d_skip", 16), ("conv4", GROUPS * 4 * (CONV4 + 1)), ("dt_bias", 1), ("a_log", 1),
                  ("pre2", 8), ("post2", 8), ("fpre2", 8), ("fpost2", 8), ("ple", 8),
                  ("conv31", 4 * (CONV31 + 1)), ("ln_w", 4), ("ln_b", 4)):
    VEC[_name] = _at
    _at += _n
NVEC = _at

STATS = {}
_q, _k = 0, 0
for _name, _n, _chunks in (("pre1", 1, 8), ("ssm", GROUPS, 2), ("post1", 1, 8), ("fpre1", 1, 8), ("fpost1", 1, 8),
                           ("pre2", 1, 8), ("retain", R_HEADS, 1), ("ln", 0, 4), ("post2", 1, 8), ("fpre2", 1, 8),
                           ("fpost2", 1, 8), ("ple", 1, 8)):
    STATS[_name] = (_q, _k)
    _q, _k = _q + max(1, _n) * _chunks, _k + _n


class Turn:

    def __init__(self, name, i=0):
        _, self.slots, *self.outs = PHASES[name]
        self.ends = ENDS[name]
        self.unit0, self.out0, self.i = UNIT0[name], OUT0[name], i

    def unit(self, j):
        return self.i * self.slots + (self.unit0 + j)

    def out(self, bank, m):
        return self.i * self.outs[bank] + (self.out0[bank] + m)


def block_program(nc, weights, w_dt, x, p, vectors, constants, att_tables, ret_tables, acs_dram, out):
    base = (nc.sbuf_base + 63) // 64 * 64
    top = [base]

    def place(name, shape, dt=F32, at=None):
        size = 4 * int(np.prod(shape[1:]))
        offset = top[0] if at is None else at
        if at is None:
            top[0] += (size + 31) // 32 * 32
        return nc.alloc_sbuf_tensor_at(name, shape, dt, offset=offset)

    raw = place("raw", [P, RING, TILES * P])
    w_hi = place("w_hi", [P, RING, TILES * P], F32R)
    w_lo = place("w_lo", [P, RING, TILES * P], F32R)
    u_at = top[0]
    u_hi = place("u_hi", [P, C8, T], F32R)
    u_lo = place("u_lo", [P, C8, T], F32R)
    xs = place("xs", [P, C8, T])
    s_hi = place("s_hi", [P, 2, T], F32R)
    s_lo = place("s_lo", [P, 2, T], F32R)
    vec = place("vec", [P, NVEC])
    half = place("half", [P, 33])
    cst = place("cst", [P, 4 * P + N_HEADS])
    heads_t = place("heads_t", [P, 3, QB, S_HEADS])
    tiny = place("tiny", [P, 64])
    diag = place("diag", [P, T])
    sq = place("sq", [P, 2, T])
    ident, ones, tri, perm = (cst[:, k * P:(k + 1) * P] for k in range(4))
    slopes = cst[:, 4 * P:4 * P + N_HEADS]
    y_u = place("y_u", [P, C8, T], at=u_at)
    work = top[0]
    K = 1024

    att_acc = place("att_acc", [P, C8, T], at=work)
    ssm_acc = place("ssm_acc", [P, C8, T], at=work + 16 * K)
    a_at = work + 32 * K
    k_t = place("k_t", [P, T], at=a_at)
    q_t = place("q_t", [P, T], at=a_at + 2 * K)
    v_t = place("v_t", [P, T], at=a_at + 4 * K)
    v_tok = place("v_tok", [P, QB, P], at=a_at + 6 * K)
    dist = place("dist", [P, 2 * T], at=a_at + 8 * K)
    bias = place("bias", [P, 2, T], at=a_at + 12 * K)
    logits = place("logits", [P, 4, T], at=a_at + 16 * K)
    p_t = place("p_t", [P, 2, QB, P], at=a_at + 24 * K)
    dt_at = a_at + 28 * K
    dt_raw = place("dt_raw", [P, TILES * P], at=dt_at)
    hf = place("hf", [32, 10, T], at=dt_at + 4 * K)
    cat = place("cat", [P, 4, T + 3], at=a_at)
    g_at = a_at + 8256
    post = place("post", [P, 4, T], at=g_at)
    zz = place("zz", [P, 2, T], at=g_at + 8 * K)
    xd = place("xd", [P, QB, 2 * P], at=g_at + 12 * K)
    xw = place("xw", [P, QB, 2 * P], at=g_at + 16 * K)
    b_tok = place("b_tok", [P, QB, P], at=g_at + 20 * K)
    bc = place("bc", [P, HPG, T], at=g_at + 22 * K)
    gm = place("gm", [P, QB, P], at=g_at + 30 * K)
    states = place("states", [P, 3, 2 * P], at=g_at + 32 * K)
    y_g = place("y_g", [P, 2, T], at=g_at + 35 * K)
    decay = place("decay", [P, HPG, T], at=g_at + 39 * K)
    v_hi = place("v_hi", [P, C8, T], F32R, at=work + 32 * K)
    v_lo = place("v_lo", [P, C8, T], F32R, at=work + 48 * K)
    t_at = work + 64 * K
    tmp = place("tmp", [P, 6, T], at=t_at)
    p_raw = place("p_raw", [P, 2, T], at=t_at + 12 * K)
    ffn_acc = place("ffn_acc", [P, C8, T], at=work)
    cat31 = place("cat31", [P, 4, T + CONV31 - 1], at=work)
    cv = place("cv", [P, 4, T], at=work + 8704)
    rt = place("rt", [P, 6, T], at=work + 17 * K)
    r_at = t_at
    r_q = place("r_q", [P, T], at=r_at)
    r_k = place("r_k", [P, T], at=r_at + 2 * K)
    r_v = place("r_v", [P, T], at=r_at + 4 * K)
    r_g = place("r_g", [P, 2, T], at=r_at + 6 * K)
    rot_q = place("rot_q", [P, T], at=r_at + 10 * K)
    rot_k = place("rot_k", [P, T], at=r_at + 12 * K)
    rot_s = place("rot_s", [P, 2, T], at=r_at + 14 * K)
    r_vtok = place("r_vtok", [P, QB, P], at=r_at + 18 * K)
    r_s = place("r_s", [P, QB * (QB + 1) // 2 * P], at=r_at + 20 * K)
    r_o = place("r_o", [P, T], at=r_at + 25 * K)
    S_OFF = [0, 512, 896, 1152]
    h_hi = place("h_hi", [P, H2, T], F32R, at=work)
    h_lo = place("h_lo", [P, H2, T], F32R, at=work + 44 * K)
    h_tmp = place("h_tmp", [P, T], at=work + 88 * K)
    pj = place("pj", [P, C8, T], at=work)
    ple_tanh = place("ple_tanh", [P, 2, T], at=t_at)

    ps = [nc.alloc_psum_tensor(f"bank{i}", [P, T], F32) for i in range(8)]
    ms, rb = ps[2], ps[3]

    sems = {}

    def sem(name):
        if name not in sems:
            sems[name] = nc.alloc_semaphore(name)
        return sems[name]

    landed = [sem(f"slot_landed{s}") for s in range(RING)]
    hi_done, lo_done, slot_inside = sem("hi_done"), sem("lo_done"), sem("slot_ended_inside_output")
    out_ready = [sem("out_ready0"), sem("out_ready1")]
    out_free = [sem("out_free0"), sem("out_free1")]
    sq_ready, sq_used = sem("sq_ready"), sem("sq_used")
    var_ready, sd_ready = sem("var_ready"), sem("sd_ready")
    diag_ready, rb_ready = sem("diag_ready"), sem("rb_ready")
    n_ready, u_hi_ready, u_ready = sem("n_ready"), sem("u_hi_ready"), sem("u_ready")
    x_ready = sem("x_ready")

    def v(name, k=0, n=1):
        return vec[:, VEC[name] + k:VEC[name] + k + n]

    def freed(engine, turn, bank, m):
        engine.wait_ge(out_free[bank], turn.out(bank, m) + 2)

    def ended(engine, turn, j):
        if j < 0:
            engine.wait_ge(out_free[1], turn.out(1, 0) + 1)
        elif turn.ends[j]:
            bank, m = turn.ends[j]
            engine.wait_ge(out_ready[bank], turn.out(bank, m) + 1)
        else:
            engine.wait_ge(slot_inside, turn.i * 8 + (j - j // 3 + 1))

    block = nc.Block()
    with block:

        @block.sync
        def _(sp):
            sp.dma_start(xs[:], x).then_inc(sem("x_landed"), 16)
            sp.dma_start(vec[:], vectors).then_inc(sem("const_landed"), 16)
            sp.dma_start(cst[:], constants).then_inc(sem("const_landed"), 16)
            stream = weights.rearrange("(g r) p n -> g r p n", r=RING)
            for s in range(RING):
                sp.dma_start(raw[:, s, :], stream[0, s]).then_inc(landed[s], 16)
            sp.dma_start(dt_raw[:], w_dt).then_inc(sem("dtw_landed"), 16)
            sp.dma_start(dist[:], att_tables).then_inc(sem("dist_landed"), 16)
            with sp.Fori(1, SLOTS // RING) as g:
                for s in range(RING):
                    sp.wait_ge(lo_done, g * RING + (s + 1 - RING))
                    sp.dma_start(raw[:, s, :], stream[g, s]).then_inc(landed[s], 16)
            for c in range(C8):
                sp.wait_ge(sem("result_ready"), c + 1)
                sp.dma_start(out[:, c, :], xs[:, c, :]).then_inc(sem("stored"), 16)
            sp.wait_ge(sem("stored"), 16 * C8)

        @block.gpsimd
        def _(pool):
            with pool.Fori(0, SLOTS // RING) as g:
                for s in range(RING):
                    pool.wait_ge(hi_done, g * RING + (s + 1))
                    if s == 0:
                        pass
                    nc.gpsimd.tensor_tensor(w_lo[:, s, :], raw[:, s, :], w_hi[:, s, :].bitcast(F32),
                                            ALU.subtract).then_inc(lo_done, 1)

        @block.tensor
        def _(pe):
            mm = nc.tensor.matmul

            def exact(dst, slot, tile, hi, lo, first, last):
                w = slice(tile * P, tile * P + P)
                mm(dst, w_hi[:, slot, w], hi, start=first, stop=False)
                mm(dst, w_hi[:, slot, w], lo, start=False, stop=False)
                return mm(dst, w_lo[:, slot, w], hi, start=False, stop=last)

            def unit(turn, j, bank, m, hi, lo, ready=None, ready0=0, tiles=None, first=True, last=True):
                pe.wait_ge(lo_done, turn.unit(j) + 1)
                if first:
                    pe.wait_ge(out_free[bank], turn.out(bank, m) + 1)
                tiles = tiles or [(t, t) for t in range(TILES)]
                for n, (t, c) in enumerate(tiles):
                    if ready is not None:
                        pe.wait_ge(ready, ready0 + c + 1)
                    last_mm = exact(ps[bank][:], j % RING, t, hi[:, c, :], lo[:, c, :],
                                    first and n == 0, last and n == len(tiles) - 1)
                last_mm.then_inc(out_ready[bank] if last else slot_inside, 1)

            def stat_chunk(q, c, n):
                pe.wait_ge(sq_ready, q + 1)
                for t in range(QB):
                    last_mm = mm(ms[:, t:t + 1], sq[:, c % 2, t * P:(t + 1) * P], ones[:, 0:1],
                                 start=(c == 0 and t == 0), stop=(c == n - 1 and t == QB - 1),
                                 skip_group_check=True)
                last_mm.then_inc(sq_used, 1)

            def stat_broadcast(k):
                pe.wait_ge(diag_ready, k + 1)
                mm(rb[:], ones, diag[:], start=True, stop=True).then_inc(rb_ready, 1)

            def norm(name, n=C8):
                q, k = STATS[name]
                for c in range(n):
                    stat_chunk(q + c, c, n)
                stat_broadcast(k)

            pe.wait_ge(sem("const_landed"), 32)
            norm("pre1")
            pe.wait_ge(sem("dtw_ready"), 1)
            for c in range(C8):
                pe.wait_ge(u_ready, c + 1)
                w = slice(c * P, c * P + P)
                hi_w = s_hi[:].rearrange("p a t -> p (a t)")[:, w]
                lo_w = s_lo[:].rearrange("p a t -> p (a t)")[:, w]
                mm(ps[4][:], hi_w, u_hi[:, c, :], start=(c == 0), stop=False)
                mm(ps[4][:], hi_w, u_lo[:, c, :], start=False, stop=False)
                last = mm(ps[4][:], lo_w, u_hi[:, c, :], start=False, stop=(c == C8 - 1))
            last.then_inc(sem("dt_logits"), 1)

            with pe.Fori(0, PAIRS) as i:
                turn = Turn("attend", i)
                unit(turn, 0, 0, 0, u_hi, u_lo)
                unit(turn, 1, 1, 0, u_hi, u_lo)
                unit(turn, 2, 0, 1, u_hi, u_lo)

                def scores(b):
                    h, qb = divmod(b, QB)
                    if b == 0:
                        freed(pe, turn, 0, 0)
                        freed(pe, turn, 1, 0)
                    if b >= 3:
                        pe.wait_ge(sem("logits_done"), i * 8 + (b - 2))
                    rows = slice(h * HEAD, h * HEAD + HEAD)
                    n = (qb + 1) * P
                    mm(ps[3 + b % 3][:, 0:n], q_t[rows, qb * P:(qb + 1) * P], k_t[rows, 0:n],
                       start=True, stop=True).then_inc(sem("scores_ready"), 1)

                def turned(b):
                    pe.wait_ge(sem("probs_ready"), i * 8 + b + 1)
                    if b >= 2:
                        pe.wait_ge(sem("p_t_ready"), i * 8 + (b - 1))
                    if b == 1:
                        pe.wait_ge(sem("v_tok_ready"), i + 1)
                    for kb in range(b % QB + 1):
                        last = nc.tensor.transpose(ps[2 + 4 * (b % 2)][:, kb * P:(kb + 1) * P],
                                                   logits[:, b % 4, kb * P:(kb + 1) * P], ident)
                    last.then_inc(sem("turned"), 1)

                def attended(b):
                    h, qb = divmod(b, QB)
                    pe.wait_ge(sem("p_t_ready"), i * 8 + b + 1)
                    if b == 0:
                        pe.wait_ge(sem("v_tok_ready"), i + 1)
                    for kb in range(qb + 1):
                        last = mm(ps[7][h * HEAD:(h + 1) * HEAD, qb * P:(qb + 1) * P],
                                  v_tok[:, kb, h * HEAD:(h + 1) * HEAD], p_t[:, b % 2, kb, :],
                                  start=(kb == 0), stop=(kb == qb))
                    last.then_inc(sem("attended"), 1)

                for b in range(3):
                    scores(b)
                freed(pe, turn, 0, 1)
                for t in range(QB):
                    last = nc.tensor.transpose(ps[6][:, t * P:(t + 1) * P], v_t[:, t * P:(t + 1) * P], ident)
                last.then_inc(sem("v_turned"), 1)
                for b in range(8):
                    turned(b)
                    if b + 3 < 8:
                        scores(b + 3)
                    if b >= 1:
                        attended(b - 1)
                attended(7)
                pe.wait_ge(lo_done, turn.unit(3) + 1)
                pe.wait_ge(sem("att_split"), i + 1)
                for n in range(C8):
                    bank = n % 2
                    m = (2 if bank == 0 else 1) + n // 2
                    pe.wait_ge(out_free[bank], turn.out(bank, m) + 1)
                    last = exact(ps[bank][:], 3, n, s_hi[:, 0, :], s_lo[:, 0, :], True, True)
                    last.then_inc(out_ready[bank], 1)

            q0, k0 = STATS["ssm"]
            with pe.Fori(0, GROUPS) as i:
                turn = Turn("ssm", i)
                for j in range(6):
                    unit(turn, j, j % 2, j // 2, u_hi, u_lo)
                for j in range(2):
                    pe.wait_ge(sem("silu_done"), i * 4 + j + 1)
                    for t in range(QB):
                        last = nc.tensor.transpose(ps[2 + j][:, t * P:(t + 1) * P],
                                                   post[:, j, t * P:(t + 1) * P], ident)
                    last.then_inc(sem("x_turned"), 1)
                pe.wait_ge(sem("silu_done"), i * 4 + 3)
                for t in range(QB):
                    last = nc.tensor.transpose(ps[4][:, t * P:(t + 1) * P], post[:, 2, t * P:(t + 1) * P], ident)
                last.then_inc(sem("b_turned"), 1)
                pe.wait_ge(sem("silu_done"), i * 4 + 4)
                for t in range(QB):
                    w = slice(t * P, (t + 1) * P)
                    last = mm(ps[5][:, w], post[:, 2, w], post[:, 3, w], start=True, stop=True)
                last.then_inc(sem("bc_product"), 1)
                pe.wait_ge(sem("xw_ready"), i * 2 + 2)
                pe.wait_ge(sem("b_tok_ready"), i + 1)
                for c in range(3):
                    last = mm(ps[2 + c // 2][:, c % 2 * 256:c % 2 * 256 + 256], b_tok[:, c, :], xw[:, c, :],
                              start=True, stop=True)
                last.then_inc(sem("state_sums"), 1)
                for h in range(HPG):
                    rows = slice(h % 2 * HEAD, h % 2 * HEAD + HEAD)
                    cols = slice(h * HEAD, h * HEAD + HEAD)
                    pe.wait_ge(sem("kernel_ready"), i * 4 + h + 1)
                    pe.wait_ge(sem("c_decayed"), i * 4 + h + 1)
                    if h == 0:
                        pe.wait_ge(sem("states_ready"), i + 1)
                    for c in range(QB):
                        w = slice(c * P, (c + 1) * P)
                        last = mm(ps[6 + h // 2][rows, w], xd[:, c, cols], decay[:, h, w],
                                  start=True, stop=(c == 0))
                        if c:
                            last = mm(ps[6 + h // 2][rows, w], states[:, c - 1, cols], bc[:, h, w],
                                      start=False, stop=True)
                    last.then_inc(sem("y_done"), 1)
                for c in range(2):
                    stat_chunk(i * 2 + (q0 + c), c, 2)
                stat_broadcast(i + k0)
                for n in range(C8):
                    bank = n % 2
                    pe.wait_ge(out_free[bank], turn.out(bank, 3 + n // 2) + 1)
                    if n % 4 == 0:
                        pe.wait_ge(lo_done, turn.unit(6 + n // 4) + 1)
                    for c in range(2):
                        if n == 0:
                            pe.wait_ge(sem("ssm_split"), i * 2 + c + 3)
                        last = exact(ps[bank][:], 2 + n // 4, n % 4 * 2 + c, s_hi[:, c, :], s_lo[:, c, :],
                                     c == 0, c == 1)
                    last.then_inc(out_ready[bank], 1)

            with pe.Fori(0, 4) as i:
                turn = Turn("gates", i)
                for j in range(4):
                    unit(turn, j, j % 2, j // 2, u_hi, u_lo)

            def outputs_with_stats(name, stat, hi, lo, ready, ready0=0):
                q, k = STATS[stat]
                for i in range(2):
                    turn = Turn(name, i)
                    for j in range(4):
                        unit(turn, j, j % 2, j // 2, hi, lo, ready if (i, j) == (0, 0) else None, ready0)
                        c = 4 * i + j
                        if c:
                            stat_chunk(q + c - 1, c - 1, C8)
                stat_chunk(q + C8 - 1, C8 - 1, C8)
                stat_broadcast(k)

            outputs_with_stats("mix_out", "post1", v_hi, v_lo, sem("mixed_ready"))
            norm("fpre1")

            with pe.Fori(0, 4) as i:
                turn = Turn("ffn", i)
                for j in range(8):
                    unit(turn, j, j % 2, j // 2, u_hi, u_lo, u_ready if j == 0 else None, 8)
                for j in range(8):
                    unit(turn, 8 + j, j % 2, 4 + j // 2, v_hi, v_lo,
                         sem("hidden_ready") if j == 0 else None, i * 8)
            norm("fpost1")
            norm("pre2")

            turn = Turn("glu")
            for j in range(8):
                unit(turn, j, j % 2, j // 2, u_hi, u_lo, u_ready if j == 0 else None, 16)
            q0, k0 = STATS["retain"]
            with pe.Fori(0, R_HEADS) as i:
                turn = Turn("retain", i)
                for j in range(4):
                    unit(turn, j, j % 2, j // 2, u_hi, u_lo)
                freed(pe, turn, 0, 0)
                mm(ps[4][:], perm, r_q[:], start=True, stop=True).then_inc(sem("swapped"), 1)
                freed(pe, turn, 1, 0)
                mm(ps[5][:], perm, r_k[:], start=True, stop=True).then_inc(sem("swapped"), 1)
                freed(pe, turn, 0, 1)
                for t in range(QB):
                    last = nc.tensor.transpose(ps[6][:, t * P:(t + 1) * P], r_v[:, t * P:(t + 1) * P], ident)
                last.then_inc(sem("r_v_turned"), 1)
                pe.wait_ge(sem("rotated"), i * 2 + 2)
                for kb in range(QB):
                    n = T - kb * P
                    if kb >= 2:
                        pe.wait_ge(sem("decayed"), i * 4 + (kb - 1))
                    mm(ps[4 + kb % 2][:, 0:n], rot_k[:, kb * P:(kb + 1) * P], rot_q[:, kb * P:T],
                       start=True, stop=True).then_inc(sem("r_scores"), 1)
                pe.wait_ge(sem("r_vtok_ready"), i + 1)
                for kb in range(QB):
                    n = T - kb * P
                    pe.wait_ge(sem("decayed"), i * 4 + kb + 1)
                    last = mm(ps[7][:, kb * P:T], r_vtok[:, kb, :], r_s[:, S_OFF[kb]:S_OFF[kb] + n],
                              start=(kb == 0), stop=(kb == QB - 1), skip_group_check=True)
                last.then_inc(sem("retained"), 1)
                stat_chunk(i + q0, 0, 1)
                stat_broadcast(i + k0)
            q0, k0 = STATS["ln"]
            for c in range(4):
                pe.wait_ge(sem("conv_done"), c + 1)
                for t in range(QB):
                    last = mm(ms[:, t:t + 1], cv[:, c, t * P:(t + 1) * P], ones[:, 0:1],
                              start=(c == 0 and t == 0), stop=(c == 3 and t == 3), skip_group_check=True)
            last.then_inc(sem("mean_sum"), 1)
            pe.wait_ge(sem("mean_diag"), 1)
            mm(rb[:], ones, diag[:], start=True, stop=True).then_inc(sem("mean_ready"), 1)
            for c in range(4):
                stat_chunk(q0 + c, c, 4)
            pe.wait_ge(sem("ln_diag"), 1)
            mm(rb[:], ones, diag[:], start=True, stop=True).then_inc(sem("ln_ready"), 1)
            pe.wait_ge(sem("ret_split"), R_HEADS)
            outputs_with_stats("mix2_out", "post2", v_hi, v_lo, sem("y2_ready"))
            norm("fpre2")

            with pe.Fori(0, H2 // 2) as i:
                turn = Turn("swiglu", i)
                for j in range(4):
                    unit(turn, j, j % 2, j // 2, u_hi, u_lo, u_ready if j == 0 else None, 24)
            q, k = STATS["fpost2"]
            for i in range(2):
                turn = Turn("down2", i)
                for n in range(4):
                    for s in range(3):
                        chunks = range(s * TILES, min(H2, (s + 1) * TILES))
                        unit(turn, 3 * n + s, n % 2, n // 2, h_hi, h_lo,
                             sem("hidden2_ready") if (i, n) == (0, 0) else None, 0,
                             [(t, c) for t, c in enumerate(chunks)], first=(s == 0), last=(s == 2))
                    c = 4 * i + n
                    if c:
                        stat_chunk(q + c - 1, c - 1, C8)
            stat_chunk(q + C8 - 1, C8 - 1, C8)
            stat_broadcast(k)
            turn = Turn("ple_proj")
            pe.wait_ge(sem("p_split"), 1)
            for n in range(C8):
                bank = n % 2
                if n % 4 == 0:
                    pe.wait_ge(lo_done, turn.unit(n // 4) + 1)
                pe.wait_ge(out_free[bank], turn.out(bank, n // 2) + 1)
                for c in range(2):
                    last = exact(ps[bank][:], n // 4, n % 4 * 2 + c, s_hi[:, c, :], s_lo[:, c, :], c == 0, c == 1)
                last.then_inc(out_ready[bank], 1)
            q, k = STATS["ple"]
            for i in range(2):
                turn = Turn("ple_gate", i)
                for j in range(4):
                    unit(turn, j, j % 2, j // 2, u_hi, u_lo, u_ready if (i, j) == (0, 0) else None, 32)
                    c = 4 * i + j
                    if c:
                        stat_chunk(q + c - 1, c - 1, C8)
            stat_chunk(q + C8 - 1, C8 - 1, C8)
            stat_broadcast(k)

        @block.scalar
        def _(act):
            af = nc.scalar.activation

            def split(u, slot):
                if isinstance(u, int):
                    act.wait_ge(landed[slot], 16 * (u // RING + 1))
                else:
                    act.wait_ge(landed[slot], (u - slot) * (16 // RING) + 16)
                af(w_hi[:, slot, :], raw[:, slot, :], ACT.Copy).then_inc(hi_done, 1)

            def ahead(turn, j):
                if isinstance(turn.unit(j), int) and turn.unit(j) + 3 >= SLOTS:
                    return
                ended(act, turn, j - 1)
                split(turn.unit(j + 3), (j + 3) % RING)

            def ready(turn, bank, m):
                act.wait_ge(out_ready[bank], turn.out(bank, m) + 1)

            def square(q, c, src, wait_all=False):
                if not isinstance(q, int) or q >= 2:
                    act.wait_ge(sq_used, q if wait_all else q - 1)
                return af(sq[:, c % 2, :], src, ACT.Square).then_inc(sq_ready, 1)

            def stat_root(k):
                act.wait_ge(var_ready, k + 1)
                af(tiny[:, 4:8], tiny[:, 0:4], ACT.Sqrt).then_inc(sd_ready, 1)

            def x_squares(name, first_x):
                q, k = STATS[name]
                for c in range(C8):
                    act.wait_ge(x_ready, first_x + c + 1)
                    square(q + c, c, xs[:, c, :])
                stat_root(k)

            def round_u(n0):
                for c in range(C8):
                    act.wait_ge(n_ready, n0 + c + 1)
                    af(u_hi[:, c, :], sq[:, c % 2, :], ACT.Copy).then_inc(u_hi_ready, 1)

            def outputs(turn_name, stat):
                q, k = STATS[stat]
                for i in range(2):
                    turn = Turn(turn_name, i)
                    for j in range(4):
                        ahead(turn, j)
                        ready(turn, j % 2, j // 2)
                        c = 4 * i + j
                        square(q + c, c, ps[j % 2][:])
                        af(y_u[:, c, :], ps[j % 2][:], ACT.Copy).then_inc(out_free[j % 2], 1)
                stat_root(k)

            act.wait_ge(sem("x_landed"), 16)
            for c in range(C8):
                square(c, c, xs[:, c, :])
            split(0, 0)
            stat_root(0)
            act.wait_ge(sem("dtw_landed"), 16)
            af(s_hi[:].rearrange("p a t -> p (a t)"), dt_raw[:], ACT.Copy).then_inc(sem("dtw_hi"), 1)
            split(1, 1)
            split(2, 2)
            round_u(0)
            act.wait_ge(sem("dt_abs"), 1)
            af(hf[:, 1, :], hf[:, 0, :], ACT.Exp, scale=-1.0).then_inc(sem("dt_exp"), 1)
            af(half[0:32, 32:33], vec[0:32, VEC["a_log"]:VEC["a_log"] + 1], ACT.Exp).then_inc(sem("dt_exp"), 1)
            act.wait_ge(sem("acs_ready"), 1)
            act.dma_start(acs_dram, hf[:, 5, :]).then_inc(sem("acs_stored"), 16)
            af(hf[:, 6, :], hf[:, 6, :], ACT.Exp).then_inc(sem("dt_exp"), 1)

            with act.Fori(0, PAIRS) as i:
                turn = Turn("attend", i)
                ahead(turn, 0)
                ready(turn, 0, 0)
                af(k_t[:], ps[0][:], ACT.Copy).then_inc(out_free[0], 1)
                ahead(turn, 1)
                ready(turn, 1, 0)
                af(q_t[:], ps[1][:], ACT.Copy, scale=-float(HEAD) ** -0.5).then_inc(out_free[1], 1)
                ahead(turn, 2)
                ready(turn, 0, 1)
                af(v_t[:], ps[0][:], ACT.Copy).then_inc(out_free[0], 1)
                ahead(turn, 3)

                def p_copy(b):
                    act.wait_ge(sem("turned"), i * 8 + b + 1)
                    if b >= 2:
                        act.wait_ge(sem("attended"), i * 8 + (b - 1))
                    n = b % QB + 1
                    af(p_t[:, b % 2, 0:n, :].rearrange("p k t -> p (k t)"), ps[2 + 4 * (b % 2)][:, 0:n * P],
                       ACT.Copy).then_inc(sem("p_t_ready"), 1)

                for b in range(8):
                    n = (b % QB + 1) * P
                    act.wait_ge(sem("logits_done"), i * 8 + b + 1)
                    af(logits[:, b % 4, 0:n], logits[:, b % 4, 0:n], ACT.Exp, scale=-1.0,
                       bias=tiny[:, 8 + b:9 + b], accum_out=tiny[:, 16 + b:17 + b])\
                        .then_inc(sem("exp_done"), 1)
                    if b >= 2:
                        p_copy(b - 2)
                p_copy(6)
                p_copy(7)
                act.wait_ge(sem("attended"), i * 8 + 8)
                af(s_hi[:, 0, :], ps[7][:], ACT.Copy).then_inc(sem("att_hi"), 1)

            q0, k0 = STATS["ssm"]
            act.wait_ge(sem("acs_stored"), 16)
            with act.Fori(0, GROUPS) as i:
                turn = Turn("ssm", i)
                rows = acs_dram.rearrange("(g h) t -> g h t", h=HPG)[i]
                act.wait_ge(sem("ssm_split"), i * 2 + 2)
                act.dma_start(bc[:], rows.partition_broadcast(P)).then_inc(sem("bc_landed"), 16)

                def tanh_conv(j):
                    act.wait_ge(sem("conv4_done"), i * 4 + j + 1)
                    if j >= 2:
                        act.wait_ge(sem("silu_done"), i * 4 + (j - 1))
                    af(sq[:, j % 2, :], post[:, j, :], ACT.Tanh, scale=0.5).then_inc(sem("tanh_done"), 1)

                for j in range(4):
                    ahead(turn, j)
                    ready(turn, j % 2, j // 2)
                    af(cat[:, j, 3:T + 3], ps[j % 2][:], ACT.Copy).then_inc(out_free[j % 2], 1)
                    if j:
                        tanh_conv(j - 1)
                for j in range(2):
                    ahead(turn, 4 + j)
                    ready(turn, j, 2)
                    af(zz[:, j, :], ps[j][:], ACT.Tanh, scale=0.5).then_inc(sem("z_tanh"), 1)
                    if j == 0:
                        tanh_conv(3)
                ahead(turn, 6)
                act.wait_ge(sem("bc_landed"), i * 16 + 16)
                af(tiny[:, 24:40].rearrange("p (h c) -> p h c", h=HPG), bc[:, :, P - 1:T:P], ACT.Exp)\
                    .then_inc(sem("ends_done"), 1)
                act.wait_ge(sem("b_turned"), i + 1)
                af(b_tok[:].rearrange("p c n -> p (c n)"), ps[4][:], ACT.Copy).then_inc(sem("b_tok_ready"), 1)
                for h in range(HPG):
                    act.wait_ge(sem("differences"), i * 4 + h + 1)
                    af(decay[:, h, :], decay[:, h, :], ACT.Exp).then_inc(sem("decay_exp"), 1)
                    if h == 0:
                        act.wait_ge(sem("ends_done"), i + 1)
                    af(bc[:, h, :], bc[:, h, :], ACT.Exp).then_inc(sem("bc_exp"), 1)
                act.wait_ge(sem("state_sums"), i + 1)
                af(states[:, 0, :], ps[2][:, 0:256], ACT.Copy).then_inc(sem("state0"), 1)
                for j in range(2):
                    act.wait_ge(sem("y_gated"), i * 2 + j + 1)
                    square(i * 2 + (q0 + j), j, y_g[:, j, :])
                stat_root(i + k0)
                for j in range(2):
                    act.wait_ge(sem("y_normed"), i * 2 + j + 1)
                    af(s_hi[:, j, :], y_g[:, j, :], ACT.Copy).then_inc(sem("ssm_hi"), 1)
                ahead(turn, 7)

            with act.Fori(0, 4) as i:
                turn = Turn("gates", i)
                for n in range(2):
                    for j in range(2):
                        ahead(turn, 2 * n + j)
                        ready(turn, j, n)
                        act.wait_ge(sem("mixed"), i * 2 + n + 1)
                        af(tmp[:, 2 * n + j, :], ps[j][:], ACT.Tanh, scale=0.5,
                           bias=half[:, bass.ds(i * 2 + (8 * j + n), 1)]).then_inc(out_free[j], 1)
                for n in range(2):
                    act.wait_ge(sem("mixed"), i * 2 + n + 3)
                    af(v_hi[:, i * 2 + n, :], tmp[:, 4 + n, :], ACT.Copy).then_inc(sem("mixed_hi"), 1)

            outputs("mix_out", "post1")
            x_squares("fpre1", 0)
            round_u(8)
            act.wait_ge(u_ready, 16)
            act.dma_start(rt[:], ret_tables).then_inc(sem("rt_landed"), 16)
            act.dma_start(p_raw[:], p).then_inc(sem("p_landed"), 16)

            with act.Fori(0, 4) as i:
                turn = Turn("ffn", i)

                def round_hidden(j):
                    freed(act, turn, j % 2, j // 2)
                    af(v_hi[:, j, :], tmp[:, j % 2, :], ACT.Copy).then_inc(sem("hidden_hi"), 1)

                for j in range(8):
                    ahead(turn, j)
                    ready(turn, j % 2, j // 2)
                    if j >= 2:
                        act.wait_ge(sem("hidden_ready"), i * 8 + (j - 1))
                    af(tmp[:, j % 2, :], ps[j % 2][:], ACT.Relu).then_inc(sem("relu_done"), 1)
                    if j:
                        round_hidden(j - 1)
                round_hidden(7)
                for j in range(8):
                    ahead(turn, 8 + j)
            act.wait_ge(sem("p_landed"), 16)
            af(s_hi[:], p_raw[:], ACT.Copy).then_inc(sem("p_hi"), 1)
            act.wait_ge(out_free[0], OUT0["glu"][0] + 1)
            act.wait_ge(out_free[1], OUT0["glu"][1] + 1)
            q, k = STATS["fpost1"]
            for c in range(C8):
                square(q + c, c, ffn_acc[:, c, :])
            stat_root(k)
            x_squares("pre2", 8)
            round_u(16)

            turn = Turn("glu")
            for n in range(4):
                for j in range(2):
                    ahead(turn, 2 * n + j)
                    ready(turn, j, n)
                    if n >= 1:
                        act.wait_ge(sem("glu_done"), n)
                    if j == 0:
                        af(tmp[:, 0, :], ps[0][:], ACT.Copy, scale=0.5).then_inc(out_free[0], 1)
                    else:
                        af(tmp[:, 1, :], ps[1][:], ACT.Tanh, scale=0.5).then_inc(out_free[1], 1)
            act.wait_ge(sem("glu_done"), 4)

            q0, k0 = STATS["retain"]
            with act.Fori(0, R_HEADS) as i:
                turn = Turn("retain", i)
                for j, dst in enumerate((r_q, r_k, r_v)):
                    ahead(turn, j)
                    ready(turn, j % 2, j // 2)
                    af(dst[:], ps[j % 2][:], ACT.Copy).then_inc(out_free[j % 2], 1)
                ahead(turn, 3)
                ready(turn, 1, 1)
                act.wait_ge(sem("ret_normed"), i + 1)
                af(r_g[:, 0, :], ps[1][:], ACT.Copy, scale=0.5)
                af(r_g[:, 1, :], ps[1][:], ACT.Tanh, scale=0.5).then_inc(out_free[1], 1)
                act.wait_ge(sem("r_v_turned"), i + 1)
                af(r_vtok[:].rearrange("p k t -> p (k t)"), ps[6][:], ACT.Copy).then_inc(sem("r_vtok_ready"), 1)
                act.wait_ge(sem("retained"), i + 1)
                square(i + q0, 0, ps[7][:], wait_all=True)
                stat_root(i + k0)
                act.wait_ge(sem("ret_normed"), i + 2)
                af(v_hi[:, i + 4, :], r_o[:], ACT.Copy).then_inc(sem("ret_hi"), 1)
            q0, k0 = STATS["ln"]
            for c in range(4):
                act.wait_ge(sem("centred"), c + 1)
                if c == 0:
                    act.wait_ge(sq_used, q0)
                square(q0 + c, c, cv[:, c, :])
            act.wait_ge(sem("ln_var"), 1)
            af(tiny[:, 4:8], tiny[:, 0:4], ACT.Sqrt).then_inc(sem("ln_sd"), 1)
            for c in range(4):
                act.wait_ge(sem("ln_scaled"), c + 1)
                if c >= 2:
                    act.wait_ge(sem("conv_silu"), c - 1)
                af(sq[:, c % 2, :], cv[:, c, :], ACT.Tanh).then_inc(sem("ln_tanh"), 1)
                if c:
                    act.wait_ge(sem("conv_silu"), c)
                    af(v_hi[:, c - 1, :], cv[:, c - 1, :], ACT.Copy).then_inc(sem("conv_hi"), 1)
            act.wait_ge(sem("conv_silu"), 4)
            af(v_hi[:, 3, :], cv[:, 3, :], ACT.Copy).then_inc(sem("conv_hi"), 1)

            outputs("mix2_out", "post2")
            x_squares("fpre2", 16)
            round_u(24)

            with act.Fori(0, H2 // 2) as i:
                turn = Turn("swiglu", i)
                for n in range(2):
                    ahead(turn, 2 * n)
                    ready(turn, 0, n)
                    act.wait_ge(out_free[1], turn.out(1, n) + 1)
                    af(sq[:, 0, :], ps[0][:], ACT.Tanh, scale=0.5)
                    af(sq[:, 1, :], ps[0][:], ACT.Copy, scale=0.5).then_inc(out_free[0], 1)
                    ahead(turn, 2 * n + 1)
                    freed(act, turn, 1, n)
                    af(h_hi[:, i * 2 + n, :], h_tmp[:], ACT.Copy).then_inc(sem("hidden2_hi"), 1)
            q, k = STATS["fpost2"]
            for i in range(2):
                turn = Turn("down2", i)
                for n in range(4):
                    for s in range(3):
                        ahead(turn, 3 * n + s)
                    ready(turn, n % 2, n // 2)
                    c = 4 * i + n
                    square(q + c, c, ps[n % 2][:])
                    af(y_u[:, c, :], ps[n % 2][:], ACT.Copy).then_inc(out_free[n % 2], 1)
            stat_root(k)
            turn = Turn("ple_proj")
            for n in range(C8):
                if n in (1, 5):
                    ahead(turn, n // 4)
                ready(turn, n % 2, n // 2)
                af(pj[:, n, :], ps[n % 2][:], ACT.Copy).then_inc(out_free[n % 2], 1)
            ahead(turn, 2)
            ahead(turn, 3)
            for c in range(C8):
                act.wait_ge(x_ready, 24 + c + 1)
                af(u_hi[:, c, :], xs[:, c, :], ACT.Copy).then_inc(u_hi_ready, 1)
            q, k = STATS["ple"]
            for i in range(2):
                turn = Turn("ple_gate", i)
                for j in range(4):
                    ahead(turn, j)
                    ready(turn, j % 2, j // 2)
                    c = 4 * i + j
                    if c >= 2:
                        act.wait_ge(sem("e_ready"), c - 1)
                    af(ple_tanh[:, c % 2, :], ps[j % 2][:], ACT.Tanh, scale=0.5).then_inc(out_free[j % 2], 1)
                    if c:
                        act.wait_ge(sem("e_ready"), c)
                        square(q + c - 1, c - 1, pj[:, c - 1, :])
            act.wait_ge(sem("e_ready"), 8)
            square(q + 7, 7, pj[:, 7, :])
            stat_root(k)

        @block.vector
        def _(dve):
            tt, ts, stt = nc.vector.tensor_tensor, nc.vector.tensor_scalar, nc.vector.scalar_tensor_tensor

            def ready(turn, bank, m):
                dve.wait_ge(out_ready[bank], turn.out(bank, m) + 1)

            def factors(width, eps, q, k, var_sem, sd_sem, diag_sem):
                dve.wait_ge(sq_used, q)
                ts(tiny[:, 0:4], ms[:, 0:4], 1.0 / width, eps, ALU.mult, ALU.add).then_inc(var_sem, 1)
                dve.wait_ge(sd_sem, k + 1)
                nc.vector.reciprocal(tiny[:, 40:44], tiny[:, 4:8])
                dve.drain()
                tt(tiny[:, 52:56], tiny[:, 40:44], tiny[:, 40:44], ALU.mult)
                dve.drain()
                tt(tiny[:, 52:56], tiny[:, 52:56], tiny[:, 0:4], ALU.mult)
                dve.drain()
                ts(tiny[:, 52:56], tiny[:, 52:56], -0.5, 1.5, ALU.mult, ALU.add)
                dve.drain()
                tt(tiny[:, 40:44], tiny[:, 40:44], tiny[:, 52:56], ALU.mult)
                dve.drain()
                for t in range(QB):
                    last = ts(diag[:, t * P:(t + 1) * P], ident, tiny[:, 40 + t:41 + t], None, ALU.mult)
                last.then_inc(diag_sem, 1)

            def stat(name, chunks=C8, i=0, width=D, eps=EPS):
                q, k = STATS[name]
                factors(width, eps, i * chunks + (q + chunks), i + k, var_ready, sd_ready, diag_ready)
                dve.wait_ge(rb_ready, i + k + 1)

            def pre_norm(name, n0):
                stat(name)

                def rest(c):
                    dve.wait_ge(u_hi_ready, n0 + c + 1)
                    tt(u_lo[:, c, :], sq[:, c % 2, :], u_hi[:, c, :].bitcast(F32), ALU.subtract)\
                        .then_inc(u_ready, 1)

                for c in range(C8):
                    if c >= 2:
                        dve.wait_ge(u_ready, n0 + c - 1)
                    stt(out=sq[:, c % 2, :], in0=xs[:, c, :], scalar=v(name, c), in1=rb[:], op0=ALU.mult,
                        op1=ALU.mult).then_inc(n_ready, 1)
                    if c:
                        rest(c - 1)
                rest(C8 - 1)

            def post_norm(name, y, eps=EPS, done=x_ready, after=None):
                if after:
                    dve.wait_ge(out_free[0], OUT0[after][0] + 1)
                    dve.wait_ge(out_free[1], OUT0[after][1] + 1)
                stat(name, eps=eps)
                for c in range(C8):
                    stt(out=y[:, c, :], in0=y[:, c, :], scalar=v(name, c), in1=rb[:], op0=ALU.mult, op1=ALU.mult)
                    dve.drain()
                    tt(xs[:, c, :], xs[:, c, :], y[:, c, :], ALU.add).then_inc(done, 1)

            nc.vector.memset(tiny[:], 0.0).then_inc(out_free[0], 1)
            nc.vector.memset(half[:], 0.0).then_inc(out_free[1], 1)
            nc.vector.memset(heads_t[:], 0.0).then_inc(sem("ssm_split"), 2)
            dve.wait_ge(sem("const_landed"), 32)
            dve.drain()
            ts(half[:, 0:16], v("gate_b", 0, 16), 0.5, None, ALU.mult)
            ts(half[:, 16:32], v("d_skip", 0, 16), 0.5, None, ALU.mult)
            nc.vector.memset(hf[:, 9, :], 1.0)
            dve.wait_ge(sem("x_landed"), 16)
            pre_norm("pre1", 0)
            dve.wait_ge(sem("dtw_hi"), 1)
            tt(s_lo[:].rearrange("p a t -> p (a t)"), dt_raw[:], s_hi[:].rearrange("p a t -> p (a t)").bitcast(F32),
               ALU.subtract).then_inc(sem("dtw_ready"), 1)
            nc.vector.memset(att_acc[:], 0.0)
            nc.vector.memset(ssm_acc[:], 0.0)
            dve.wait_ge(sem("dt_logits"), 1)
            bias_dt = vec[0:32, VEC["dt_bias"]:VEC["dt_bias"] + 1]
            ts(hf[:, 2, :], ps[4][0:32, :], bias_dt, 0.0, ALU.add, ALU.min)
            ts(hf[:, 3, :], ps[4][0:32, :], bias_dt, 0.0, ALU.add, ALU.max)
            dve.drain()
            tt(hf[:, 0, :], hf[:, 3, :], hf[:, 2, :], ALU.subtract).then_inc(sem("dt_abs"), 1)
            dve.wait_ge(sem("dt_exp"), 2)
            ts(hf[:, 2, :], hf[:, 1, :], 2.0, None, ALU.add)
            ts(half[0:32, 32:33], half[0:32, 32:33], -1.0, None, ALU.mult)
            dve.drain()
            nc.vector.reciprocal(hf[:, 4, :], hf[:, 2, :])
            dve.drain()
            tt(hf[:, 2, :], hf[:, 1, :], hf[:, 4, :], ALU.mult)
            dve.drain()
            tt(hf[:, 4, :], hf[:, 2, :], hf[:, 2, :], ALU.mult)
            dve.drain()
            ts(hf[:, 0, :], hf[:, 4, :], 1.0 / 17, None, ALU.mult)
            for n in (15, 13, 11, 9, 7, 5, 3):
                dve.drain()
                stt(out=hf[:, 0, :], in0=hf[:, 0, :], scalar=1.0 / n, in1=hf[:, 4, :], op0=ALU.add, op1=ALU.mult)
            dve.drain()
            stt(out=hf[:, 0, :], in0=hf[:, 0, :], scalar=1.0, in1=hf[:, 2, :], op0=ALU.add, op1=ALU.mult)
            dve.drain()
            stt(out=hf[:, 3, :], in0=hf[:, 0, :], scalar=2.0, in1=hf[:, 3, :], op0=ALU.mult, op1=ALU.add)
            dve.drain()
            ts(hf[:, 4, :], hf[:, 3, :], half[0:32, 32:33], None, ALU.mult)
            dve.drain()
            for c in range(QB):
                w = slice(c * P, (c + 1) * P)
                nc.vector.tensor_tensor_scan(hf[:, 5, w], hf[:, 9, w], hf[:, 4, w], 0.0, ALU.mult, ALU.add)
            dve.drain()
            for c in range(QB):
                w = slice(c * P, (c + 1) * P)
                last = ts(hf[:, 6, w], hf[:, 5, w], -1.0, hf[:, 5, (c + 1) * P - 1:(c + 1) * P], ALU.mult, ALU.add)
            last.then_inc(sem("acs_ready"), 1)
            dve.wait_ge(sem("dt_exp"), 3)
            stt(out=hf[:, 7, :], in0=hf[:, 6, :], scalar=0.125, in1=hf[:, 3, :], op0=ALU.mult, op1=ALU.mult)
            ts(hf[:, 8, :], hf[:, 3, :], 0.125, None, ALU.mult)
            dve.drain()
            for n, k in enumerate((8, 5, 7)):
                for c in range(QB):
                    for r in range(4):
                        nc.vector.transpose(heads_t[32 * r:32 * r + 32, n, c, :],
                                            hf[:, k, c * P + 32 * r:c * P + 32 * r + 32])

            dve.wait_ge(sem("dist_landed"), 16)
            with dve.Fori(0, PAIRS) as i:
                turn = Turn("attend", i)
                dve.drain()
                for h in range(2):
                    stt(out=bias[:, h, :], in0=dist[:, 0:T], scalar=slopes[:, bass.ds(i * 2 + h, 1)],
                        in1=dist[:, T:2 * T], op0=ALU.mult, op1=ALU.add)
                dve.drain()

                def logit(b):
                    h, qb = divmod(b, QB)
                    n = (qb + 1) * P
                    if b >= 4:
                        dve.wait_ge(sem("turned"), i * 8 + (b - 3))
                    dve.wait_ge(sem("scores_ready"), i * 8 + b + 1)
                    nc.vector.memset(tiny[:, 44 + b:45 + b], 0.0)
                    nc.vector.tensor_tensor_reduce(
                        out=logits[:, b % 4, 0:n], in0=ps[3 + b % 3][:, 0:n], in1=bias[:, h, T - n:T],
                        scale=1.0, scalar=3e38, op0=ALU.add, op1=ALU.min,
                        accum_out=tiny[:, 8 + b:9 + b]).then_inc(sem("logits_done"), 1)

                def normal(b):
                    n = (b % QB + 1) * P
                    dve.wait_ge(sem("exp_done"), i * 8 + b + 1)
                    nc.vector.reciprocal(tiny[:, 44 + b:45 + b], tiny[:, 16 + b:17 + b])
                    dve.drain()
                    ts(logits[:, b % 4, 0:n], logits[:, b % 4, 0:n], tiny[:, 44 + b:45 + b], None, ALU.mult)\
                        .then_inc(sem("probs_ready"), 1)

                for b in range(8):
                    logit(b)
                    if b == 1:
                        dve.wait_ge(sem("v_turned"), i + 1)
                        nc.vector.tensor_copy(v_tok[:].rearrange("p k t -> p (k t)"), ps[6][:])\
                            .then_inc(sem("v_tok_ready"), 1)
                    if b >= 1:
                        normal(b - 1)
                normal(7)
                dve.wait_ge(sem("att_hi"), i + 1)
                tt(s_lo[:, 0, :], ps[7][:], s_hi[:, 0, :].bitcast(F32), ALU.subtract).then_inc(sem("att_split"), 1)
                for n in range(C8):
                    bank = n % 2
                    ready(turn, bank, (2 if bank == 0 else 1) + n // 2)
                    tt(att_acc[:, n, :], att_acc[:, n, :], ps[bank][:], ALU.add).then_inc(out_free[bank], 1)

            q0, k0 = STATS["ssm"]
            dve.drain()
            nc.vector.memset(cat[:, :, 0:3], 0.0)
            dve.drain()
            with dve.Fori(0, GROUPS) as i:
                turn = Turn("ssm", i)
                cw = VEC["conv4"]

                def silu(j):
                    dve.wait_ge(sem("tanh_done"), i * 4 + j + 1)
                    stt(out=post[:, j, :], in0=sq[:, j % 2, :], scalar=1.0, in1=post[:, j, :],
                        op0=ALU.add, op1=ALU.mult).then_inc(sem("silu_done"), 1)

                for j in range(4):
                    freed(dve, turn, j % 2, j // 2)

                    def weight(t):
                        return vec[:, bass.ds(i * (4 * (CONV4 + 1)) + (cw + j * (CONV4 + 1) + t), 1)]

                    ts(post[:, j, :], cat[:, j, 0:T], weight(0), weight(CONV4), ALU.mult, ALU.add)
                    for t in range(1, CONV4):
                        dve.drain()
                        last = stt(out=post[:, j, :], in0=cat[:, j, t:t + T], scalar=weight(t), in1=post[:, j, :],
                                   op0=ALU.mult, op1=ALU.add)
                    last.then_inc(sem("conv4_done"), 1)
                    if j:
                        silu(j - 1)
                silu(3)
                for j in range(2):
                    dve.wait_ge(sem("z_tanh"), i * 2 + j + 1)
                    stt(out=zz[:, j, :], in0=zz[:, j, :], scalar=1.0, in1=ps[j][:], op0=ALU.add, op1=ALU.mult)\
                        .then_inc(out_free[j], 1)

                def per_head(n, j):
                    return heads_t[:, n, :, bass.ds(i * HPG + 2 * j, 2)].unsqueeze(3).broadcast_to([P, QB, 2, HEAD])

                for j in range(2):
                    dve.wait_ge(sem("x_turned"), i * 2 + j + 1)
                    src = ps[2 + j][:].rearrange("p (c h f) -> p c h f", c=QB, h=2)
                    cols = slice(j * P, (j + 1) * P)
                    tt(xd[:, :, cols].rearrange("p c (h f) -> p c h f", h=2), src, per_head(0, j), ALU.mult)
                    tt(xw[:, :, cols].rearrange("p c (h f) -> p c h f", h=2), src, per_head(2, j), ALU.mult)\
                        .then_inc(sem("xw_ready"), 1)
                dve.wait_ge(sem("bc_product"), i + 1)
                tt(gm[:], ps[5][:].rearrange("p (c t) -> p c t", c=QB), tri.unsqueeze(1).broadcast_to([P, QB, P]),
                   ALU.mult)
                dve.wait_ge(sem("bc_landed"), i * 16 + 16)
                for h in range(HPG):
                    for c in range(QB):
                        w = slice(c * P, (c + 1) * P)
                        last = ts(decay[:, h, w], bc[:, h, w], heads_t[:, 1, c, bass.ds(i * HPG + h, 1)], 0.0,
                                  ALU.subtract, ALU.min)
                    last.then_inc(sem("differences"), 1)
                for h in range(HPG):
                    dve.wait_ge(sem("decay_exp"), i * 4 + h + 1)
                    tt(decay[:, h, :], decay[:, h, :], gm[:].rearrange("p c t -> p (c t)"), ALU.mult)\
                        .then_inc(sem("kernel_ready"), 1)
                    dve.wait_ge(sem("bc_exp"), i * 4 + h + 1)
                    tt(bc[:, h, :], bc[:, h, :], post[:, 3, :], ALU.mult).then_inc(sem("c_decayed"), 1)
                for c in range(1, 3):
                    dve.drain()
                    if c == 1:
                        dve.wait_ge(sem("state0"), i + 1)
                    for h in range(HPG):
                        cols = slice(h * HEAD, (h + 1) * HEAD)
                        at = c % 2 * 256 + h * HEAD
                        last = stt(out=states[:, c, cols], in0=states[:, c - 1, cols],
                                   scalar=tiny[:, 24 + 4 * h + c:25 + 4 * h + c], in1=ps[2 + c // 2][:, at:at + HEAD],
                                   op0=ALU.mult, op1=ALU.add)
                last.then_inc(sem("states_ready"), 1)
                for j in range(2):
                    dve.wait_ge(sem("y_done"), i * 4 + 2 * j + 2)
                    last = stt(out=y_g[:, j, :], in0=post[:, j, :], scalar=half[:, bass.ds(i * 2 + (16 + j), 1)],
                               in1=ps[6 + j][:], op0=ALU.mult, op1=ALU.add)
                    dve.drain()
                    tt(y_g[:, j, :], y_g[:, j, :], zz[:, j, :], ALU.mult).then_inc(sem("y_gated"), 1)
                stat("ssm", 2, i, width=2 * P, eps=4 * EPS)
                for j in range(2):
                    stt(out=y_g[:, j, :], in0=y_g[:, j, :],
                        scalar=vec[:, bass.ds(i * 2 + (VEC["ssm_norm"] + j), 1)], in1=rb[:],
                        op0=ALU.mult, op1=ALU.mult).then_inc(sem("y_normed"), 1)
                for j in range(2):
                    dve.wait_ge(sem("ssm_hi"), i * 2 + j + 1)
                    tt(s_lo[:, j, :], y_g[:, j, :], s_hi[:, j, :].bitcast(F32), ALU.subtract)\
                        .then_inc(sem("ssm_split"), 1)
                for n in range(C8):
                    bank = n % 2
                    ready(turn, bank, 3 + n // 2)
                    tt(ssm_acc[:, n, :], ssm_acc[:, n, :], ps[bank][:], ALU.add).then_inc(out_free[bank], 1)

            dve.drain()
            nc.vector.memset(tiny[:, 60:61], 0.0).then_inc(sem("mixed"), 2)
            with dve.Fori(0, 4) as i:
                turn = Turn("gates", i)
                for n in range(2):
                    freed(dve, turn, 0, n)
                    stt(out=tmp[:, 2 * n, :], in0=tmp[:, 2 * n, :], scalar=1.0, in1=att_acc[:, i * 2 + n, :],
                        op0=ALU.add, op1=ALU.mult)
                    freed(dve, turn, 1, n)
                    stt(out=tmp[:, 2 * n + 1, :], in0=tmp[:, 2 * n + 1, :], scalar=1.0, in1=ssm_acc[:, i * 2 + n, :],
                        op0=ALU.add, op1=ALU.mult)
                    dve.drain()
                    tt(tmp[:, 4 + n, :], tmp[:, 2 * n, :], tmp[:, 2 * n + 1, :], ALU.add).then_inc(sem("mixed"), 1)
                for n in range(2):
                    dve.wait_ge(sem("mixed_hi"), i * 2 + n + 1)
                    tt(v_lo[:, i * 2 + n, :], tmp[:, 4 + n, :], v_hi[:, i * 2 + n, :].bitcast(F32), ALU.subtract)\
                        .then_inc(sem("mixed_ready"), 1)
                dve.drain()

            post_norm("post1", y_u, eps=4 * EPS, after="ffn")
            nc.vector.memset(ffn_acc[:], 0.0)
            pre_norm("fpre1", 8)

            with dve.Fori(0, 4) as i:
                turn = Turn("ffn", i)

                def rest_hidden(j):
                    dve.wait_ge(sem("hidden_hi"), i * 8 + j + 1)
                    tt(v_lo[:, j, :], tmp[:, j % 2, :], v_hi[:, j, :].bitcast(F32), ALU.subtract)\
                        .then_inc(sem("hidden_ready"), 1)

                for j in range(8):
                    dve.wait_ge(sem("relu_done"), i * 8 + j + 1)
                    stt(out=tmp[:, j % 2, :], in0=ps[j % 2][:], scalar=0.0, in1=tmp[:, j % 2, :],
                        op0=ALU.max, op1=ALU.mult).then_inc(out_free[j % 2], 1)
                    if j:
                        rest_hidden(j - 1)
                rest_hidden(7)
                dve.drain()
                for j in range(8):
                    ready(turn, j % 2, 4 + j // 2)
                    tt(ffn_acc[:, j, :], ffn_acc[:, j, :], ps[j % 2][:], ALU.add).then_inc(out_free[j % 2], 1)
            dve.wait_ge(sem("p_hi"), 1)
            tt(s_lo[:], p_raw[:], s_hi[:].bitcast(F32), ALU.subtract).then_inc(sem("p_split"), 1)
            dve.drain()
            post_norm("fpost1", ffn_acc)
            pre_norm("pre2", 16)

            nc.vector.memset(cat31[:, :, 0:CONV31 - 1], 0.0)
            turn = Turn("glu")
            for n in range(4):
                freed(dve, turn, 0, n)
                freed(dve, turn, 1, n)
                stt(out=cat31[:, n, CONV31 - 1:], in0=tmp[:, 1, :], scalar=1.0, in1=tmp[:, 0, :],
                    op0=ALU.add, op1=ALU.mult).then_inc(sem("glu_done"), 1)
            dve.wait_ge(sem("rt_landed"), 16)
            dve.drain()
            nc.vector.memset(tiny[:, 60:61], 0.0).then_inc(sem("ret_normed"), 1)

            q0, k0 = STATS["retain"]
            with dve.Fori(0, R_HEADS) as i:
                turn = Turn("retain", i)
                cw = VEC["conv31"]

                def tap(t):
                    return vec[:, bass.ds(i * (CONV31 + 1) + (cw + t), 1)]

                ts(cv[:, i, :], cat31[:, i, 0:T], tap(0), tap(CONV31), ALU.mult, ALU.add)
                for t in range(1, CONV31):
                    dve.drain()
                    last = stt(out=cv[:, i, :], in0=cat31[:, i, t:t + T], scalar=tap(t), in1=cv[:, i, :],
                               op0=ALU.mult, op1=ALU.add)
                last.then_inc(sem("conv_done"), 1)
                for j, (src, dst) in enumerate(((r_q, rot_q), (r_k, rot_k))):
                    dve.wait_ge(sem("swapped"), i * 2 + j + 1)
                    tt(dst[:], src[:], rt[:, 0, :], ALU.mult)
                    tt(rot_s[:, j, :], ps[4 + j][:], rt[:, 1, :], ALU.mult)
                    dve.drain()
                    tt(dst[:], dst[:], rot_s[:, j, :], ALU.add).then_inc(sem("rotated"), 1)
                for kb in range(QB):
                    n = T - kb * P
                    dve.wait_ge(sem("r_scores"), i * 4 + kb + 1)
                    tt(r_s[:, S_OFF[kb]:S_OFF[kb] + n], ps[4 + kb % 2][:, 0:n], rt[:, i + 2, 0:n], ALU.mult)\
                        .then_inc(sem("decayed"), 1)
                freed(dve, turn, 1, 1)
                stt(out=r_g[:, 0, :], in0=r_g[:, 1, :], scalar=1.0, in1=r_g[:, 0, :], op0=ALU.add, op1=ALU.mult)
                dve.drain()
                stat("retain", 1, i, width=P)
                tt(r_g[:, 0, :], r_g[:, 0, :], rb[:], ALU.mult)
                dve.drain()
                tt(r_o[:], r_g[:, 0, :], ps[7][:], ALU.mult).then_inc(sem("ret_normed"), 1)
                dve.wait_ge(sem("ret_hi"), i + 1)
                tt(v_lo[:, i + 4, :], r_o[:], v_hi[:, i + 4, :].bitcast(F32), ALU.subtract)\
                    .then_inc(sem("ret_split"), 1)
                dve.drain()

            dve.wait_ge(sem("mean_sum"), 1)
            ts(tiny[:, 40:44], ms[:, 0:4], 1.0 / D_CONV, None, ALU.mult)
            dve.drain()
            for t in range(QB):
                last = ts(diag[:, t * P:(t + 1) * P], ident, tiny[:, 40 + t:41 + t], None, ALU.mult)
            last.then_inc(sem("mean_diag"), 1)
            dve.wait_ge(sem("mean_ready"), 1)
            for c in range(4):
                tt(cv[:, c, :], cv[:, c, :], rb[:], ALU.subtract).then_inc(sem("centred"), 1)
            factors(D_CONV, EPS, STATS["ln"][0] + 4, 0, sem("ln_var"), sem("ln_sd"), sem("ln_diag"))
            dve.wait_ge(sem("ln_ready"), 1)

            def conv_rest(c):
                dve.wait_ge(sem("conv_hi"), c + 1)
                tt(v_lo[:, c, :], cv[:, c, :], v_hi[:, c, :].bitcast(F32), ALU.subtract).then_inc(sem("y2_ready"), 1)

            for c in range(4):
                stt(out=cv[:, c, :], in0=cv[:, c, :], scalar=v("ln_w", c), in1=rb[:], op0=ALU.mult, op1=ALU.mult)
                dve.drain()
                ts(cv[:, c, :], cv[:, c, :], v("ln_b", c), 0.5, ALU.add, ALU.mult).then_inc(sem("ln_scaled"), 1)
            for c in range(4):
                dve.wait_ge(sem("ln_tanh"), c + 1)
                stt(out=cv[:, c, :], in0=sq[:, c % 2, :], scalar=1.0, in1=cv[:, c, :], op0=ALU.add, op1=ALU.mult)\
                    .then_inc(sem("conv_silu"), 1)
                if c:
                    conv_rest(c - 1)
            conv_rest(3)
            nc.vector.memset(tiny[:, 60:61], 0.0).then_inc(sem("y2_ready"), 4)

            post_norm("post2", y_u, after="swiglu")
            pre_norm("fpre2", 24)

            with dve.Fori(0, H2 // 2) as i:
                turn = Turn("swiglu", i)
                for n in range(2):
                    freed(dve, turn, 0, n)
                    stt(out=sq[:, 1, :], in0=sq[:, 0, :], scalar=1.0, in1=sq[:, 1, :], op0=ALU.add, op1=ALU.mult)
                    dve.drain()
                    ready(turn, 1, n)
                    tt(h_tmp[:], sq[:, 1, :], ps[1][:], ALU.mult).then_inc(out_free[1], 1)
                    dve.wait_ge(sem("hidden2_hi"), i * 2 + n + 1)
                    tt(h_lo[:, i * 2 + n, :], h_tmp[:], h_hi[:, i * 2 + n, :].bitcast(F32), ALU.subtract)\
                        .then_inc(sem("hidden2_ready"), 1)
                    dve.drain()
            post_norm("fpost2", y_u, after="ple_proj")
            for c in range(C8):
                dve.wait_ge(u_hi_ready, 32 + c + 1)
                tt(u_lo[:, c, :], xs[:, c, :], u_hi[:, c, :].bitcast(F32), ALU.subtract).then_inc(u_ready, 1)
            for c in range(C8):
                freed(dve, Turn("ple_gate", c // 4), c % 2, c % 4 // 2)
                stt(out=pj[:, c, :], in0=ple_tanh[:, c % 2, :], scalar=1.0, in1=pj[:, c, :], op0=ALU.add, op1=ALU.mult)\
                    .then_inc(sem("e_ready"), 1)
            post_norm("ple", pj, eps=4 * EPS, done=sem("result_ready"))


def weight_stream(w):
    w_in, w_att, w_ssm, w_out = w["w_in"][0], w["w_att_proj"][0], w["w_ssm_proj"][0], w["w_out"][0]
    up, down = w["w_up"][0], w["w_down"][0]
    w_in2, w_out2 = w["w_in_2"][0], w["w_out_2"][0]
    gate2, up2, down2 = w["w_ffn_gate_2"][0], w["w_ffn_up_2"][0], w["w_ffn_down_2"][0]
    q0, k0, v0 = 0, ATT_W, 2 * ATT_W
    z0 = 3 * ATT_W
    x0 = z0 + S_INNER
    b0 = x0 + S_INNER
    c0 = b0 + GROUPS * S_STATE
    dt0 = c0 + GROUPS * S_STATE
    g0 = dt0 + S_HEADS
    stream = np.zeros((SLOTS, P, TILES * P), np.float32)
    n = [0]

    def slot(tiles):
        for t, tile in enumerate(tiles):
            stream[n[0], :, t * P:(t + 1) * P] = tile
        n[0] += 1

    def columns(m, c, k0=0, k1=TILES):
        slot([m[k * P:(k + 1) * P, c:c + P] for k in range(k0, k1)])

    for i in range(PAIRS):
        for at in (k0, q0, v0):
            columns(w_in, at + i * P)
        slot([w_att[i * P:(i + 1) * P, c * P:(c + 1) * P] for c in range(C8)])
    for g in range(GROUPS):
        for at in (x0 + g * 256, x0 + g * 256 + P, b0 + g * P, c0 + g * P, z0 + g * 256, z0 + g * 256 + P):
            columns(w_in, at)
        for m in range(2):
            slot([w_ssm[(2 * g + k) * P:(2 * g + k + 1) * P, c * P:(c + 1) * P]
                  for c in range(4 * m, 4 * m + 4) for k in range(2)])
    for c in range(C8):
        columns(w_in, g0 + c * P)
        columns(w_in, g0 + D + c * P)
    for c in range(C8):
        columns(w_out, c * P)
    for i in range(4):
        for c in range(8):
            columns(up, (8 * i + c) * P)
        for c in range(C8):
            columns(down, c * P, 8 * i, 8 * i + 8)
    for c in range(4):
        columns(w_in2, c * P)
        columns(w_in2, D_CONV + c * P)
    for h in range(R_HEADS):
        for part in range(4):
            columns(w_in2, 2 * D_CONV + part * 512 + h * P)
    for c in range(C8):
        columns(w_out2, c * P)
    for c in range(H2):
        columns(gate2, c * P)
        columns(up2, c * P)
    for c in range(C8):
        for s in range(3):
            columns(down2, c * P, 8 * s, min(H2, 8 * s + 8))
    proj = w["w_ple_proj_2"][0]
    for m in range(2):
        slot([proj[k * P:(k + 1) * P, c * P:(c + 1) * P] for c in range(4 * m, 4 * m + 4) for k in range(2)])
    n[0] += 2
    for c in range(C8):
        columns(w["w_ple_gate_2"][0], c * P)
    assert n[0] == SLOTS
    w_dt = np.zeros((P, TILES, P), np.float32)
    w_dt[:, :, 0:S_HEADS] = w_in[:, dt0:dt0 + S_HEADS].reshape(TILES, P, S_HEADS).transpose(1, 0, 2)
    return stream, w_dt.reshape(P, TILES * P)


def feature_vectors(w):
    vec = np.zeros((P, NVEC), np.float32)

    def put(name, a, at=0):
        a = a.reshape(-1, P).T
        vec[:, VEC[name] + at:VEC[name] + at + a.shape[1]] = a

    for name, key in (("pre1", "norm_mix_pre_w"), ("post1", "norm_mix_post_w"), ("fpre1", "norm_ffn_pre_w"),
                      ("fpost1", "norm_ffn_post_w"), ("gate_b", "b_gate"), ("ssm_norm", "ssm_norm_w"),
                      ("pre2", "mix_pre_norm_2"), ("post2", "mix_post_norm_2"), ("fpre2", "ffn_pre_norm_2"),
                      ("fpost2", "ffn_post_norm_2"), ("ple", "ple_post_norm_2"),
                      ("ln_w", "conv_ln_w_2"), ("ln_b", "conv_ln_b_2")):
        put(name, w[key][0])
    put("d_skip", np.repeat(w["d_skip"][0], HEAD))
    taps = np.concatenate([w["conv_w"][0], w["conv_b"]])
    for g in range(GROUPS):
        for j, c in enumerate((2 * g, 2 * g + 1, 16 + g, 24 + g)):
            vec[:, VEC["conv4"] + (4 * g + j) * 5:VEC["conv4"] + (4 * g + j + 1) * 5] = taps[:, c * P:(c + 1) * P].T
    taps = np.concatenate([w["conv_dw_w_2"][0], w["conv_dw_b_2"]])
    for c in range(4):
        vec[:, VEC["conv31"] + c * 32:VEC["conv31"] + (c + 1) * 32] = taps[:, c * P:(c + 1) * P].T
    vec[0:S_HEADS, VEC["dt_bias"]] = w["dt_bias"][0]
    vec[0:S_HEADS, VEC["a_log"]] = w["a_log"][0]
    return vec


def shape_constants():
    i = np.arange(P)
    cst = np.zeros((P, 4 * P + N_HEADS), np.float32)
    cst[:, 0:P] = np.eye(P)
    cst[:, P:2 * P] = 1.0
    cst[:, 2 * P:3 * P] = i[:, None] <= i[None, :]
    cst[i, 3 * P + (i + 64) % P] = 1.0
    small = 2 ** int(np.floor(np.log2(N_HEADS)))

    def powers(m):
        return [2.0 ** (-8.0 / m * (k + 1)) for k in range(m)]

    cst[:, 4 * P:] = np.array(powers(small) + powers(2 * small)[0::2][:N_HEADS - small], np.float32)
    d = i[:, None] - np.arange(T)[None, :] + (T - P)
    times = (d <= 128).astype(int) + (d % 4 == 0) + (d % 16 == 0)
    seen = (d >= 0) & (times > 0)
    tables = np.zeros((P, 2 * T), np.float32)
    tables[:, 0:T] = np.where(seen, d, 0)
    tables[:, T:] = np.where(seen, -np.log(np.maximum(times, 1)), MASKED)
    f = np.float32(10000.0) ** (-np.arange(64, dtype=np.float32) / np.float32(64))
    ang = np.arange(T, dtype=np.float32)[None, :] * np.concatenate([f, f])[:, None].astype(np.float32)
    ret = np.zeros((P, 6, T), np.float32)
    ret[:, 0] = np.cos(ang)
    ret[:, 1] = np.sin(ang) * np.where(i < 64, -1.0, 1.0)[:, None]
    rel = np.arange(T)[None, :] - i[:, None]
    for h in range(R_HEADS):
        log_g = np.log(np.float32(1.0 - 2.0 ** (-5.0 - h)))
        ret[:, 2 + h] = np.where(rel >= 0, np.exp(np.float64(log_g) * np.maximum(rel, 0)), 0.0) * 128.0 ** -0.5
    return cst, tables, ret


def kernel(**inputs):
    from concourse import bacc
    from concourse.bass_utils import run_bass_kernel_spmd

    w = {k: np.asarray(a) for k, a in inputs.items()}
    stream, w_dt = weight_stream(w)
    cst, att_tables, ret_tables = shape_constants()

    def by_feature(a):
        return np.ascontiguousarray(a.T.reshape(-1, P, a.shape[0]).transpose(1, 0, 2))

    arrays = {
        "weights": stream, "w_dt": w_dt, "x": by_feature(w["x"][0]), "p": by_feature(w["p_2"][0, 0]),
        "vectors": feature_vectors(w), "constants": cst, "att_tables": att_tables, "ret_tables": ret_tables,
    }
    nc = bacc.Bacc("TRN2", target_bir_lowering=False, num_devices=1)
    aps = [nc.dram_tensor(k, a.shape, F32, kind="ExternalInput").ap() for k, a in arrays.items()]
    acs = nc.dram_tensor("acs", (S_HEADS, T), F32, kind="Internal").ap()
    out = nc.dram_tensor("out", (P, C8, T), F32, kind="ExternalOutput").ap()
    block_program(nc, *aps, acs, out)
    r = run_bass_kernel_spmd(nc, [arrays], core_ids=[0])
    y = np.asarray(r.results[0]["out"])
    return np.ascontiguousarray(y.transpose(1, 0, 2).reshape(D, T).T)[None]
```

```python
import numpy as np

import concourse.bass as bass
from concourse import mybir

F32 = mybir.dt.float32
F32R = mybir.dt.float32r
ALU = mybir.AluOpType
ACT = mybir.ActivationFunctionType

P = 128
T = 512
D = 1024
C8 = D // P
QB = T // P
EPS = 1e-6
RING = 4
TILES = 8

N_HEADS, HEAD = 12, 64
ATT_W = N_HEADS * HEAD
PAIRS = N_HEADS // 2
S_HEADS, GROUPS, S_INNER, S_STATE = 32, 8, 2048, 128
HPG = S_HEADS // GROUPS
CONV4 = 4
FFN1 = 4096
D_CONV, CONV31, R_HEADS = 512, 31, 4
FFN2 = 2816
H2 = FFN2 // P
D_PLE = 256
MASKED = 1e30

def by_output(n):
    return [(j % 2, j // 2) for j in range(n)]


PHASES = {
    "att_first": (1, 3, 2, 1, [(0, 0), (1, 0), (0, 1)]),
    "attend": (PAIRS - 1, 4, 6, 5, [(0, 0), (1, 0), (0, 1), (1, 4)]),
    "att_last": (1, 1, 4, 4, [(1, 3)]),
    "ssm_first": (1, 6, 3, 3, by_output(6)),
    "ssm": (GROUPS - 1, 8, 7, 7, [*by_output(6), (1, 4), (1, 6)]),
    "gates_first": (1, 4, 2, 2, by_output(4)),
    "ssm_last": (1, 2, 4, 4, [(1, 1), (1, 3)]),
    "gates": (3, 4, 2, 2, by_output(4)),
    "mix_out": (2, 4, 2, 2, by_output(4)),
    "ffn": (4, 16, 8, 8, by_output(16)),
    "glu": (1, 8, 4, 4, by_output(8)),
    "retain": (R_HEADS, 4, 2, 2, by_output(4)),
    "mix2_out": (2, 4, 2, 2, by_output(4)),
    "swiglu": (H2 // 2, 4, 2, 2, by_output(4)),
    "down2": (2, 12, 2, 2, [None, None, (0, 0), None, None, (1, 0),
                            None, None, (0, 1), None, None, (1, 1)]),
    "ple_proj": (1, 4, 4, 4, [(1, 1), (1, 3), (1, 3), (1, 3)]),
    "ple_gate": (2, 4, 2, 2, by_output(4)),
}
UNIT0, OUT0 = {}, {}
_u, _a, _b = 0, 0, 0
for _name, (_t, _n, _p, _q, _) in PHASES.items():
    UNIT0[_name], OUT0[_name] = _u, (_a, _b)
    _u, _a, _b = _u + _t * _n, _a + _t * _p, _b + _t * _q
SLOTS = _u

VEC = {}
_at = 0
for _name, _n in (("pre1", 8), ("post1", 8), ("fpre1", 8), ("fpost1", 8), ("gate_b", 16), ("ssm_norm", 16),
                  ("d_skip", 16), ("conv4", GROUPS * 4 * (CONV4 + 1)),
                  ("pre2", 8), ("post2", 8), ("fpre2", 8), ("fpost2", 8), ("ple", 8),
                  ("conv31", 4 * (CONV31 + 1)), ("ln_w", 4), ("ln_b", 4),
                  ("dt_bias", S_HEADS), ("a_log", S_HEADS)):
    VEC[_name] = _at
    _at += _n
NVEC = _at

STATS = {}
_q, _k = 0, 0
for _name, _n, _chunks in (("pre1", 1, 8), ("ssm", GROUPS, 2), ("post1", 1, 8), ("fpre1", 1, 8), ("fpost1", 1, 8),
                           ("pre2", 1, 8), ("retain", R_HEADS, 1), ("ln", 0, 4), ("post2", 1, 8), ("fpre2", 1, 8),
                           ("fpost2", 1, 8), ("ple", 1, 8)):
    STATS[_name] = (_q, _k)
    _q, _k = _q + max(1, _n) * _chunks, _k + _n


class Turn:

    def __init__(self, name, i=0, first=0):
        _, self.slots, *self.outs, self.ends = PHASES[name]
        self.unit0 = UNIT0[name] - first * self.slots
        self.out0 = [a - first * n for a, n in zip(OUT0[name], self.outs)]
        self.i = i

    def unit(self, j):
        return self.i * self.slots + (self.unit0 + j)

    def slot(self, j):
        return (self.unit0 + j) % RING

    def out(self, bank, m):
        return self.i * self.outs[bank] + (self.out0[bank] + m)


def block_program(nc, weights, w_dt, x, p, vectors, constants, att_tables, ret_tables, acs_dram, out):
    base = (nc.sbuf_base + 63) // 64 * 64
    top = [base]

    def place(name, shape, dt=F32, at=None):
        size = 4 * int(np.prod(shape[1:]))
        offset = top[0] if at is None else at
        if at is None:
            top[0] += (size + 31) // 32 * 32
        return nc.alloc_sbuf_tensor_at(name, shape, dt, offset=offset)

    raw = place("raw", [P, RING, TILES * P])
    w_hi = place("w_hi", [P, RING, TILES * P], F32R)
    w_lo = place("w_lo", [P, RING, TILES * P], F32R)
    u_at = top[0]
    u_hi = place("u_hi", [P, C8, T], F32R)
    u_lo = place("u_lo", [P, C8, T], F32R)
    xs = place("xs", [P, C8, T])
    s_hi = place("s_hi", [P, 2, T], F32R)
    s_lo = place("s_lo", [P, 2, T], F32R)
    vec = place("vec", [P, NVEC])
    half = place("half", [P, 32])
    cst = place("cst", [P, 4 * P + N_HEADS])
    heads_t = place("heads_t", [P, 3, QB, S_HEADS])
    tiny = place("tiny", [P, 64])
    diag = place("diag", [P, T])
    sq = place("sq", [P, 2, T])
    ident, ones, tri, perm = (cst[:, k * P:(k + 1) * P] for k in range(4))
    slopes = cst[:, 4 * P:4 * P + N_HEADS]
    y_u = place("y_u", [P, C8, T], at=u_at)
    work = top[0]
    K = 1024

    att_acc = place("att_acc", [P, C8, T], at=work)
    ssm_acc = place("ssm_acc", [P, C8, T], at=work + 16 * K)
    a_at = work + 32 * K
    k_t = place("k_t", [P, T], at=a_at)
    q_t = place("q_t", [P, T], at=a_at + 2 * K)
    v_t = place("v_t", [P, T], at=a_at + 4 * K)
    v_tok = place("v_tok", [P, QB, P], at=a_at + 6 * K)
    dist = place("dist", [P, 2 * T], at=a_at + 8 * K)
    bias = place("bias", [P, 2, T], at=a_at + 12 * K)
    logits = place("logits", [P, 4, T], at=a_at + 16 * K)
    p_t = place("p_t", [P, 2, QB, P], at=a_at + 24 * K)
    dt_at = a_at + 28 * K
    dt_raw = place("dt_raw", [P, TILES * S_HEADS], at=dt_at)
    dt_hi, dt_lo = (a[:].rearrange("p a t -> p (a t)")[:, 0:TILES * S_HEADS] for a in (s_hi, s_lo))
    hd = place("hd", [P, 8, P], at=dt_at + K)
    acs_h = place("acs_h", [S_HEADS, T], at=dt_at + 5 * K)
    cat = place("cat", [P, 4, T + 3], at=a_at)
    g_at = a_at + 8256
    post = place("post", [P, 4, T], at=g_at)
    zz = place("zz", [P, 2, T], at=g_at + 8 * K)
    xd = place("xd", [P, QB, 2 * P], at=g_at + 12 * K)
    xw = place("xw", [P, QB, 2 * P], at=g_at + 16 * K)
    b_tok = place("b_tok", [P, QB, P], at=g_at + 20 * K)
    bc = place("bc", [P, HPG, T], at=g_at + 22 * K)
    gm = place("gm", [P, QB, P], at=g_at + 30 * K)
    states = place("states", [P, 3, 2 * P], at=g_at + 32 * K)
    y_g = place("y_g", [P, 2, T], at=g_at + 35 * K)
    decay = place("decay", [P, HPG, T], at=g_at + 39 * K)
    th = place("th", [P, 2, T], at=g_at + 47 * K)
    gate = place("gate", [P, 4, T], at=a_at)
    v_at = work + 40 * K
    v_hi = place("v_hi", [P, C8, T], F32R, at=v_at)
    v_lo = place("v_lo", [P, C8, T], F32R, at=v_at + 16 * K)
    t_at = work + 72 * K
    tmp = place("tmp", [P, 2, T], at=t_at)
    p_raw = place("p_raw", [P, 2, T], at=t_at + 12 * K)
    ffn_acc = place("ffn_acc", [P, C8, T], at=work)
    glu = place("glu", [P, 8, T], at=v_at)
    cat31 = place("cat31", [P, 4, T + CONV31 - 1], at=work)
    cv = place("cv", [P, 4, T], at=work + 8704)
    rt = place("rt", [P, 6, T], at=work + 17 * K)
    r_at = work + 29 * K
    r_q = place("r_q", [P, T], at=r_at)
    r_k = place("r_k", [P, T], at=r_at + 2 * K)
    r_v = place("r_v", [P, T], at=r_at + 4 * K)
    r_g = place("r_g", [P, 2, T], at=r_at + 6 * K)
    rot_q = place("rot_q", [P, T], at=t_at)
    rot_k = place("rot_k", [P, T], at=t_at + 2 * K)
    rot_s = place("rot_s", [P, 2, T], at=t_at + 4 * K)
    r_vtok = place("r_vtok", [P, QB, P], at=t_at + 8 * K)
    r_s = place("r_s", [P, QB * (QB + 1) // 2 * P], at=t_at + 10 * K)
    r_o = place("r_o", [P, T], at=t_at + 15 * K)
    cv_odd = place("cv_odd", [P, T], at=t_at + 17 * K)
    S_OFF = [0, 512, 896, 1152]
    h_hi = place("h_hi", [P, H2, T], F32R, at=work)
    h_lo = place("h_lo", [P, H2, T], F32R, at=work + 44 * K)
    h_tmp = place("h_tmp", [P, T], at=work + 88 * K)
    pj = place("pj", [P, C8, T], at=work)
    ple_tanh = place("ple_tanh", [P, 2, T], at=t_at)

    ps = [nc.alloc_psum_tensor(f"bank{i}", [P, T], F32) for i in range(8)]
    ms, rb = ps[2], ps[3]

    sems = {}

    def sem(name):
        if name not in sems:
            sems[name] = nc.alloc_semaphore(name)
        return sems[name]

    landed = [sem(f"slot_landed{s}") for s in range(RING)]
    hi_done, lo_done, slot_inside = sem("hi_done"), sem("lo_done"), sem("slot_ended_inside_output")
    out_ready = [sem("out_ready0"), sem("out_ready1")]
    out_free = [sem("out_free0"), sem("out_free1")]
    sq_ready, sq_used = sem("sq_ready"), sem("sq_used")
    var_ready, sd_ready = sem("var_ready"), sem("sd_ready")
    diag_ready, rb_ready = sem("diag_ready"), sem("rb_ready")
    n_ready, u_hi_ready, u_ready = sem("n_ready"), sem("u_hi_ready"), sem("u_ready")
    x_ready = sem("x_ready")

    def v(name, k=0, n=1):
        return vec[:, VEC[name] + k:VEC[name] + k + n]

    def freed(engine, turn, bank, m):
        engine.wait_ge(out_free[bank], turn.out(bank, m) + 2)

    def ended(engine, turn, j):
        if j < 0:
            engine.wait_ge(out_ready[0], turn.out(0, 0))
            engine.wait_ge(out_ready[1], turn.out(1, 0))
        elif turn.ends[j]:
            bank, m = turn.ends[j]
            engine.wait_ge(out_ready[bank], turn.out(bank, m) + 1)
        else:
            engine.wait_ge(slot_inside, turn.i * 8 + (j - j // 3 + 1))

    block = nc.Block()
    with block:

        @block.sync
        def _(sp):
            sp.dma_start(xs[:], x).then_inc(sem("x_landed"), 16)
            sp.dma_start(vec[:], vectors).then_inc(sem("const_landed"), 16)
            sp.dma_start(cst[:], constants).then_inc(sem("const_landed"), 16)
            stream = weights.rearrange("(g r) p n -> g r p n", r=RING)
            for s in range(RING):
                sp.dma_start(raw[:, s, :], stream[0, s]).then_inc(landed[s], 16)
            sp.dma_start(dt_raw[:], w_dt).then_inc(sem("dtw_landed"), 16)
            sp.dma_start(dist[:], att_tables).then_inc(sem("dist_landed"), 16)
            with sp.Fori(1, SLOTS // RING) as g:
                for s in range(RING):
                    sp.wait_ge(lo_done, g * RING + (s + 1 - RING))
                    sp.dma_start(raw[:, s, :], stream[g, s]).then_inc(landed[s], 16)
            for c in range(C8):
                sp.wait_ge(sem("result_ready"), c + 1)
                sp.dma_start(out[:, c, :], xs[:, c, :]).then_inc(sem("stored"), 16)
            sp.wait_ge(sem("stored"), 16 * C8)

        @block.gpsimd
        def _(pool):
            with pool.Fori(0, SLOTS // RING) as g:
                for s in range(RING):
                    pool.wait_ge(hi_done, g * RING + (s + 1))
                    nc.gpsimd.tensor_tensor(w_lo[:, s, :], raw[:, s, :], w_hi[:, s, :].bitcast(F32),
                                            ALU.subtract).then_inc(lo_done, 1)

        @block.tensor
        def _(pe):
            mm = nc.tensor.matmul

            def exact(dst, slot, tile, hi, lo, first, last):
                w = slice(tile * P, tile * P + P)
                mm(dst, w_hi[:, slot, w], hi, start=first, stop=False)
                mm(dst, w_hi[:, slot, w], lo, start=False, stop=False)
                return mm(dst, w_lo[:, slot, w], hi, start=False, stop=last)

            def unit(turn, j, bank, m, hi, lo, ready=None, ready0=0, tiles=None, first=True, last=True):
                pe.wait_ge(lo_done, turn.unit(j) + 1)
                if first:
                    pe.wait_ge(out_free[bank], turn.out(bank, m) + 1)
                tiles = tiles or [(t, t) for t in range(TILES)]
                for n, (t, c) in enumerate(tiles):
                    if ready is not None:
                        pe.wait_ge(ready, ready0 + c + 1)
                    last_mm = exact(ps[bank][:], turn.slot(j), t, hi[:, c, :], lo[:, c, :],
                                    first and n == 0, last and n == len(tiles) - 1)
                last_mm.then_inc(out_ready[bank] if last else slot_inside, 1)

            def unit_pair(turn, hi, lo, ready, ready0, m0=0, m1=0):
                for j in range(2):
                    pe.wait_ge(lo_done, turn.unit(j) + 1)
                    pe.wait_ge(out_free[j], turn.out(j, (m0, m1)[j]) + 1)
                for c in range(TILES):
                    pe.wait_ge(ready, ready0 + c + 1)
                    for j in range(2):
                        last_mm = exact(ps[j][:], turn.slot(j), c, hi[:, c, :], lo[:, c, :], c == 0, c == TILES - 1)
                        if c == TILES - 1:
                            last_mm.then_inc(out_ready[j], 1)

            def stat_chunk(q, c, n):
                pe.wait_ge(sq_ready, q + 1)
                for t in range(QB):
                    last_mm = mm(ms[:, t:t + 1], sq[:, c % 2, t * P:(t + 1) * P], ones[:, 0:1],
                                 start=(c == 0 and t == 0), stop=(c == n - 1 and t == QB - 1),
                                 skip_group_check=True)
                last_mm.then_inc(sq_used, 1)

            def stat_broadcast(k):
                pe.wait_ge(diag_ready, k + 1)
                mm(rb[:], ones, diag[:], start=True, stop=True).then_inc(rb_ready, 1)

            def norm(name, n=C8):
                q, k = STATS[name]
                for c in range(n):
                    stat_chunk(q + c, c, n)
                stat_broadcast(k)

            pe.wait_ge(sem("const_landed"), 32)
            norm("pre1")
            turn = Turn("att_first")
            unit_pair(turn, u_hi, u_lo, u_ready, 0)
            unit(turn, 2, 0, 1, u_hi, u_lo)
            pe.wait_ge(sem("dtw_ready"), 1)
            for t in range(QB):
                rows, dst = slice(t * P, (t + 1) * P), ps[7][:, t * S_HEADS:(t + 1) * S_HEADS]
                for c in range(C8):
                    w = slice(c * S_HEADS, (c + 1) * S_HEADS)
                    mm(dst, u_hi[:, c, rows], dt_hi[:, w], start=(c == 0), stop=False)
                    mm(dst, u_hi[:, c, rows], dt_lo[:, w], start=False, stop=False)
                    last = mm(dst, u_lo[:, c, rows], dt_hi[:, w], start=False, stop=(c == C8 - 1))
            last.then_inc(sem("dt_logits"), 1)

            def attention(turn, i, between):
                def scores(b):
                    h, qb = divmod(b, QB)
                    if b == 0:
                        freed(pe, turn, 0, 0)
                        freed(pe, turn, 1, 0)
                    if b >= 3:
                        pe.wait_ge(sem("logits_done"), i * 8 + (b - 2))
                    rows = slice(h * HEAD, h * HEAD + HEAD)
                    n = (qb + 1) * P
                    mm(ps[3 + b % 3][:, 0:n], q_t[rows, qb * P:(qb + 1) * P], k_t[rows, 0:n],
                       start=True, stop=True).then_inc(sem("scores_ready"), 1)

                def turned(b):
                    pe.wait_ge(sem("probs_ready"), i * 8 + b + 1)
                    if b >= 2:
                        pe.wait_ge(sem("p_t_ready"), i * 8 + (b - 1))
                    if b == 1:
                        pe.wait_ge(sem("v_tok_ready"), i + 1)
                    for kb in range(b % QB + 1):
                        last = nc.tensor.transpose(ps[2 + 4 * (b % 2)][:, kb * P:(kb + 1) * P],
                                                   logits[:, b % 4, kb * P:(kb + 1) * P], ident)
                    last.then_inc(sem("turned"), 1)

                def attended(b):
                    h, qb = divmod(b, QB)
                    pe.wait_ge(sem("p_t_ready"), i * 8 + b + 1)
                    if b == 0:
                        pe.wait_ge(sem("v_tok_ready"), i + 1)
                        pe.wait_ge(sem("dt_read"), 1)
                    for kb in range(qb + 1):
                        last = mm(ps[7][h * HEAD:(h + 1) * HEAD, qb * P:(qb + 1) * P],
                                  v_tok[:, kb, h * HEAD:(h + 1) * HEAD], p_t[:, b % 2, kb, :],
                                  start=(kb == 0), stop=(kb == qb))
                    last.then_inc(sem("attended"), 1)

                for b in range(3):
                    scores(b)
                freed(pe, turn, 0, 1)
                for t in range(QB):
                    last = nc.tensor.transpose(ps[6][:, t * P:(t + 1) * P], v_t[:, t * P:(t + 1) * P], ident)
                last.then_inc(sem("v_turned"), 1)
                for b in range(8):
                    between(b)
                    turned(b)
                    if b + 3 < 8:
                        scores(b + 3)
                    if b >= 1:
                        attended(b - 1)
                attended(7)

            def att_project(turn, slot, i, n, m0, m1):
                bank = n % 2
                if n == 0:
                    pe.wait_ge(lo_done, turn.unit(slot) + 1)
                    pe.wait_ge(sem("att_split"), i + 1)
                pe.wait_ge(out_free[bank], turn.out(bank, (m0, m1)[bank] + n // 2) + 1)
                exact(ps[bank][:], turn.slot(slot), n, s_hi[:, 0, :], s_lo[:, 0, :], True, True)\
                    .then_inc(out_ready[bank], 1)

            attention(turn, 0, lambda b: None)
            with pe.Fori(1, PAIRS) as i:
                turn = Turn("attend", i, 1)
                for j in range(3):
                    unit(turn, j, j % 2, j // 2, u_hi, u_lo)
                attention(turn, i, lambda b: att_project(turn, 3, i - 1, b, 2, 1))
            turn = Turn("att_last")
            pe.wait_ge(sem("la_ready"), 1)
            mm(ps[4][:, 0:P], tri, hd[:, 4, :], start=True, stop=True).then_inc(sem("acs_sum"), 1)
            mm(ps[5][:, 0:P], ones, hd[:, 4, :], start=True, stop=True).then_inc(sem("acs_sum"), 1)
            for n in range(C8):
                att_project(turn, 0, PAIRS - 1, n, 0, 0)
            pe.wait_ge(sem("acs_tok"), 1)
            for t in range(QB):
                last = nc.tensor.transpose(ps[3][0:S_HEADS, t * P:(t + 1) * P], heads_t[:, 1, t, :], ident)
            last.then_inc(sem("acs_turned"), 1)

            q0, k0 = STATS["ssm"]

            def ssm_group(i, between):
                for j in range(2):
                    pe.wait_ge(sem("silu_done"), i * 4 + j + 1)
                    for t in range(QB):
                        last = nc.tensor.transpose(ps[2 + j][:, t * P:(t + 1) * P],
                                                   post[:, j, t * P:(t + 1) * P], ident)
                    last.then_inc(sem("x_turned"), 1)
                pe.wait_ge(sem("silu_done"), i * 4 + 3)
                for t in range(QB):
                    last = nc.tensor.transpose(ps[4][:, t * P:(t + 1) * P], post[:, 2, t * P:(t + 1) * P], ident)
                last.then_inc(sem("b_turned"), 1)
                pe.wait_ge(sem("silu_done"), i * 4 + 4)
                for t in range(QB):
                    w = slice(t * P, (t + 1) * P)
                    last = mm(ps[5][:, w], post[:, 2, w], post[:, 3, w], start=True, stop=True)
                last.then_inc(sem("bc_product"), 1)
                between(0)
                pe.wait_ge(sem("xw_ready"), i * 2 + 2)
                pe.wait_ge(sem("b_tok_ready"), i + 1)
                for c in range(3):
                    last = mm(ps[2 + c // 2][:, c % 2 * 256:c % 2 * 256 + 256], b_tok[:, c, :], xw[:, c, :],
                              start=True, stop=True)
                last.then_inc(sem("state_sums"), 1)
                between(1)
                for h in range(HPG):
                    rows = slice(h % 2 * HEAD, h % 2 * HEAD + HEAD)
                    cols = slice(h * HEAD, h * HEAD + HEAD)
                    pe.wait_ge(sem("kernel_ready"), i * 4 + h + 1)
                    pe.wait_ge(sem("c_decayed"), i * 4 + h + 1)
                    if h == 0:
                        pe.wait_ge(sem("states_ready"), i + 1)
                    for c in range(QB):
                        w = slice(c * P, (c + 1) * P)
                        last = mm(ps[6 + h // 2][rows, w], xd[:, c, cols], decay[:, h, w],
                                  start=True, stop=(c == 0))
                        if c:
                            last = mm(ps[6 + h // 2][rows, w], states[:, c - 1, cols], bc[:, h, w],
                                      start=False, stop=True)
                    last.then_inc(sem("y_done"), 1)
                    if h == 1:
                        between(2)
                between(3)
                for c in range(2):
                    stat_chunk(i * 2 + (q0 + c), c, 2)
                between(4)
                stat_broadcast(i + k0)
                between(5)

            def ssm_project(turn, slot0, i, m0):
                for n in range(C8):
                    bank = n % 2
                    pe.wait_ge(out_free[bank], turn.out(bank, m0 + n // 2) + 1)
                    if n % 4 == 0:
                        pe.wait_ge(lo_done, turn.unit(slot0 + n // 4) + 1)
                    for c in range(2):
                        if n == 0:
                            pe.wait_ge(sem("ssm_split"), i * 2 + c + 1)
                        last = exact(ps[bank][:], turn.slot(slot0 + n // 4), n % 4 * 2 + c, s_hi[:, c, :],
                                     s_lo[:, c, :], c == 0, c == 1)
                    last.then_inc(out_ready[bank], 1)

            def some_unit(turn, count):
                return lambda j: unit(turn, j, j % 2, j // 2, u_hi, u_lo) if j < count else None

            turn = Turn("ssm_first")
            for j in range(6):
                unit(turn, j, j % 2, j // 2, u_hi, u_lo)
            with pe.Fori(0, GROUPS - 1) as i:
                turn = Turn("ssm", i)
                ssm_group(i, some_unit(turn, 6))
                ssm_project(turn, 6, i, 3)
            ssm_group(GROUPS - 1, some_unit(Turn("gates_first"), 4))
            ssm_project(Turn("ssm_last"), 0, GROUPS - 1, 0)

            with pe.Fori(0, 3) as i:
                turn = Turn("gates", i)
                for j in range(4):
                    unit(turn, j, j % 2, j // 2, u_hi, u_lo)

            def outputs_with_stats(name, stat, hi, lo, ready, ready0=0):
                q, k = STATS[stat]
                for i in range(2):
                    turn = Turn(name, i)
                    for j in range(4):
                        c = 4 * i + j
                        if c == 0:
                            unit_pair(turn, hi, lo, ready, ready0)
                            continue
                        if c > 1:
                            unit(turn, j, j % 2, j // 2, hi, lo)
                        stat_chunk(q + c - 1, c - 1, C8)
                stat_chunk(q + C8 - 1, C8 - 1, C8)
                stat_broadcast(k)

            outputs_with_stats("mix_out", "post1", v_hi, v_lo, sem("mixed_ready"))
            norm("fpre1")

            with pe.Fori(0, 4) as i:
                turn = Turn("ffn", i)
                unit_pair(turn, u_hi, u_lo, u_ready, 8)
                for j in range(2, 8):
                    unit(turn, j, j % 2, j // 2, u_hi, u_lo)
                for j in range(8):
                    unit(turn, 8 + j, j % 2, 4 + j // 2, v_hi, v_lo,
                         sem("hidden_ready") if j == 0 else None, i * 8)
            norm("fpost1")
            norm("pre2")

            turn = Turn("glu")
            unit_pair(turn, u_hi, u_lo, u_ready, 16)
            for j in range(2, 8):
                unit(turn, j, j % 2, j // 2, u_hi, u_lo)
            q0, k0 = STATS["retain"]

            def retention(i, between):
                turn = Turn("retain", i)
                freed(pe, turn, 0, 0)
                mm(ps[4][:], perm, r_q[:], start=True, stop=True).then_inc(sem("swapped"), 1)
                freed(pe, turn, 1, 0)
                mm(ps[5][:], perm, r_k[:], start=True, stop=True).then_inc(sem("swapped"), 1)
                freed(pe, turn, 0, 1)
                for t in range(QB):
                    last = nc.tensor.transpose(ps[6][:, t * P:(t + 1) * P], r_v[:, t * P:(t + 1) * P], ident)
                last.then_inc(sem("r_v_turned"), 1)
                between(0)
                pe.wait_ge(sem("rotated"), i * 2 + 2)
                for kb in range(QB):
                    n = T - kb * P
                    if kb >= 2:
                        pe.wait_ge(sem("decayed"), i * 4 + (kb - 1))
                    mm(ps[4 + kb % 2][:, 0:n], rot_k[:, kb * P:(kb + 1) * P], rot_q[:, kb * P:T],
                       start=True, stop=True).then_inc(sem("r_scores"), 1)
                between(1)
                pe.wait_ge(sem("r_vtok_ready"), i + 1)
                for kb in range(QB):
                    n = T - kb * P
                    pe.wait_ge(sem("decayed"), i * 4 + kb + 1)
                    last = mm(ps[7][:, kb * P:T], r_vtok[:, kb, :], r_s[:, S_OFF[kb]:S_OFF[kb] + n],
                              start=(kb == 0), stop=(kb == QB - 1), skip_group_check=True)
                last.then_inc(sem("retained"), 1)
                between(2)
                stat_chunk(i + q0, 0, 1)
                between(3)
                stat_broadcast(i + k0)

            turn = Turn("retain")
            for j in range(4):
                unit(turn, j, j % 2, j // 2, u_hi, u_lo)
            with pe.Fori(1, R_HEADS) as i:
                retention(i - 1, some_unit(Turn("retain", i), 4))
            retention(R_HEADS - 1, lambda n: None)
            q0, k0 = STATS["ln"]
            for c in range(4):
                pe.wait_ge(sem("conv_done"), c + 1)
                for t in range(QB):
                    last = mm(ms[:, t:t + 1], cv[:, c, t * P:(t + 1) * P], ones[:, 0:1],
                              start=(c == 0 and t == 0), stop=(c == 3 and t == 3), skip_group_check=True)
            last.then_inc(sem("mean_sum"), 1)
            pe.wait_ge(sem("mean_diag"), 1)
            mm(rb[:], ones, diag[:], start=True, stop=True).then_inc(sem("mean_ready"), 1)
            for c in range(4):
                stat_chunk(q0 + c, c, 4)
            pe.wait_ge(sem("ln_diag"), 1)
            mm(rb[:], ones, diag[:], start=True, stop=True).then_inc(sem("ln_ready"), 1)
            pe.wait_ge(sem("ret_split"), R_HEADS)
            outputs_with_stats("mix2_out", "post2", v_hi, v_lo, sem("y2_ready"))
            norm("fpre2")

            with pe.Fori(0, H2 // 2) as i:
                turn = Turn("swiglu", i)
                unit_pair(turn, u_hi, u_lo, u_ready, 24)
                for j in range(2, 4):
                    unit(turn, j, j % 2, j // 2, u_hi, u_lo)
            q, k = STATS["fpost2"]
            for i in range(2):
                turn = Turn("down2", i)
                for n in range(4):
                    for s in range(3):
                        chunks = range(s * TILES, min(H2, (s + 1) * TILES))
                        unit(turn, 3 * n + s, n % 2, n // 2, h_hi, h_lo,
                             sem("hidden2_ready") if (i, n) == (0, 0) else None, 0,
                             [(t, c) for t, c in enumerate(chunks)], first=(s == 0), last=(s == 2))
                    c = 4 * i + n
                    if c:
                        stat_chunk(q + c - 1, c - 1, C8)
            stat_chunk(q + C8 - 1, C8 - 1, C8)
            stat_broadcast(k)
            turn = Turn("ple_proj")
            pe.wait_ge(sem("p_split"), 1)
            for n in range(C8):
                bank = n % 2
                if n % 4 == 0:
                    pe.wait_ge(lo_done, turn.unit(n // 4) + 1)
                pe.wait_ge(out_free[bank], turn.out(bank, n // 2) + 1)
                for c in range(2):
                    last = exact(ps[bank][:], turn.slot(n // 4), n % 4 * 2 + c, s_hi[:, c, :], s_lo[:, c, :],
                                 c == 0, c == 1)
                last.then_inc(out_ready[bank], 1)
            outputs_with_stats("ple_gate", "ple", u_hi, u_lo, u_ready, 32)

        @block.scalar
        def _(act):
            af = nc.scalar.activation

            def split(u, slot):
                if isinstance(u, int):
                    act.wait_ge(landed[slot], 16 * (u // RING + 1))
                else:
                    act.wait_ge(landed[slot], (u - slot) * (16 // RING) + 16)
                af(w_hi[:, slot, :], raw[:, slot, :], ACT.Copy).then_inc(hi_done, 1)

            def ahead(turn, j):
                if isinstance(turn.unit(j), int) and turn.unit(j) + 3 >= SLOTS:
                    return
                if not isinstance(turn.unit(j), int) or turn.unit(j) > 0:
                    ended(act, turn, j - 1)
                split(turn.unit(j + 3), turn.slot(j + 3))

            def ready(turn, bank, m):
                act.wait_ge(out_ready[bank], turn.out(bank, m) + 1)

            def square(q, c, src, wait_all=False):
                if not isinstance(q, int) or q >= 2:
                    act.wait_ge(sq_used, q if wait_all else q - 1)
                return af(sq[:, c % 2, :], src, ACT.Square).then_inc(sq_ready, 1)

            def stat_root(k):
                act.wait_ge(var_ready, k + 1)
                af(tiny[:, 4:8], tiny[:, 0:4], ACT.Sqrt).then_inc(sd_ready, 1)

            def x_squares(name, first_x):
                q, k = STATS[name]
                for c in range(C8):
                    act.wait_ge(x_ready, first_x + c + 1)
                    square(q + c, c, xs[:, c, :])
                stat_root(k)

            def round_u(n0):
                for c in range(C8):
                    act.wait_ge(n_ready, n0 + c + 1)
                    af(u_hi[:, c, :], sq[:, c % 2, :], ACT.Copy).then_inc(u_hi_ready, 1)

            def outputs(turn_name, stat):
                q, k = STATS[stat]
                for i in range(2):
                    turn = Turn(turn_name, i)
                    for j in range(4):
                        ahead(turn, j)
                        ready(turn, j % 2, j // 2)
                        c = 4 * i + j
                        square(q + c, c, ps[j % 2][:])
                        af(y_u[:, c, :], ps[j % 2][:], ACT.Copy).then_inc(out_free[j % 2], 1)
                stat_root(k)

            act.wait_ge(sem("x_landed"), 16)
            for c in range(C8):
                square(c, c, xs[:, c, :])
            split(0, 0)
            stat_root(0)
            act.wait_ge(sem("dtw_landed"), 16)
            af(dt_hi, dt_raw[:], ACT.Copy).then_inc(sem("dtw_hi"), 1)
            split(1, 1)
            split(2, 2)
            round_u(0)

            def att_in(turn):
                ahead(turn, 0)
                ready(turn, 0, 0)
                af(k_t[:], ps[0][:], ACT.Copy).then_inc(out_free[0], 1)
                ahead(turn, 1)
                ready(turn, 1, 0)
                af(q_t[:], ps[1][:], ACT.Copy, scale=-float(HEAD) ** -0.5).then_inc(out_free[1], 1)
                ahead(turn, 2)
                ready(turn, 0, 1)
                af(v_t[:], ps[0][:], ACT.Copy).then_inc(out_free[0], 1)

            def attention(i):
                def p_copy(b):
                    act.wait_ge(sem("turned"), i * 8 + b + 1)
                    if b >= 2:
                        act.wait_ge(sem("attended"), i * 8 + (b - 1))
                    n = b % QB + 1
                    af(p_t[:, b % 2, 0:n, :].rearrange("p k t -> p (k t)"), ps[2 + 4 * (b % 2)][:, 0:n * P],
                       ACT.Copy).then_inc(sem("p_t_ready"), 1)

                for b in range(8):
                    n = (b % QB + 1) * P
                    act.wait_ge(sem("logits_done"), i * 8 + b + 1)
                    af(logits[:, b % 4, 0:n], logits[:, b % 4, 0:n], ACT.Exp, scale=-1.0,
                       bias=tiny[:, 8 + b:9 + b], accum_out=tiny[:, 16 + b:17 + b])\
                        .then_inc(sem("exp_done"), 1)
                    if b >= 2:
                        p_copy(b - 2)
                p_copy(6)
                p_copy(7)
                act.wait_ge(sem("attended"), i * 8 + 8)
                af(s_hi[:, 0, :], ps[7][:], ACT.Copy).then_inc(sem("att_hi"), 1)

            att_in(Turn("att_first"))
            attention(0)
            act.wait_ge(sem("dt_abs"), 1)
            af(hd[:, 4, :], hd[:, 3, :], ACT.Exp, scale=-1.0).then_inc(sem("dt_exp"), 1)
            af(hd[:, 7, 0:S_HEADS], v("a_log", 0, S_HEADS), ACT.Exp).then_inc(sem("dt_exp"), 1)
            with act.Fori(1, PAIRS) as i:
                turn = Turn("attend", i, 1)
                att_in(turn)
                ahead(turn, 3)
                attention(i)
            ahead(Turn("att_last"), 0)
            act.wait_ge(sem("dt_to_end"), 1)
            af(hd[:, 5, :], hd[:, 5, :], ACT.Exp).then_inc(sem("dt_exp"), 1)
            act.wait_ge(sem("acs_turned"), 1)
            af(acs_h[:], ps[3][0:S_HEADS, :], ACT.Copy).then_inc(sem("acs_ready"), 1)
            act.wait_ge(sem("acs_ready"), 1)
            act.dma_start(acs_dram, acs_h[:]).then_inc(sem("acs_stored"), 16)

            q0, k0 = STATS["ssm"]
            acs_rows = acs_dram.rearrange("(g h) t -> g h t", h=HPG)

            def to_cat(turn, j):
                ahead(turn, j)
                ready(turn, j % 2, j // 2)
                af(cat[:, j, 3:T + 3], ps[j % 2][:], ACT.Copy).then_inc(out_free[j % 2], 1)

            def z_tanh(turn, j):
                ahead(turn, 4 + j)
                ready(turn, j, 2)
                af(zz[:, j, :], ps[j][:], ACT.Tanh, scale=0.5).then_inc(sem("z_tanh"), 1)

            def tanh_conv(g, j):
                act.wait_ge(sem("conv4_done"), g * 4 + (j + 1))
                if j >= 2:
                    act.wait_ge(sem("silu_done"), g * 4 + (j - 1))
                af(th[:, j % 2, :], post[:, j, :], ACT.Tanh, scale=0.5).then_inc(sem("tanh_done"), 1)

            def to_gate(turn, j):
                ahead(turn, j)
                ready(turn, j % 2, j // 2)
                if turn.slots == 4 and not isinstance(turn.i, int):
                    act.wait_ge(sem("mixed"), turn.i * 2 + (j // 2 + 1))
                    col = turn.i * 2 + (2 + 8 * (j % 2) + j // 2)
                    bias_half = half[:, bass.ds(col, 1)]
                else:
                    bias_half = half[:, 8 * (j % 2) + j // 2:8 * (j % 2) + j // 2 + 1]
                af(gate[:, j, :], ps[j % 2][:], ACT.Tanh, scale=0.5, bias=bias_half).then_inc(out_free[j % 2], 1)

            def load_decays(g):
                act.dma_start(bc[:], acs_rows[g].partition_broadcast(P)).then_inc(sem("bc_landed"), 16)

            def decays_of_head(i, h):
                act.wait_ge(sem("differences"), i * 4 + (h + 1))
                af(decay[:, h, :], decay[:, h, :], ACT.Exp).then_inc(sem("decay_exp"), 1)
                if h == 0:
                    act.wait_ge(sem("ends_done"), i + 1)
                af(bc[:, h, :], bc[:, h, :], ACT.Exp).then_inc(sem("bc_exp"), 1)

            def y_square(i, j):
                act.wait_ge(sem("y_gated"), i * 2 + (j + 1))
                square(i * 2 + (q0 + j), j, y_g[:, j, :])

            def y_high(i):
                for j in range(2):
                    act.wait_ge(sem("y_normed"), i * 2 + (j + 1))
                    af(s_hi[:, j, :], y_g[:, j, :], ACT.Copy).then_inc(sem("ssm_hi"), 1)

            def group_start(i):
                act.wait_ge(sem("bc_landed"), i * 16 + 16)
                af(tiny[:, 24:40].rearrange("p (h c) -> p h c", h=HPG), bc[:, :, P - 1:T:P], ACT.Exp)\
                    .then_inc(sem("ends_done"), 1)
                act.wait_ge(sem("b_turned"), i + 1)
                af(b_tok[:].rearrange("p c n -> p (c n)"), ps[4][:], ACT.Copy).then_inc(sem("b_tok_ready"), 1)

            def first_state(i):
                act.wait_ge(sem("state_sums"), i + 1)
                af(states[:, 0, :], ps[2][:, 0:256], ACT.Copy).then_inc(sem("state0"), 1)

            turn = Turn("ssm_first")
            to_cat(turn, 0)
            act.wait_ge(sem("acs_stored"), 16)
            act.wait_ge(sem("heads_ready"), 1)
            load_decays(0)
            for j in range(1, 4):
                to_cat(turn, j)
                tanh_conv(0, j - 1)
            z_tanh(turn, 0)
            tanh_conv(0, 3)
            z_tanh(turn, 1)
            with act.Fori(0, GROUPS - 1) as i:
                turn = Turn("ssm", i)
                group_start(i)
                decays_of_head(i, 0)
                decays_of_head(i, 1)
                to_cat(turn, 0)
                decays_of_head(i, 2)
                decays_of_head(i, 3)
                first_state(i)
                to_cat(turn, 1)
                y_square(i, 0)
                tanh_conv(i + 1, 0)
                to_cat(turn, 2)
                y_square(i, 1)
                load_decays(i + 1)
                to_cat(turn, 3)
                tanh_conv(i + 1, 1)
                stat_root(i + k0)
                z_tanh(turn, 0)
                y_high(i)
                tanh_conv(i + 1, 2)
                z_tanh(turn, 1)
                tanh_conv(i + 1, 3)
                ahead(turn, 6)
                ahead(turn, 7)
            i, turn = GROUPS - 1, Turn("gates_first")
            group_start(i)
            decays_of_head(i, 0)
            decays_of_head(i, 1)
            to_gate(turn, 0)
            decays_of_head(i, 2)
            decays_of_head(i, 3)
            first_state(i)
            to_gate(turn, 1)
            y_square(i, 0)
            to_gate(turn, 2)
            y_square(i, 1)
            stat_root(i + k0)
            y_high(i)
            to_gate(turn, 3)
            turn = Turn("ssm_last")
            ahead(turn, 0)
            ahead(turn, 1)

            def mixed_high(c):
                for n in range(2):
                    act.wait_ge(sem("mixed"), c + (n + 1))
                    af(v_hi[:, c + n, :], tmp[:, n, :], ACT.Copy).then_inc(sem("mixed_hi"), 1)

            with act.Fori(0, 3) as i:
                turn = Turn("gates", i)
                mixed_high(i * 2)
                for j in range(4):
                    to_gate(turn, j)
            mixed_high(6)

            outputs("mix_out", "post1")
            x_squares("fpre1", 0)
            round_u(8)
            act.wait_ge(u_ready, 16)
            act.dma_start(rt[:], ret_tables).then_inc(sem("rt_landed"), 16)
            act.dma_start(p_raw[:], p).then_inc(sem("p_landed"), 16)

            with act.Fori(0, 4) as i:
                turn = Turn("ffn", i)

                def round_hidden(j):
                    freed(act, turn, j % 2, j // 2)
                    af(v_hi[:, j, :], tmp[:, j % 2, :], ACT.Copy).then_inc(sem("hidden_hi"), 1)

                for j in range(8):
                    ahead(turn, j)
                    ready(turn, j % 2, j // 2)
                    if j >= 2:
                        act.wait_ge(sem("hidden_ready"), i * 8 + (j - 1))
                    af(tmp[:, j % 2, :], ps[j % 2][:], ACT.Relu).then_inc(sem("relu_done"), 1)
                    if j:
                        round_hidden(j - 1)
                round_hidden(7)
                for j in range(8):
                    ahead(turn, 8 + j)
            act.wait_ge(sem("p_landed"), 16)
            af(s_hi[:], p_raw[:], ACT.Copy).then_inc(sem("p_hi"), 1)
            act.wait_ge(out_free[0], OUT0["glu"][0] + 1)
            act.wait_ge(out_free[1], OUT0["glu"][1] + 1)
            q, k = STATS["fpost1"]
            for c in range(C8):
                square(q + c, c, ffn_acc[:, c, :])
            stat_root(k)
            x_squares("pre2", 8)
            round_u(16)

            turn = Turn("glu")
            for n in range(4):
                ahead(turn, 2 * n)
                ready(turn, 0, n)
                af(glu[:, 2 * n, :], ps[0][:], ACT.Copy, scale=0.5).then_inc(out_free[0], 1)
                ahead(turn, 2 * n + 1)
                ready(turn, 1, n)
                af(glu[:, 2 * n + 1, :], ps[1][:], ACT.Tanh, scale=0.5).then_inc(out_free[1], 1)

            q0, k0 = STATS["retain"]

            def retain_in(turn, j, dst):
                ahead(turn, j)
                ready(turn, j % 2, j // 2)
                if not isinstance(turn.i, int):
                    if j < 2:
                        act.wait_ge(sem("rotated"), turn.i * 2)
                    else:
                        act.wait_ge(sem("r_v_turned"), turn.i)
                af(dst[:], ps[j % 2][:], ACT.Copy).then_inc(out_free[j % 2], 1)

            def retain_gate(turn):
                ready(turn, 1, 1)
                af(r_g[:, 0, :], ps[1][:], ACT.Copy, scale=0.5)
                af(r_g[:, 1, :], ps[1][:], ACT.Tanh, scale=0.5).then_inc(out_free[1], 1)

            def values_by_token(head):
                act.wait_ge(sem("r_v_turned"), head + 1)
                af(r_vtok[:].rearrange("p k t -> p (k t)"), ps[6][:], ACT.Copy).then_inc(sem("r_vtok_ready"), 1)

            def retained_root(head):
                act.wait_ge(sem("retained"), head + 1)
                square(head + q0, 0, ps[7][:], wait_all=True)
                stat_root(head + k0)

            def retained_high(head):
                act.wait_ge(sem("ret_normed"), head + 1)
                af(v_hi[:, head + 4, :], r_o[:], ACT.Copy).then_inc(sem("ret_hi"), 1)

            turn = Turn("retain")
            for j, dst in enumerate((r_q, r_k, r_v)):
                retain_in(turn, j, dst)
            ahead(turn, 3)
            retain_gate(turn)
            with act.Fori(1, R_HEADS) as i:
                turn = Turn("retain", i)
                values_by_token(i - 1)
                for j, dst in enumerate((r_q, r_k, r_v)):
                    retain_in(turn, j, dst)
                retained_root(i - 1)
                ahead(turn, 3)
                retained_high(i - 1)
                retain_gate(turn)
            values_by_token(R_HEADS - 1)
            retained_root(R_HEADS - 1)
            retained_high(R_HEADS - 1)
            q0, k0 = STATS["ln"]
            for c in range(4):
                act.wait_ge(sem("centred"), c + 1)
                if c == 0:
                    act.wait_ge(sq_used, q0)
                square(q0 + c, c, cv[:, c, :])
            act.wait_ge(sem("ln_var"), 1)
            af(tiny[:, 4:8], tiny[:, 0:4], ACT.Sqrt).then_inc(sem("ln_sd"), 1)
            for c in range(4):
                act.wait_ge(sem("ln_scaled"), c + 1)
                if c >= 2:
                    act.wait_ge(sem("conv_silu"), c - 1)
                af(sq[:, c % 2, :], cv[:, c, :], ACT.Tanh).then_inc(sem("ln_tanh"), 1)
                if c:
                    act.wait_ge(sem("conv_silu"), c)
                    af(v_hi[:, c - 1, :], cv[:, c - 1, :], ACT.Copy).then_inc(sem("conv_hi"), 1)
            act.wait_ge(sem("conv_silu"), 4)
            af(v_hi[:, 3, :], cv[:, 3, :], ACT.Copy).then_inc(sem("conv_hi"), 1)

            outputs("mix2_out", "post2")
            x_squares("fpre2", 16)
            round_u(24)

            with act.Fori(0, H2 // 2) as i:
                turn = Turn("swiglu", i)
                for n in range(2):
                    ahead(turn, 2 * n)
                    ready(turn, 0, n)
                    act.wait_ge(out_free[1], turn.out(1, n) + 1)
                    af(sq[:, 0, :], ps[0][:], ACT.Tanh, scale=0.5)
                    af(sq[:, 1, :], ps[0][:], ACT.Copy, scale=0.5).then_inc(out_free[0], 1)
                    ahead(turn, 2 * n + 1)
                    freed(act, turn, 1, n)
                    af(h_hi[:, i * 2 + n, :], h_tmp[:], ACT.Copy).then_inc(sem("hidden2_hi"), 1)
            q, k = STATS["fpost2"]
            for i in range(2):
                turn = Turn("down2", i)
                for n in range(4):
                    for s in range(3):
                        ahead(turn, 3 * n + s)
                    ready(turn, n % 2, n // 2)
                    c = 4 * i + n
                    square(q + c, c, ps[n % 2][:])
                    af(y_u[:, c, :], ps[n % 2][:], ACT.Copy).then_inc(out_free[n % 2], 1)
            stat_root(k)
            turn = Turn("ple_proj")
            for n in range(C8):
                if n in (1, 5):
                    ahead(turn, n // 4)
                ready(turn, n % 2, n // 2)
                af(pj[:, n, :], ps[n % 2][:], ACT.Copy).then_inc(out_free[n % 2], 1)
            ahead(turn, 2)
            ahead(turn, 3)
            for c in range(C8):
                act.wait_ge(x_ready, 24 + c + 1)
                af(u_hi[:, c, :], xs[:, c, :], ACT.Copy).then_inc(u_hi_ready, 1)
            q, k = STATS["ple"]
            for i in range(2):
                turn = Turn("ple_gate", i)
                for j in range(4):
                    ahead(turn, j)
                    ready(turn, j % 2, j // 2)
                    c = 4 * i + j
                    if c >= 2:
                        act.wait_ge(sem("e_ready"), c - 1)
                    af(ple_tanh[:, c % 2, :], ps[j % 2][:], ACT.Tanh, scale=0.5).then_inc(out_free[j % 2], 1)
                    if c:
                        act.wait_ge(sem("e_ready"), c)
                        square(q + c - 1, c - 1, pj[:, c - 1, :])
            act.wait_ge(sem("e_ready"), 8)
            square(q + 7, 7, pj[:, 7, :])
            stat_root(k)

        @block.vector
        def _(dve):
            tt, ts, stt = nc.vector.tensor_tensor, nc.vector.tensor_scalar, nc.vector.scalar_tensor_tensor

            def ready(turn, bank, m):
                dve.wait_ge(out_ready[bank], turn.out(bank, m) + 1)

            def factors(width, eps, q, k, var_sem, sd_sem, diag_sem):
                dve.wait_ge(sq_used, q)
                ts(tiny[:, 0:4], ms[:, 0:4], 1.0 / width, eps, ALU.mult, ALU.add).then_inc(var_sem, 1)
                dve.wait_ge(sd_sem, k + 1)
                nc.vector.reciprocal(tiny[:, 40:44], tiny[:, 4:8])
                dve.drain()
                tt(tiny[:, 52:56], tiny[:, 40:44], tiny[:, 40:44], ALU.mult)
                dve.drain()
                tt(tiny[:, 52:56], tiny[:, 52:56], tiny[:, 0:4], ALU.mult)
                dve.drain()
                ts(tiny[:, 52:56], tiny[:, 52:56], -0.5, 1.5, ALU.mult, ALU.add)
                dve.drain()
                tt(tiny[:, 40:44], tiny[:, 40:44], tiny[:, 52:56], ALU.mult)
                dve.drain()
                for t in range(QB):
                    last = ts(diag[:, t * P:(t + 1) * P], ident, tiny[:, 40 + t:41 + t], None, ALU.mult)
                last.then_inc(diag_sem, 1)

            def stat(name, chunks=C8, i=0, width=D, eps=EPS):
                q, k = STATS[name]
                factors(width, eps, i * chunks + (q + chunks), i + k, var_ready, sd_ready, diag_ready)
                dve.wait_ge(rb_ready, i + k + 1)

            def pre_norm(name, n0):
                stat(name)

                def rest(c):
                    dve.wait_ge(u_hi_ready, n0 + c + 1)
                    tt(u_lo[:, c, :], sq[:, c % 2, :], u_hi[:, c, :].bitcast(F32), ALU.subtract)\
                        .then_inc(u_ready, 1)

                for c in range(C8):
                    if c >= 2:
                        dve.wait_ge(u_ready, n0 + c - 1)
                    stt(out=sq[:, c % 2, :], in0=xs[:, c, :], scalar=v(name, c), in1=rb[:], op0=ALU.mult,
                        op1=ALU.mult).then_inc(n_ready, 1)
                    if c:
                        rest(c - 1)
                rest(C8 - 1)

            def post_norm(name, y, eps=EPS, done=x_ready, after=None):
                if after:
                    dve.wait_ge(out_free[0], OUT0[after][0] + 1)
                    dve.wait_ge(out_free[1], OUT0[after][1] + 1)
                stat(name, eps=eps)
                first = ("post1", "fpost1", "post2", "fpost2", "ple").index(name) * C8

                def add(c):
                    dve.wait_ge(sem("y_scaled"), first + c + 1)
                    tt(xs[:, c, :], xs[:, c, :], y[:, c, :], ALU.add).then_inc(done, 1)

                for c in range(C8):
                    stt(out=y[:, c, :], in0=y[:, c, :], scalar=v(name, c), in1=rb[:], op0=ALU.mult, op1=ALU.mult)\
                        .then_inc(sem("y_scaled"), 1)
                    if c:
                        add(c - 1)
                add(C8 - 1)

            nc.vector.memset(tiny[:], 0.0).then_inc(out_free[0], 1)
            nc.vector.memset(half[:], 0.0).then_inc(out_free[1], 1)
            dve.wait_ge(sem("const_landed"), 32)
            dve.drain()
            ts(half[:, 0:16], v("gate_b", 0, 16), 0.5, None, ALU.mult)
            ts(half[:, 16:32], v("d_skip", 0, 16), 0.5, None, ALU.mult)
            dve.wait_ge(sem("x_landed"), 16)
            pre_norm("pre1", 0)
            dve.wait_ge(sem("dtw_hi"), 1)
            tt(dt_lo, dt_raw[:], dt_hi.bitcast(F32), ALU.subtract).then_inc(sem("dtw_ready"), 1)
            nc.vector.memset(att_acc[:], 0.0)
            nc.vector.memset(ssm_acc[:], 0.0)
            dve.wait_ge(sem("dist_landed"), 16)

            def by_chunk(row):
                return row.unsqueeze(1).broadcast_to([P, QB, S_HEADS])

            def heads(k):
                return hd[:, k, :].rearrange("p (c h) -> p c h", c=QB)

            def biases(columns):
                for h in range(2):
                    stt(out=bias[:, h, :], in0=dist[:, 0:T], scalar=columns[h], in1=dist[:, T:2 * T],
                        op0=ALU.mult, op1=ALU.add)
                dve.drain()

            def attention(i, between):
                def logit(b):
                    h, qb = divmod(b, QB)
                    n = (qb + 1) * P
                    if b >= 4:
                        dve.wait_ge(sem("turned"), i * 8 + (b - 3))
                    dve.wait_ge(sem("scores_ready"), i * 8 + b + 1)
                    nc.vector.memset(tiny[:, 44 + b:45 + b], 0.0)
                    nc.vector.tensor_tensor_reduce(
                        out=logits[:, b % 4, 0:n], in0=ps[3 + b % 3][:, 0:n], in1=bias[:, h, T - n:T],
                        scale=1.0, scalar=3e38, op0=ALU.add, op1=ALU.min,
                        accum_out=tiny[:, 8 + b:9 + b]).then_inc(sem("logits_done"), 1)

                def normal(b):
                    n = (b % QB + 1) * P
                    dve.wait_ge(sem("exp_done"), i * 8 + b + 1)
                    nc.vector.reciprocal(tiny[:, 44 + b:45 + b], tiny[:, 16 + b:17 + b])
                    dve.drain()
                    ts(logits[:, b % 4, 0:n], logits[:, b % 4, 0:n], tiny[:, 44 + b:45 + b], None, ALU.mult)\
                        .then_inc(sem("probs_ready"), 1)

                for b in range(8):
                    logit(b)
                    if b == 1:
                        dve.wait_ge(sem("v_turned"), i + 1)
                        nc.vector.tensor_copy(v_tok[:].rearrange("p k t -> p (k t)"), ps[6][:])\
                            .then_inc(sem("v_tok_ready"), 1)
                    if b >= 1:
                        normal(b - 1)
                    between(b)
                normal(7)
                dve.wait_ge(sem("att_hi"), i + 1)
                tt(s_lo[:, 0, :], ps[7][:], s_hi[:, 0, :].bitcast(F32), ALU.subtract).then_inc(sem("att_split"), 1)

            def add_output(acc, turn, n, m0, m1):
                bank = n % 2
                ready(turn, bank, (m0, m1)[bank] + n // 2)
                tt(acc[:, n, :], acc[:, n, :], ps[bank][:], ALU.add).then_inc(out_free[bank], 1)

            biases([slopes[:, h:h + 1] for h in range(2)])
            dve.wait_ge(sem("dt_logits"), 1)
            tt(heads(0), ps[7][:, 0:P].rearrange("p (c h) -> p c h", c=QB), by_chunk(v("dt_bias", 0, S_HEADS)),
               ALU.add).then_inc(sem("dt_read"), 1)
            attention(0, lambda b: None)
            ts(hd[:, 1, :], hd[:, 0, :], 0.0, None, ALU.min)
            ts(hd[:, 2, :], hd[:, 0, :], 0.0, None, ALU.max)
            dve.drain()
            tt(hd[:, 3, :], hd[:, 2, :], hd[:, 1, :], ALU.subtract).then_inc(sem("dt_abs"), 1)
            dve.wait_ge(sem("dt_exp"), 2)
            ts(hd[:, 1, :], hd[:, 4, :], 2.0, None, ALU.add)
            dve.drain()
            nc.vector.reciprocal(hd[:, 5, :], hd[:, 1, :])
            dve.drain()
            tt(hd[:, 1, :], hd[:, 4, :], hd[:, 5, :], ALU.mult)
            dve.drain()
            tt(hd[:, 5, :], hd[:, 1, :], hd[:, 1, :], ALU.mult)
            dve.drain()
            ts(hd[:, 0, :], hd[:, 5, :], 1.0 / 17, None, ALU.mult)
            for n in (15, 13, 11, 9, 7, 5, 3):
                dve.drain()
                stt(out=hd[:, 0, :], in0=hd[:, 0, :], scalar=1.0 / n, in1=hd[:, 5, :], op0=ALU.add, op1=ALU.mult)
            dve.drain()
            stt(out=hd[:, 0, :], in0=hd[:, 0, :], scalar=1.0, in1=hd[:, 1, :], op0=ALU.add, op1=ALU.mult)
            dve.drain()
            stt(out=hd[:, 3, :], in0=hd[:, 0, :], scalar=2.0, in1=hd[:, 2, :], op0=ALU.mult, op1=ALU.add)
            dve.drain()
            stt(out=heads(4), in0=heads(3), scalar=-1.0, in1=by_chunk(hd[:, 7, 0:S_HEADS]),
                op0=ALU.mult, op1=ALU.mult).then_inc(sem("la_ready"), 1)
            ts(heads_t[:, 0, :, :], heads(3), 0.125, None, ALU.mult)

            with dve.Fori(1, PAIRS) as i:
                turn = Turn("attend", i, 1)
                dve.drain()
                biases([slopes[:, bass.ds(i * 2 + h, 1)] for h in range(2)])
                attention(i, lambda b: add_output(att_acc, turn, b, 2, 1))
            nc.vector.memset(cat[:, :, 0:3], 0.0)
            dve.wait_ge(sem("acs_sum"), 2)
            nc.vector.tensor_copy(heads_t[:, 1, :, :], ps[4][:, 0:P].rearrange("p (c h) -> p c h", c=QB))\
                .then_inc(sem("acs_tok"), 1)
            dve.wait_ge(sem("acs_tok"), 1)
            tt(heads(5), ps[5][:, 0:P].rearrange("p (c h) -> p c h", c=QB), heads_t[:, 1, :, :], ALU.subtract)\
                .then_inc(sem("dt_to_end"), 1)
            turn = Turn("att_last")
            for n in range(C8):
                add_output(att_acc, turn, n, 0, 0)
            dve.wait_ge(sem("dt_exp"), 3)
            tt(heads_t[:, 2, :, :], heads(5), heads_t[:, 0, :, :], ALU.mult).then_inc(sem("heads_ready"), 1)
            dve.drain()

            q0, k0 = STATS["ssm"]
            cw = VEC["conv4"]

            def silu(g, j):
                dve.wait_ge(sem("tanh_done"), g * 4 + (j + 1))
                stt(out=post[:, j, :], in0=th[:, j % 2, :], scalar=1.0, in1=post[:, j, :],
                    op0=ALU.add, op1=ALU.mult).then_inc(sem("silu_done"), 1)

            def conv4(turn, g, j):
                freed(dve, turn, j % 2, j // 2)

                def weight(t):
                    col = g * (4 * (CONV4 + 1)) + (cw + j * (CONV4 + 1) + t)
                    return vec[:, col:col + 1] if isinstance(g, int) else vec[:, bass.ds(col, 1)]

                ts(post[:, j, :], cat[:, j, 0:T], weight(0), weight(CONV4), ALU.mult, ALU.add)
                for t in range(1, CONV4):
                    dve.drain()
                    last = stt(out=post[:, j, :], in0=cat[:, j, t:t + T], scalar=weight(t), in1=post[:, j, :],
                               op0=ALU.mult, op1=ALU.add)
                last.then_inc(sem("conv4_done"), 1)

            def z_silu(g, j):
                dve.wait_ge(sem("z_tanh"), g * 2 + (j + 1))
                stt(out=zz[:, j, :], in0=zz[:, j, :], scalar=1.0, in1=ps[j][:], op0=ALU.add, op1=ALU.mult)\
                    .then_inc(out_free[j], 1)

            def group_inputs(i):
                def per_head(n, j):
                    at = i * HPG + 2 * j
                    cols = slice(at, at + 2) if isinstance(i, int) else bass.ds(at, 2)
                    return heads_t[:, n, :, cols].unsqueeze(3).broadcast_to([P, QB, 2, HEAD])

                dve.wait_ge(sem("bc_landed"), i * 16 + 16)
                for h in range(HPG):
                    for c in range(QB):
                        w = slice(c * P, (c + 1) * P)
                        at = i * HPG + h
                        own = heads_t[:, 1, c, at:at + 1] if isinstance(i, int) else heads_t[:, 1, c, bass.ds(at, 1)]
                        last = ts(decay[:, h, w], bc[:, h, w], own, 0.0, ALU.subtract, ALU.min)
                    last.then_inc(sem("differences"), 1)
                for j in range(2):
                    dve.wait_ge(sem("x_turned"), i * 2 + (j + 1))
                    src = ps[2 + j][:].rearrange("p (c h f) -> p c h f", c=QB, h=2)
                    cols = slice(j * P, (j + 1) * P)
                    tt(xw[:, :, cols].rearrange("p c (h f) -> p c h f", h=2), src, per_head(2, j), ALU.mult)
                    tt(xd[:, :, cols].rearrange("p c (h f) -> p c h f", h=2), src, per_head(0, j), ALU.mult)\
                        .then_inc(sem("xw_ready"), 1)
                dve.wait_ge(sem("bc_product"), i + 1)
                tt(gm[:], ps[5][:].rearrange("p (c t) -> p c t", c=QB), tri.unsqueeze(1).broadcast_to([P, QB, P]),
                   ALU.mult)
                dve.drain()
                for h in range(HPG):
                    dve.wait_ge(sem("decay_exp"), i * 4 + (h + 1))
                    tt(decay[:, h, :], decay[:, h, :], gm[:].rearrange("p c t -> p (c t)"), ALU.mult)\
                        .then_inc(sem("kernel_ready"), 1)
                    dve.wait_ge(sem("bc_exp"), i * 4 + (h + 1))
                    tt(bc[:, h, :], bc[:, h, :], post[:, 3, :], ALU.mult).then_inc(sem("c_decayed"), 1)
                for c in range(1, 3):
                    dve.drain()
                    if c == 1:
                        dve.wait_ge(sem("state0"), i + 1)
                    for h in range(HPG):
                        cols = slice(h * HEAD, (h + 1) * HEAD)
                        at = c % 2 * 256 + h * HEAD
                        last = stt(out=states[:, c, cols], in0=states[:, c - 1, cols],
                                   scalar=tiny[:, 24 + 4 * h + c:25 + 4 * h + c], in1=ps[2 + c // 2][:, at:at + HEAD],
                                   op0=ALU.mult, op1=ALU.add)
                last.then_inc(sem("states_ready"), 1)

            def y_gate(i, j):
                dve.wait_ge(sem("y_done"), i * 4 + (2 * j + 2))
                at = i * 2 + (16 + j)
                skip = half[:, at:at + 1] if isinstance(i, int) else half[:, bass.ds(at, 1)]
                stt(out=y_g[:, j, :], in0=post[:, j, :], scalar=skip, in1=ps[6 + j][:], op0=ALU.mult, op1=ALU.add)
                dve.drain()
                tt(y_g[:, j, :], y_g[:, j, :], zz[:, j, :], ALU.mult).then_inc(sem("y_gated"), 1)

            def y_norm(i):
                stat("ssm", 2, i, width=2 * P, eps=4 * EPS)
                for j in range(2):
                    at = i * 2 + (VEC["ssm_norm"] + j)
                    scale = vec[:, at:at + 1] if isinstance(i, int) else vec[:, bass.ds(at, 1)]
                    stt(out=y_g[:, j, :], in0=y_g[:, j, :], scalar=scale, in1=rb[:],
                        op0=ALU.mult, op1=ALU.mult).then_inc(sem("y_normed"), 1)

            def y_rest(i):
                for j in range(2):
                    dve.wait_ge(sem("ssm_hi"), i * 2 + (j + 1))
                    tt(s_lo[:, j, :], y_g[:, j, :], s_hi[:, j, :].bitcast(F32), ALU.subtract)\
                        .then_inc(sem("ssm_split"), 1)

            turn = Turn("ssm_first")
            for j in range(4):
                conv4(turn, 0, j)
                if j:
                    silu(0, j - 1)
            silu(0, 3)
            z_silu(0, 0)
            z_silu(0, 1)
            with dve.Fori(0, GROUPS - 1) as i:
                turn = Turn("ssm", i)
                group_inputs(i)
                y_gate(i, 0)
                dve.drain()
                conv4(turn, i + 1, 0)
                y_gate(i, 1)
                dve.drain()
                conv4(turn, i + 1, 1)
                silu(i + 1, 0)
                conv4(turn, i + 1, 2)
                silu(i + 1, 1)
                y_norm(i)
                conv4(turn, i + 1, 3)
                y_rest(i)
                z_silu(i + 1, 0)
                z_silu(i + 1, 1)
                silu(i + 1, 2)
                silu(i + 1, 3)
                for n in range(C8):
                    add_output(ssm_acc, turn, n, 3, 3)
                dve.drain()
            group_inputs(GROUPS - 1)
            y_gate(GROUPS - 1, 0)
            y_gate(GROUPS - 1, 1)
            y_norm(GROUPS - 1)
            y_rest(GROUPS - 1)
            turn = Turn("ssm_last")
            for n in range(C8):
                add_output(ssm_acc, turn, n, 0, 0)

            def mix(c):
                dve.drain()
                for n in range(2):
                    for j, acc in enumerate((att_acc, ssm_acc)):
                        stt(out=gate[:, 2 * n + j, :], in0=gate[:, 2 * n + j, :], scalar=1.0, in1=acc[:, c + n, :],
                            op0=ALU.add, op1=ALU.mult)
                dve.drain()
                for n in range(2):
                    tt(tmp[:, n, :], gate[:, 2 * n, :], gate[:, 2 * n + 1, :], ALU.add).then_inc(sem("mixed"), 1)
                for n in range(2):
                    dve.wait_ge(sem("mixed_hi"), c + (n + 1))
                    tt(v_lo[:, c + n, :], tmp[:, n, :], v_hi[:, c + n, :].bitcast(F32), ALU.subtract)\
                        .then_inc(sem("mixed_ready"), 1)

            freed(dve, Turn("gates_first"), 0, 1)
            freed(dve, Turn("gates_first"), 1, 1)
            with dve.Fori(0, 3) as i:
                turn = Turn("gates", i)
                mix(i * 2)
                freed(dve, turn, 0, 1)
                freed(dve, turn, 1, 1)
            mix(6)
            dve.drain()

            post_norm("post1", y_u, eps=4 * EPS, after="ffn")
            nc.vector.memset(ffn_acc[:], 0.0)
            pre_norm("fpre1", 8)

            with dve.Fori(0, 4) as i:
                turn = Turn("ffn", i)

                def rest_hidden(j):
                    dve.wait_ge(sem("hidden_hi"), i * 8 + j + 1)
                    tt(v_lo[:, j, :], tmp[:, j % 2, :], v_hi[:, j, :].bitcast(F32), ALU.subtract)\
                        .then_inc(sem("hidden_ready"), 1)

                for j in range(8):
                    dve.wait_ge(sem("relu_done"), i * 8 + j + 1)
                    stt(out=tmp[:, j % 2, :], in0=ps[j % 2][:], scalar=0.0, in1=tmp[:, j % 2, :],
                        op0=ALU.max, op1=ALU.mult).then_inc(out_free[j % 2], 1)
                    if j:
                        rest_hidden(j - 1)
                rest_hidden(7)
                dve.drain()
                for j in range(8):
                    ready(turn, j % 2, 4 + j // 2)
                    tt(ffn_acc[:, j, :], ffn_acc[:, j, :], ps[j % 2][:], ALU.add).then_inc(out_free[j % 2], 1)
            dve.wait_ge(sem("p_hi"), 1)
            tt(s_lo[:], p_raw[:], s_hi[:].bitcast(F32), ALU.subtract).then_inc(sem("p_split"), 1)
            dve.drain()
            post_norm("fpost1", ffn_acc)
            pre_norm("pre2", 16)

            nc.vector.memset(cat31[:, :, 0:CONV31 - 1], 0.0)

            def glu_product(n):
                turn = Turn("glu")
                freed(dve, turn, 0, n)
                freed(dve, turn, 1, n)
                stt(out=cat31[:, n, CONV31 - 1:], in0=glu[:, 2 * n + 1, :], scalar=1.0, in1=glu[:, 2 * n, :],
                    op0=ALU.add, op1=ALU.mult)

            def conv_tap(i, t):
                at = i * (CONV31 + 1) + (VEC["conv31"] + t)
                if isinstance(i, int):
                    w, b = vec[:, at:at + 1], vec[:, at + CONV31:at + CONV31 + 1]
                else:
                    w, b = vec[:, bass.ds(at, 1)], vec[:, bass.ds(at + CONV31, 1)]
                acc = cv_odd[:] if t % 2 else cv[:, i, :]
                if t == 0:
                    op = ts(acc, cat31[:, i, 0:T], w, b, ALU.mult, ALU.add)
                elif t == 1:
                    if not isinstance(i, int) or i > 0:
                        dve.wait_ge(sem("conv_done"), i)
                    op = ts(acc, cat31[:, i, 1:T + 1], w, None, ALU.mult)
                else:
                    dve.wait_ge(sem("tap_done"), i * CONV31 + (t - 1))
                    op = stt(out=acc, in0=cat31[:, i, t:t + T], scalar=w, in1=acc, op0=ALU.mult, op1=ALU.add)
                op.then_inc(sem("tap_done"), 1)

            def conv_sum(i):
                dve.wait_ge(sem("tap_done"), i * CONV31 + CONV31)
                tt(cv[:, i, :], cv[:, i, :], cv_odd[:], ALU.add).then_inc(sem("conv_done"), 1)

            glu_product(0)
            dve.drain()
            for t in range(CONV31):
                conv_tap(0, t)
            conv_sum(0)
            for n in range(1, 4):
                glu_product(n)
            dve.wait_ge(sem("rt_landed"), 16)
            dve.drain()

            def rotate(i):
                for j, (src, dst) in enumerate(((r_q, rot_q), (r_k, rot_k))):
                    dve.wait_ge(sem("swapped"), i * 2 + (j + 1))
                    tt(dst[:], src[:], rt[:, 0, :], ALU.mult)
                    tt(rot_s[:, j, :], ps[4 + j][:], rt[:, 1, :], ALU.mult)
                    dve.drain()
                    tt(dst[:], dst[:], rot_s[:, j, :], ALU.add).then_inc(sem("rotated"), 1)

            def decayed(i):
                for kb in range(QB):
                    n = T - kb * P
                    dve.wait_ge(sem("r_scores"), i * 4 + (kb + 1))
                    tt(r_s[:, S_OFF[kb]:S_OFF[kb] + n], ps[4 + kb % 2][:, 0:n], rt[:, i + 2, 0:n], ALU.mult)\
                        .then_inc(sem("decayed"), 1)

            def ret_factors(turn):
                freed(dve, turn, 1, 1)
                stt(out=r_g[:, 0, :], in0=r_g[:, 1, :], scalar=1.0, in1=r_g[:, 0, :], op0=ALU.add, op1=ALU.mult)
                dve.drain()
                q, k = STATS["retain"]
                factors(P, EPS, turn.i + (q + 1), turn.i + k, var_ready, sd_ready, diag_ready)

            def ret_norm(i):
                dve.drain()
                dve.wait_ge(rb_ready, i + (STATS["retain"][1] + 1))
                tt(r_g[:, 0, :], r_g[:, 0, :], rb[:], ALU.mult)
                dve.drain()
                tt(r_o[:], r_g[:, 0, :], ps[7][:], ALU.mult).then_inc(sem("ret_normed"), 1)
                dve.wait_ge(sem("ret_hi"), i + 1)
                tt(v_lo[:, i + 4, :], r_o[:], v_hi[:, i + 4, :].bitcast(F32), ALU.subtract)\
                    .then_inc(sem("ret_split"), 1)
                dve.drain()

            with dve.Fori(1, R_HEADS) as i:
                rotate(i - 1)
                for t in range(3):
                    conv_tap(i, t)
                decayed(i - 1)
                for t in range(3, 22):
                    conv_tap(i, t)
                ret_factors(Turn("retain", i - 1))
                for t in range(22, CONV31):
                    conv_tap(i, t)
                conv_sum(i)
                ret_norm(i - 1)
            rotate(R_HEADS - 1)
            decayed(R_HEADS - 1)
            ret_factors(Turn("retain", R_HEADS - 1))
            ret_norm(R_HEADS - 1)

            dve.wait_ge(sem("mean_sum"), 1)
            ts(tiny[:, 40:44], ms[:, 0:4], 1.0 / D_CONV, None, ALU.mult)
            dve.drain()
            for t in range(QB):
                last = ts(diag[:, t * P:(t + 1) * P], ident, tiny[:, 40 + t:41 + t], None, ALU.mult)
            last.then_inc(sem("mean_diag"), 1)
            dve.wait_ge(sem("mean_ready"), 1)
            for c in range(4):
                tt(cv[:, c, :], cv[:, c, :], rb[:], ALU.subtract).then_inc(sem("centred"), 1)
            factors(D_CONV, EPS, STATS["ln"][0] + 4, 0, sem("ln_var"), sem("ln_sd"), sem("ln_diag"))
            dve.wait_ge(sem("ln_ready"), 1)

            def conv_rest(c):
                dve.wait_ge(sem("conv_hi"), c + 1)
                tt(v_lo[:, c, :], cv[:, c, :], v_hi[:, c, :].bitcast(F32), ALU.subtract).then_inc(sem("y2_ready"), 1)

            for c in range(4):
                stt(out=cv[:, c, :], in0=cv[:, c, :], scalar=v("ln_w", c), in1=rb[:], op0=ALU.mult, op1=ALU.mult)
                dve.drain()
                ts(cv[:, c, :], cv[:, c, :], v("ln_b", c), 0.5, ALU.add, ALU.mult).then_inc(sem("ln_scaled"), 1)
            for c in range(4):
                dve.wait_ge(sem("ln_tanh"), c + 1)
                stt(out=cv[:, c, :], in0=sq[:, c % 2, :], scalar=1.0, in1=cv[:, c, :], op0=ALU.add, op1=ALU.mult)\
                    .then_inc(sem("conv_silu"), 1)
                if c:
                    conv_rest(c - 1)
            conv_rest(3)
            nc.vector.memset(tiny[:, 60:61], 0.0).then_inc(sem("y2_ready"), 4)

            post_norm("post2", y_u, after="swiglu")
            pre_norm("fpre2", 24)

            with dve.Fori(0, H2 // 2) as i:
                turn = Turn("swiglu", i)
                for n in range(2):
                    freed(dve, turn, 0, n)
                    stt(out=sq[:, 1, :], in0=sq[:, 0, :], scalar=1.0, in1=sq[:, 1, :], op0=ALU.add, op1=ALU.mult)
                    dve.drain()
                    ready(turn, 1, n)
                    tt(h_tmp[:], sq[:, 1, :], ps[1][:], ALU.mult).then_inc(out_free[1], 1)
                    dve.wait_ge(sem("hidden2_hi"), i * 2 + n + 1)
                    tt(h_lo[:, i * 2 + n, :], h_tmp[:], h_hi[:, i * 2 + n, :].bitcast(F32), ALU.subtract)\
                        .then_inc(sem("hidden2_ready"), 1)
                    dve.drain()
            post_norm("fpost2", y_u, after="ple_proj")
            for c in range(C8):
                dve.wait_ge(u_hi_ready, 32 + c + 1)
                tt(u_lo[:, c, :], xs[:, c, :], u_hi[:, c, :].bitcast(F32), ALU.subtract).then_inc(u_ready, 1)
            for c in range(C8):
                freed(dve, Turn("ple_gate", c // 4), c % 2, c % 4 // 2)
                stt(out=pj[:, c, :], in0=ple_tanh[:, c % 2, :], scalar=1.0, in1=pj[:, c, :], op0=ALU.add, op1=ALU.mult)\
                    .then_inc(sem("e_ready"), 1)
            post_norm("ple", pj, eps=4 * EPS, done=sem("result_ready"))


def weight_stream(w):
    w_in, w_att, w_ssm, w_out = w["w_in"][0], w["w_att_proj"][0], w["w_ssm_proj"][0], w["w_out"][0]
    up, down = w["w_up"][0], w["w_down"][0]
    w_in2, w_out2 = w["w_in_2"][0], w["w_out_2"][0]
    gate2, up2, down2 = w["w_ffn_gate_2"][0], w["w_ffn_up_2"][0], w["w_ffn_down_2"][0]
    q0, k0, v0 = 0, ATT_W, 2 * ATT_W
    z0 = 3 * ATT_W
    x0 = z0 + S_INNER
    b0 = x0 + S_INNER
    c0 = b0 + GROUPS * S_STATE
    dt0 = c0 + GROUPS * S_STATE
    g0 = dt0 + S_HEADS
    stream = np.zeros((SLOTS, P, TILES * P), np.float32)
    n = [0]

    def slot(tiles):
        for t, tile in enumerate(tiles):
            stream[n[0], :, t * P:(t + 1) * P] = tile
        n[0] += 1

    def columns(m, c, k0=0, k1=TILES):
        slot([m[k * P:(k + 1) * P, c:c + P] for k in range(k0, k1)])

    def att_in(i):
        for at in (k0, q0, v0):
            columns(w_in, at + i * P)

    def att_out(i):
        slot([w_att[i * P:(i + 1) * P, c * P:(c + 1) * P] for c in range(C8)])

    def group_in(g):
        for at in (x0 + g * 256, x0 + g * 256 + P, b0 + g * P, c0 + g * P, z0 + g * 256, z0 + g * 256 + P):
            columns(w_in, at)

    def group_out(g):
        for m in range(2):
            slot([w_ssm[(2 * g + k) * P:(2 * g + k + 1) * P, c * P:(c + 1) * P]
                  for c in range(4 * m, 4 * m + 4) for k in range(2)])

    def gates(c):
        columns(w_in, g0 + c * P)
        columns(w_in, g0 + D + c * P)

    att_in(0)
    for i in range(1, PAIRS):
        att_in(i)
        att_out(i - 1)
    att_out(PAIRS - 1)
    group_in(0)
    for g in range(GROUPS - 1):
        group_in(g + 1)
        group_out(g)
    gates(0)
    gates(1)
    group_out(GROUPS - 1)
    for c in range(2, C8):
        gates(c)
    for c in range(C8):
        columns(w_out, c * P)
    for i in range(4):
        for c in range(8):
            columns(up, (8 * i + c) * P)
        for c in range(C8):
            columns(down, c * P, 8 * i, 8 * i + 8)
    for c in range(4):
        columns(w_in2, c * P)
        columns(w_in2, D_CONV + c * P)
    for h in range(R_HEADS):
        for part in range(4):
            columns(w_in2, 2 * D_CONV + part * 512 + h * P)
    for c in range(C8):
        columns(w_out2, c * P)
    for c in range(H2):
        columns(gate2, c * P)
        columns(up2, c * P)
    for c in range(C8):
        for s in range(3):
            columns(down2, c * P, 8 * s, min(H2, 8 * s + 8))
    proj = w["w_ple_proj_2"][0]
    for m in range(2):
        slot([proj[k * P:(k + 1) * P, c * P:(c + 1) * P] for c in range(4 * m, 4 * m + 4) for k in range(2)])
    n[0] += 2
    for c in range(C8):
        columns(w["w_ple_gate_2"][0], c * P)
    assert n[0] == SLOTS
    w_dt = w_in[:, dt0:dt0 + S_HEADS].reshape(TILES, P, S_HEADS).transpose(1, 0, 2)
    return stream, np.ascontiguousarray(w_dt.reshape(P, TILES * S_HEADS))



def feature_vectors(w):
    vec = np.zeros((P, NVEC), np.float32)

    def put(name, a, at=0):
        a = a.reshape(-1, P).T
        vec[:, VEC[name] + at:VEC[name] + at + a.shape[1]] = a

    for name, key in (("pre1", "norm_mix_pre_w"), ("post1", "norm_mix_post_w"), ("fpre1", "norm_ffn_pre_w"),
                      ("fpost1", "norm_ffn_post_w"), ("gate_b", "b_gate"), ("ssm_norm", "ssm_norm_w"),
                      ("pre2", "mix_pre_norm_2"), ("post2", "mix_post_norm_2"), ("fpre2", "ffn_pre_norm_2"),
                      ("fpost2", "ffn_post_norm_2"), ("ple", "ple_post_norm_2"),
                      ("ln_w", "conv_ln_w_2"), ("ln_b", "conv_ln_b_2")):
        put(name, w[key][0])
    put("d_skip", np.repeat(w["d_skip"][0], HEAD))
    taps = np.concatenate([w["conv_w"][0], w["conv_b"]])
    for g in range(GROUPS):
        for j, c in enumerate((2 * g, 2 * g + 1, 16 + g, 24 + g)):
            vec[:, VEC["conv4"] + (4 * g + j) * 5:VEC["conv4"] + (4 * g + j + 1) * 5] = taps[:, c * P:(c + 1) * P].T
    taps = np.concatenate([w["conv_dw_w_2"][0], w["conv_dw_b_2"]])
    for c in range(4):
        vec[:, VEC["conv31"] + c * 32:VEC["conv31"] + (c + 1) * 32] = taps[:, c * P:(c + 1) * P].T
    for name in ("dt_bias", "a_log"):
        vec[:, VEC[name]:VEC[name] + S_HEADS] = w[name]
    return vec


def shape_constants():
    i = np.arange(P)
    cst = np.zeros((P, 4 * P + N_HEADS), np.float32)
    cst[:, 0:P] = np.eye(P)
    cst[:, P:2 * P] = 1.0
    cst[:, 2 * P:3 * P] = i[:, None] <= i[None, :]
    cst[i, 3 * P + (i + 64) % P] = 1.0
    small = 2 ** int(np.floor(np.log2(N_HEADS)))

    def powers(m):
        return [2.0 ** (-8.0 / m * (k + 1)) for k in range(m)]

    cst[:, 4 * P:] = np.array(powers(small) + powers(2 * small)[0::2][:N_HEADS - small], np.float32)
    d = i[:, None] - np.arange(T)[None, :] + (T - P)
    times = (d <= 128).astype(int) + (d % 4 == 0) + (d % 16 == 0)
    seen = (d >= 0) & (times > 0)
    tables = np.zeros((P, 2 * T), np.float32)
    tables[:, 0:T] = np.where(seen, d, 0)
    tables[:, T:] = np.where(seen, -np.log(np.maximum(times, 1)), MASKED)
    f = np.float32(10000.0) ** (-np.arange(64, dtype=np.float32) / np.float32(64))
    ang = np.arange(T, dtype=np.float32)[None, :] * np.concatenate([f, f])[:, None].astype(np.float32)
    ret = np.zeros((P, 6, T), np.float32)
    ret[:, 0] = np.cos(ang)
    ret[:, 1] = np.sin(ang) * np.where(i < 64, -1.0, 1.0)[:, None]
    rel = np.arange(T)[None, :] - i[:, None]
    for h in range(R_HEADS):
        log_g = np.log(np.float32(1.0 - 2.0 ** (-5.0 - h)))
        ret[:, 2 + h] = np.where(rel >= 0, np.exp(np.float64(log_g) * np.maximum(rel, 0)), 0.0) * 128.0 ** -0.5
    return cst, tables, ret


def kernel(**inputs):
    from concourse import bacc
    from concourse.bass_utils import run_bass_kernel_spmd

    w = {k: np.asarray(a) for k, a in inputs.items()}
    stream, w_dt = weight_stream(w)
    cst, att_tables, ret_tables = shape_constants()

    def by_feature(a):
        return np.ascontiguousarray(a.T.reshape(-1, P, a.shape[0]).transpose(1, 0, 2))

    arrays = {
        "weights": stream, "w_dt": w_dt, "x": by_feature(w["x"][0]), "p": by_feature(w["p_2"][0, 0]),
        "vectors": feature_vectors(w), "constants": cst, "att_tables": att_tables, "ret_tables": ret_tables,
    }
    nc = bacc.Bacc("TRN2", target_bir_lowering=False, num_devices=1)
    aps = [nc.dram_tensor(k, a.shape, F32, kind="ExternalInput").ap() for k, a in arrays.items()]
    acs = nc.dram_tensor("acs", (S_HEADS, T), F32, kind="Internal").ap()
    out = nc.dram_tensor("out", (P, C8, T), F32, kind="ExternalOutput").ap()
    block_program(nc, *aps, acs, out)
    r = run_bass_kernel_spmd(nc, [arrays], core_ids=[0])
    y = np.asarray(r.results[0]["out"])
    return np.ascontiguousarray(y.transpose(1, 0, 2).reshape(D, T).T)[None]
```

```python
import numpy as np

import concourse.bass as bass
from concourse import mybir

F32 = mybir.dt.float32
F32R = mybir.dt.float32r
ALU = mybir.AluOpType
ACT = mybir.ActivationFunctionType

P = 128
T = 512
D = 1024
C8 = D // P
QB = T // P
EPS = 1e-6
RING = 4
TILES = 8

N_HEADS, HEAD = 12, 64
ATT_W = N_HEADS * HEAD
PAIRS = N_HEADS // 2
S_HEADS, GROUPS, S_INNER, S_STATE = 32, 8, 2048, 128
HPG = S_HEADS // GROUPS
CONV4 = 4
FFN1 = 4096
D_CONV, CONV31, R_HEADS = 512, 31, 4
FFN2 = 2816
H2 = FFN2 // P
D_PLE = 256
MASKED = 1e30

def by_output(n):
    return [(j % 2, j // 2) for j in range(n)]


PHASES = {
    "att_first": (1, 3, 2, 1, [(0, 0), (1, 0), (0, 1)]),
    "attend": (PAIRS - 1, 4, 6, 5, [(0, 0), (1, 0), (0, 1), (1, 4)]),
    "att_last": (1, 1, 4, 4, [(1, 3)]),
    "ssm_first": (1, 6, 3, 3, by_output(6)),
    "ssm": (GROUPS - 1, 8, 7, 7, [*by_output(6), (1, 4), (1, 6)]),
    "gates_first": (1, 4, 2, 2, by_output(4)),
    "ssm_last": (1, 2, 4, 4, [(1, 1), (1, 3)]),
    "gates": (3, 4, 2, 2, by_output(4)),
    "mix_out": (2, 4, 2, 2, by_output(4)),
    "ffn": (4, 16, 8, 8, by_output(16)),
    "glu": (1, 8, 4, 4, by_output(8)),
    "retain": (R_HEADS, 4, 2, 2, by_output(4)),
    "mix2_out": (2, 4, 2, 2, by_output(4)),
    "swiglu": (H2 // 2, 4, 2, 2, by_output(4)),
    "down2": (2, 12, 2, 2, [None, None, (0, 0), None, None, (1, 0),
                            None, None, (0, 1), None, None, (1, 1)]),
    "ple_proj": (1, 4, 4, 4, [(1, 1), (1, 3), (1, 3), (1, 3)]),
    "ple_gate": (2, 4, 2, 2, by_output(4)),
}
UNIT0, OUT0 = {}, {}
_u, _a, _b = 0, 0, 0
for _name, (_t, _n, _p, _q, _) in PHASES.items():
    UNIT0[_name], OUT0[_name] = _u, (_a, _b)
    _u, _a, _b = _u + _t * _n, _a + _t * _p, _b + _t * _q
SLOTS = _u

VEC = {}
_at = 0
for _name, _n in (("pre1", 8), ("post1", 8), ("fpre1", 8), ("fpost1", 8), ("gate_b", 16), ("ssm_norm", 16),
                  ("d_skip", 16), ("conv4", GROUPS * 4 * (CONV4 + 1)),
                  ("pre2", 8), ("post2", 8), ("fpre2", 8), ("fpost2", 8), ("ple", 8),
                  ("conv31", 4 * (CONV31 + 1)), ("ln_w", 4), ("ln_b", 4),
                  ("dt_bias", S_HEADS), ("a_log", S_HEADS)):
    VEC[_name] = _at
    _at += _n
NVEC = _at

STATS = {}
_q, _k = 0, 0
for _name, _n, _chunks in (("pre1", 1, 8), ("ssm", GROUPS, 2), ("post1", 1, 8), ("fpre1", 0, 8), ("fpost1", 1, 8),
                           ("pre2", 1, 8), ("retain", R_HEADS - 1, 1), ("ln", 0, 4), ("retain_last", 1, 1),
                           ("post2", 1, 8), ("fpre2", 1, 8), ("fpost2", 1, 8), ("ple", 1, 8)):
    STATS[_name] = (_q, _k)
    _q, _k = _q + max(1, _n) * _chunks, _k + _n
SUMMED = {"pre1": 0, "ssm": 1, "post1": 1 + GROUPS, "fpost1": 2 + GROUPS, "post2": 3 + GROUPS,
          "fpost2": 4 + GROUPS, "ple": 5 + GROUPS}


class Turn:

    def __init__(self, name, i=0, first=0):
        _, self.slots, *self.outs, self.ends = PHASES[name]
        self.unit0 = UNIT0[name] - first * self.slots
        self.out0 = [a - first * n for a, n in zip(OUT0[name], self.outs)]
        self.i = i

    def unit(self, j):
        return self.i * self.slots + (self.unit0 + j)

    def slot(self, j):
        return (self.unit0 + j) % RING

    def out(self, bank, m):
        return self.i * self.outs[bank] + (self.out0[bank] + m)


def block_program(nc, weights, w_dt, x, p, vectors, constants, att_tables, ret_tables, acs_dram, out):
    base = (nc.sbuf_base + 63) // 64 * 64
    top = [base]

    def place(name, shape, dt=F32, at=None):
        size = 4 * int(np.prod(shape[1:]))
        offset = top[0] if at is None else at
        if at is None:
            top[0] += (size + 31) // 32 * 32
        return nc.alloc_sbuf_tensor_at(name, shape, dt, offset=offset)

    raw = place("raw", [P, RING, TILES * P])
    w_hi = place("w_hi", [P, RING, TILES * P], F32R)
    w_lo = place("w_lo", [P, RING, TILES * P], F32R)
    u_at = top[0]
    u_hi = place("u_hi", [P, C8, T], F32R)
    u_lo = place("u_lo", [P, C8, T], F32R)
    xs = place("xs", [P, C8, T])
    s_hi = place("s_hi", [P, 2, T], F32R)
    s_lo = place("s_lo", [P, 2, T], F32R)
    vec = place("vec", [P, NVEC])
    half = place("half", [P, 32])
    cst = place("cst", [P, 4 * P + N_HEADS])
    heads_t = place("heads_t", [P, 3, QB, S_HEADS])
    tiny = place("tiny", [P, 64])
    diag = place("diag", [P, T])
    sq = place("sq", [P, 2, T])
    ident, ones, tri, perm = (cst[:, k * P:(k + 1) * P] for k in range(4))
    slopes = cst[:, 4 * P:4 * P + N_HEADS]
    y_u = place("y_u", [P, C8, T], at=u_at)
    work = top[0]
    K = 1024

    att_acc = place("att_acc", [P, C8, T], at=work)
    ssm_acc = place("ssm_acc", [P, C8, T], at=work + 16 * K)
    a_at = work + 32 * K
    k_t = place("k_t", [P, T], at=a_at)
    q_t = place("q_t", [P, T], at=a_at + 2 * K)
    v_t = place("v_t", [P, T], at=a_at + 4 * K)
    v_tok = place("v_tok", [P, QB, P], at=a_at + 6 * K)
    dist = place("dist", [P, 2 * T], at=a_at + 8 * K)
    bias = place("bias", [P, 2, T], at=a_at + 12 * K)
    logits = place("logits", [P, 4, T], at=a_at + 16 * K)
    p_t = place("p_t", [P, 2, QB, P], at=a_at + 24 * K)
    dt_at = a_at + 28 * K
    dt_raw = place("dt_raw", [P, TILES * S_HEADS], at=dt_at)
    dt_hi, dt_lo = (a[:].rearrange("p a t -> p (a t)")[:, 0:TILES * S_HEADS] for a in (s_hi, s_lo))
    hd = place("hd", [P, 8, P], at=dt_at + K)
    acs_h = place("acs_h", [S_HEADS, T], at=dt_at + 5 * K)
    cat = place("cat", [P, 4, T + 3], at=a_at)
    g_at = a_at + 8256
    post = place("post", [P, 4, T], at=g_at)
    zz = place("zz", [P, 2, T], at=g_at + 8 * K)
    xd = place("xd", [P, QB, 2 * P], at=g_at + 12 * K)
    xw = place("xw", [P, QB, 2 * P], at=g_at + 16 * K)
    b_tok = place("b_tok", [P, QB, P], at=g_at + 20 * K)
    bc = place("bc", [P, HPG, T], at=g_at + 22 * K)
    gm = place("gm", [P, QB, P], at=g_at + 30 * K)
    states = place("states", [P, 3, 2 * P], at=g_at + 32 * K)
    y_g = place("y_g", [P, 2, T], at=g_at + 35 * K)
    decay = place("decay", [P, HPG, T], at=g_at + 39 * K)
    th = place("th", [P, 2, T], at=g_at + 47 * K)
    gate = place("gate", [P, 4, T], at=a_at)
    v_at = work + 40 * K
    v_hi = place("v_hi", [P, C8, T], F32R, at=v_at)
    v_lo = place("v_lo", [P, C8, T], F32R, at=v_at + 16 * K)
    t_at = work + 72 * K
    tmp = place("tmp", [P, 2, T], at=t_at)
    p_raw = place("p_raw", [P, 2, T], at=t_at + 12 * K)
    ffn_acc = place("ffn_acc", [P, C8, T], at=work)
    glu = place("glu", [P, 8, T], at=v_at)
    cat31 = place("cat31", [P, 4, T + CONV31 - 1], at=work)
    cv = place("cv", [P, 4, T], at=work + 8704)
    rt = place("rt", [P, 6, T], at=work + 17 * K)
    r_at = work + 29 * K
    r_q = place("r_q", [P, T], at=r_at)
    r_k = place("r_k", [P, T], at=r_at + 2 * K)
    r_v = place("r_v", [P, T], at=r_at + 4 * K)
    r_g = place("r_g", [P, 2, T], at=r_at + 6 * K)
    rot_q = place("rot_q", [P, T], at=t_at)
    rot_k = place("rot_k", [P, T], at=t_at + 2 * K)
    rot_s = place("rot_s", [P, 2, T], at=t_at + 4 * K)
    r_vtok = place("r_vtok", [P, QB, P], at=t_at + 8 * K)
    r_s = place("r_s", [P, QB * (QB + 1) // 2 * P], at=t_at + 10 * K)
    r_o = place("r_o", [P, T], at=t_at + 15 * K)
    cv_odd = place("cv_odd", [P, T], at=t_at + 17 * K)
    x_scale = place("x_scale", [P, T], at=v_at + 22 * K)
    S_OFF = [0, 512, 896, 1152]
    h_hi = place("h_hi", [P, H2, T], F32R, at=work)
    h_lo = place("h_lo", [P, H2, T], F32R, at=work + 44 * K)
    h_tmp = place("h_tmp", [P, T], at=work + 88 * K)
    h_scale = place("h_scale", [P, T], at=work + 90 * K)
    pj = place("pj", [P, C8, T], at=work)
    ple_tanh = place("ple_tanh", [P, 2, T], at=t_at)

    ps = [nc.alloc_psum_tensor(f"bank{i}", [P, T], F32) for i in range(8)]
    ms, rb = ps[2], ps[3]

    sems = {}

    def sem(name):
        if name not in sems:
            sems[name] = nc.alloc_semaphore(name)
        return sems[name]

    landed = [sem(f"slot_landed{s}") for s in range(RING)]
    x_landed = [sem(f"x_landed{c}") for c in range(C8 // 2)]
    hi_done, lo_done, slot_inside = sem("hi_done"), sem("lo_done"), sem("slot_ended_inside_output")
    out_ready = [sem("out_ready0"), sem("out_ready1")]
    out_free = [sem("out_free0"), sem("out_free1")]
    sq_ready, sq_used = sem("sq_ready"), sem("sq_used")
    var_ready, sd_ready = sem("var_ready"), sem("sd_ready")
    diag_ready, rb_ready = sem("diag_ready"), sem("rb_ready")
    n_ready, u_hi_ready, u_ready = sem("n_ready"), sem("u_hi_ready"), sem("u_ready")
    x_ready = sem("x_ready")

    def v(name, k=0, n=1):
        return vec[:, VEC[name] + k:VEC[name] + k + n]

    def freed(engine, turn, bank, m):
        engine.wait_ge(out_free[bank], turn.out(bank, m) + 2)

    def ended(engine, turn, j):
        if j < 0:
            engine.wait_ge(out_ready[0], turn.out(0, 0))
            engine.wait_ge(out_ready[1], turn.out(1, 0))
        elif turn.ends[j]:
            bank, m = turn.ends[j]
            engine.wait_ge(out_ready[bank], turn.out(bank, m) + 1)
        else:
            engine.wait_ge(slot_inside, turn.i * 8 + (j - j // 3 + 1))

    block = nc.Block()
    with block:

        @block.sync
        def _(sp):
            for c in range(0, C8, 2):
                sp.dma_start(xs[:, c:c + 2, :], x[:, c:c + 2, :]).then_inc(x_landed[c // 2], 16)
            sp.dma_start(vec[:], vectors).then_inc(sem("const_landed"), 16)
            sp.dma_start(cst[:], constants).then_inc(sem("const_landed"), 16)
            stream = weights.rearrange("(g r) p n -> g r p n", r=RING)
            for s in range(RING):
                sp.dma_start(raw[:, s, :], stream[0, s]).then_inc(landed[s], 16)
            sp.dma_start(dt_raw[:], w_dt).then_inc(sem("dtw_landed"), 16)
            sp.dma_start(dist[:], att_tables).then_inc(sem("dist_landed"), 16)
            with sp.Fori(1, SLOTS // RING) as g:
                for s in range(RING):
                    sp.wait_ge(lo_done, g * RING + (s + 1 - RING))
                    sp.dma_start(raw[:, s, :], stream[g, s]).then_inc(landed[s], 16)
            for c in range(C8):
                sp.wait_ge(sem("odd_result_ready" if c % 2 else "result_ready"), c // 2 + 1)
                sp.dma_start(out[:, c, :], xs[:, c, :]).then_inc(sem("stored"), 16)
            sp.wait_ge(sem("stored"), 16 * C8)

        @block.gpsimd
        def _(pool):
            with pool.Fori(0, SLOTS // RING) as g:
                for s in range(RING):
                    pool.wait_ge(hi_done, g * RING + (s + 1))
                    nc.gpsimd.tensor_tensor(w_lo[:, s, :], raw[:, s, :], w_hi[:, s, :].bitcast(F32),
                                            ALU.subtract).then_inc(lo_done, 1)
            for c in range(1, C8, 2):
                pool.wait_ge(sem("y_scaled"), 4 * C8 + c + 1)
                nc.gpsimd.tensor_tensor(xs[:, c, :], xs[:, c, :], pj[:, c, :], ALU.add)\
                    .then_inc(sem("odd_result_ready"), 1)

        @block.tensor
        def _(pe):
            mm = nc.tensor.matmul

            def exact(dst, slot, tile, hi, lo, first, last):
                w = slice(tile * P, tile * P + P)
                mm(dst, w_hi[:, slot, w], hi, start=first, stop=False)
                mm(dst, w_hi[:, slot, w], lo, start=False, stop=False)
                return mm(dst, w_lo[:, slot, w], hi, start=False, stop=last)

            def unit(turn, j, bank, m, hi, lo, ready=None, ready0=0, tiles=None, first=True, last=True):
                pe.wait_ge(lo_done, turn.unit(j) + 1)
                if first:
                    pe.wait_ge(out_free[bank], turn.out(bank, m) + 1)
                tiles = tiles or [(t, t) for t in range(TILES)]
                for n, (t, c) in enumerate(tiles):
                    if ready is not None:
                        pe.wait_ge(ready, ready0 + c + 1)
                    last_mm = exact(ps[bank][:], turn.slot(j), t, hi[:, c, :], lo[:, c, :],
                                    first and n == 0, last and n == len(tiles) - 1)
                last_mm.then_inc(out_ready[bank] if last else slot_inside, 1)

            def unit_pair(turn, hi, lo, ready, ready0, beside=lambda c: None):
                for j in range(2):
                    pe.wait_ge(lo_done, turn.unit(j) + 1)
                    pe.wait_ge(out_free[j], turn.out(j, 0) + 1)
                for c in range(TILES):
                    beside(c)
                    pe.wait_ge(ready, ready0 + c + 1)
                    for j in range(2):
                        last_mm = exact(ps[j][:], turn.slot(j), c, hi[:, c, :], lo[:, c, :], c == 0, c == TILES - 1)
                        if c == TILES - 1:
                            last_mm.then_inc(out_ready[j], 1)

            def stat_chunk(q, c, n):
                pe.wait_ge(sq_ready, q + 1)
                mm(ms[:], ones, sq[:, c % 2, :], start=(c == 0), stop=(c == n - 1)).then_inc(sq_used, 1)

            def keep_clock(n):
                for _ in range(n):
                    mm(ps[4][:], ones, cst[:, 0:T], start=True, stop=True)

            def stat_sum(q_end):
                pe.wait_ge(sq_used, q_end)
                mm(ms[:], ones, diag[:], start=True, stop=True).then_inc(sem("summed"), 1)

            def stat_broadcast(k):
                pe.wait_ge(diag_ready, k + 1)
                mm(rb[:], ones, diag[:], start=True, stop=True).then_inc(rb_ready, 1)

            def early_stats(name):
                q, _ = STATS[name]

                def beside(c):
                    if c < C8 // 2:
                        stat_chunk(q + 2 * c, 2 * c, C8)
                        stat_chunk(q + 2 * c + 1, 2 * c + 1, C8)
                return beside

            pe.wait_ge(sem("const_landed"), 32)
            keep_clock(1)
            stat_sum(STATS["pre1"][0] + C8)
            keep_clock(3)
            stat_broadcast(STATS["pre1"][1])
            keep_clock(2)
            turn = Turn("att_first")
            unit_pair(turn, u_hi, u_lo, u_ready, 0)
            unit(turn, 2, 0, 1, u_hi, u_lo)
            pe.wait_ge(sem("dtw_ready"), 1)
            for t in range(QB):
                rows, dst = slice(t * P, (t + 1) * P), ps[7][:, t * S_HEADS:(t + 1) * S_HEADS]
                for c in range(C8):
                    w = slice(c * S_HEADS, (c + 1) * S_HEADS)
                    mm(dst, u_hi[:, c, rows], dt_hi[:, w], start=(c == 0), stop=False)
                    mm(dst, u_hi[:, c, rows], dt_lo[:, w], start=False, stop=False)
                    last = mm(dst, u_lo[:, c, rows], dt_hi[:, w], start=False, stop=(c == C8 - 1))
            last.then_inc(sem("dt_logits"), 1)

            def attention(turn, i, between):
                def scores(b):
                    h, qb = divmod(b, QB)
                    if b == 0:
                        freed(pe, turn, 0, 0)
                        freed(pe, turn, 1, 0)
                    if b >= 3:
                        pe.wait_ge(sem("logits_done"), i * 8 + (b - 2))
                    rows = slice(h * HEAD, h * HEAD + HEAD)
                    n = (qb + 1) * P
                    mm(ps[3 + b % 3][:, 0:n], q_t[rows, qb * P:(qb + 1) * P], k_t[rows, 0:n],
                       start=True, stop=True).then_inc(sem("scores_ready"), 1)

                def turned(b):
                    pe.wait_ge(sem("probs_ready"), i * 8 + b + 1)
                    if b >= 2:
                        pe.wait_ge(sem("p_t_ready"), i * 8 + (b - 1))
                    if b == 1:
                        pe.wait_ge(sem("v_tok_ready"), i + 1)
                    for kb in range(b % QB + 1):
                        last = nc.tensor.transpose(ps[2 + 4 * (b % 2)][:, kb * P:(kb + 1) * P],
                                                   logits[:, b % 4, kb * P:(kb + 1) * P], ident)
                    last.then_inc(sem("turned"), 1)

                def attended(b):
                    h, qb = divmod(b, QB)
                    pe.wait_ge(sem("p_t_ready"), i * 8 + b + 1)
                    if b == 0:
                        pe.wait_ge(sem("v_tok_ready"), i + 1)
                        pe.wait_ge(sem("dt_read"), 1)
                    for kb in range(qb + 1):
                        last = mm(ps[7][h * HEAD:(h + 1) * HEAD, qb * P:(qb + 1) * P],
                                  v_tok[:, kb, h * HEAD:(h + 1) * HEAD], p_t[:, b % 2, kb, :],
                                  start=(kb == 0), stop=(kb == qb))
                    last.then_inc(sem("attended"), 1)

                for b in range(3):
                    scores(b)
                freed(pe, turn, 0, 1)
                for t in range(QB):
                    last = nc.tensor.transpose(ps[6][:, t * P:(t + 1) * P], v_t[:, t * P:(t + 1) * P], ident)
                last.then_inc(sem("v_turned"), 1)
                for b in range(8):
                    between(b)
                    turned(b)
                    if b + 3 < 8:
                        scores(b + 3)
                    if b >= 1:
                        attended(b - 1)
                attended(7)

            def att_project(turn, slot, i, n, m0, m1):
                bank = n % 2
                if n == 0:
                    pe.wait_ge(lo_done, turn.unit(slot) + 1)
                    pe.wait_ge(sem("att_split"), i + 1)
                pe.wait_ge(out_free[bank], turn.out(bank, (m0, m1)[bank] + n // 2) + 1)
                exact(ps[bank][:], turn.slot(slot), n, s_hi[:, 0, :], s_lo[:, 0, :], True, True)\
                    .then_inc(out_ready[bank], 1)

            attention(turn, 0, lambda b: None)
            with pe.Fori(1, PAIRS) as i:
                turn = Turn("attend", i, 1)
                for j in range(3):
                    unit(turn, j, j % 2, j // 2, u_hi, u_lo)
                attention(turn, i, lambda b: att_project(turn, 3, i - 1, b, 2, 1))
            turn = Turn("att_last")
            pe.wait_ge(sem("la_ready"), 1)
            mm(ps[4][:, 0:P], tri, hd[:, 4, :], start=True, stop=True).then_inc(sem("acs_sum"), 1)
            mm(ps[5][:, 0:P], ones, hd[:, 4, :], start=True, stop=True).then_inc(sem("acs_sum"), 1)
            for n in range(C8):
                att_project(turn, 0, PAIRS - 1, n, 0, 0)
            pe.wait_ge(sem("acs_tok"), 1)
            for t in range(QB):
                last = nc.tensor.transpose(ps[3][0:S_HEADS, t * P:(t + 1) * P], heads_t[:, 1, t, :], ident)
            last.then_inc(sem("acs_turned"), 1)

            q0, k0 = STATS["ssm"]

            def ssm_group(i, between):
                for j in range(2):
                    pe.wait_ge(sem("silu_done"), i * 4 + j + 1)
                    for t in range(QB):
                        last = nc.tensor.transpose(ps[2 + j][:, t * P:(t + 1) * P],
                                                   post[:, j, t * P:(t + 1) * P], ident)
                    last.then_inc(sem("x_turned"), 1)
                pe.wait_ge(sem("silu_done"), i * 4 + 3)
                for t in range(QB):
                    last = nc.tensor.transpose(ps[4][:, t * P:(t + 1) * P], post[:, 2, t * P:(t + 1) * P], ident)
                last.then_inc(sem("b_turned"), 1)
                pe.wait_ge(sem("silu_done"), i * 4 + 4)
                for t in range(QB):
                    w = slice(t * P, (t + 1) * P)
                    last = mm(ps[5][:, w], post[:, 2, w], post[:, 3, w], start=True, stop=True)
                last.then_inc(sem("bc_product"), 1)
                between(0)
                pe.wait_ge(sem("xw_ready"), i * 2 + 2)
                pe.wait_ge(sem("b_tok_ready"), i + 1)
                for c in range(3):
                    last = mm(ps[2 + c // 2][:, c % 2 * 256:c % 2 * 256 + 256], b_tok[:, c, :], xw[:, c, :],
                              start=True, stop=True)
                last.then_inc(sem("state_sums"), 1)
                between(1)
                for h in range(HPG):
                    rows = slice(h % 2 * HEAD, h % 2 * HEAD + HEAD)
                    cols = slice(h * HEAD, h * HEAD + HEAD)
                    pe.wait_ge(sem("kernel_ready"), i * 4 + h + 1)
                    pe.wait_ge(sem("c_decayed"), i * 4 + h + 1)
                    if h == 0:
                        pe.wait_ge(sem("states_ready"), i + 1)
                    for c in range(QB):
                        w = slice(c * P, (c + 1) * P)
                        last = mm(ps[6 + h // 2][rows, w], xd[:, c, cols], decay[:, h, w],
                                  start=True, stop=(c == 0))
                        if c:
                            last = mm(ps[6 + h // 2][rows, w], states[:, c - 1, cols], bc[:, h, w],
                                      start=False, stop=True)
                    last.then_inc(sem("y_done"), 1)
                    if h == 1:
                        between(2)
                between(3)
                stat_sum(i * 2 + (q0 + 2))
                between(4)
                stat_broadcast(i + k0)
                between(5)

            def ssm_project(turn, slot0, i, m0):
                for n in range(C8):
                    bank = n % 2
                    pe.wait_ge(out_free[bank], turn.out(bank, m0 + n // 2) + 1)
                    if n % 4 == 0:
                        pe.wait_ge(lo_done, turn.unit(slot0 + n // 4) + 1)
                    for c in range(2):
                        if n == 0:
                            pe.wait_ge(sem("ssm_split"), i * 2 + c + 1)
                        last = exact(ps[bank][:], turn.slot(slot0 + n // 4), n % 4 * 2 + c, s_hi[:, c, :],
                                     s_lo[:, c, :], c == 0, c == 1)
                    last.then_inc(out_ready[bank], 1)

            def some_unit(turn, count):
                return lambda j: unit(turn, j, j % 2, j // 2, u_hi, u_lo) if j < count else None

            turn = Turn("ssm_first")
            for j in range(6):
                unit(turn, j, j % 2, j // 2, u_hi, u_lo)
            with pe.Fori(0, GROUPS - 1) as i:
                turn = Turn("ssm", i)
                ssm_group(i, some_unit(turn, 6))
                ssm_project(turn, 6, i, 3)
            ssm_group(GROUPS - 1, some_unit(Turn("gates_first"), 4))
            ssm_project(Turn("ssm_last"), 0, GROUPS - 1, 0)

            with pe.Fori(0, 3) as i:
                turn = Turn("gates", i)
                for j in range(4):
                    unit(turn, j, j % 2, j // 2, u_hi, u_lo)

            def outputs_and_norm(name, stat, hi, lo, ready, ready0=0):
                q, k = STATS[stat]
                for i in range(2):
                    turn = Turn(name, i)
                    for j in range(4):
                        c = 4 * i + j
                        if c == 0:
                            unit_pair(turn, hi, lo, ready, ready0)
                            continue
                        if c > 1:
                            unit(turn, j, j % 2, j // 2, hi, lo)
                stat_sum(q + C8)
                keep_clock(3)
                stat_broadcast(k)
                if name != "ple_gate":
                    keep_clock(3)

            outputs_and_norm("mix_out", "post1", v_hi, v_lo, sem("mixed_ready"))

            def ffn_turn(i):
                turn = Turn("ffn", i)
                for j in range(2 if isinstance(i, int) and i == 0 else 0, 8):
                    unit(turn, j, j % 2, j // 2, u_hi, u_lo)
                for j in range(8):
                    unit(turn, 8 + j, j % 2, 4 + j // 2, v_hi, v_lo,
                         sem("hidden_ready") if j == 0 else None, i * 8)

            unit_pair(Turn("ffn"), u_hi, u_lo, u_ready, 8, early_stats("fpre1"))
            ffn_turn(0)
            with pe.Fori(1, 4) as i:
                ffn_turn(i)
            q, k = STATS["fpost1"]
            stat_sum(q + C8)
            keep_clock(3)
            stat_broadcast(k)
            keep_clock(3)

            turn = Turn("glu")
            unit_pair(turn, u_hi, u_lo, u_ready, 16, early_stats("pre2"))
            stat_broadcast(STATS["pre2"][1])
            for j in range(2, 8):
                unit(turn, j, j % 2, j // 2, u_hi, u_lo)
            def retention(i, between):
                last_head = isinstance(i, int)
                q, k = STATS["retain_last"] if last_head else (i + n for n in STATS["retain"])
                turn = Turn("retain", i)
                freed(pe, turn, 0, 0)
                mm(ps[4][:], perm, r_q[:], start=True, stop=True).then_inc(sem("swapped"), 1)
                freed(pe, turn, 1, 0)
                mm(ps[5][:], perm, r_k[:], start=True, stop=True).then_inc(sem("swapped"), 1)
                freed(pe, turn, 0, 1)
                for t in range(QB):
                    last = nc.tensor.transpose(ps[6][:, t * P:(t + 1) * P], r_v[:, t * P:(t + 1) * P], ident)
                last.then_inc(sem("r_v_turned"), 1)
                between(0)
                pe.wait_ge(sem("rotated"), i * 2 + 2)
                for kb in range(QB):
                    n = T - kb * P
                    if kb >= 2:
                        pe.wait_ge(sem("decayed"), i * 4 + (kb - 1))
                    mm(ps[4 + kb % 2][:, 0:n], rot_k[:, kb * P:(kb + 1) * P], rot_q[:, kb * P:T],
                       start=True, stop=True).then_inc(sem("r_scores"), 1)
                between(1)
                pe.wait_ge(sem("r_vtok_ready"), i + 1)
                for kb in range(QB):
                    n = T - kb * P
                    pe.wait_ge(sem("decayed"), i * 4 + kb + 1)
                    last = mm(ps[7][:, kb * P:T], r_vtok[:, kb, :], r_s[:, S_OFF[kb]:S_OFF[kb] + n],
                              start=(kb == 0), stop=(kb == QB - 1), skip_group_check=True)
                last.then_inc(sem("retained"), 1)
                between(2)
                stat_chunk(q, 0, 1)
                between(3)
                stat_broadcast(k)

            turn = Turn("retain")
            for j in range(4):
                unit(turn, j, j % 2, j // 2, u_hi, u_lo)
            with pe.Fori(1, R_HEADS) as i:
                retention(i - 1, some_unit(Turn("retain", i), 4))
            def layer_norm(step):
                q0, k0 = STATS["ln"]
                if step == 0:
                    for c in range(4):
                        pe.wait_ge(sem("conv_done"), c + 1)
                        last = mm(ms[:], ones, cv[:, c, :], start=(c == 0), stop=(c == 3))
                    last.then_inc(sem("mean_sum"), 1)
                    pe.wait_ge(sem("mean_diag"), 1)
                    mm(rb[:], ones, diag[:], start=True, stop=True).then_inc(sem("mean_ready"), 1)
                if step == 2:
                    for c in range(4):
                        stat_chunk(q0 + c, c, 4)
                    pe.wait_ge(sem("ln_diag"), 1)
                    mm(rb[:], ones, diag[:], start=True, stop=True).then_inc(sem("ln_ready"), 1)

            retention(R_HEADS - 1, layer_norm)
            keep_clock(3)
            outputs_and_norm("mix2_out", "post2", v_hi, v_lo, sem("y2_ready"))

            unit_pair(Turn("swiglu"), u_hi, u_lo, u_ready, 24, early_stats("fpre2"))
            stat_broadcast(STATS["fpre2"][1])
            for j in range(2, 4):
                unit(Turn("swiglu"), j, j % 2, j // 2, u_hi, u_lo)
            with pe.Fori(1, H2 // 2) as i:
                turn = Turn("swiglu", i)
                for j in range(4):
                    unit(turn, j, j % 2, j // 2, u_hi, u_lo)
            q, k = STATS["fpost2"]
            for i in range(2):
                turn = Turn("down2", i)
                for n in range(4):
                    for s in range(3):
                        chunks = range(s * TILES, min(H2, (s + 1) * TILES))
                        unit(turn, 3 * n + s, n % 2, n // 2, h_hi, h_lo,
                             sem("hidden2_ready") if (i, n) == (0, 0) else None, 0,
                             [(t, c) for t, c in enumerate(chunks)], first=(s == 0), last=(s == 2))
            stat_sum(q + C8)
            keep_clock(3)
            stat_broadcast(k)
            turn = Turn("ple_proj")
            pe.wait_ge(sem("p_split"), 1)
            for n in range(C8):
                bank = n % 2
                if n % 4 == 0:
                    pe.wait_ge(lo_done, turn.unit(n // 4) + 1)
                pe.wait_ge(out_free[bank], turn.out(bank, n // 2) + 1)
                for c in range(2):
                    last = exact(ps[bank][:], turn.slot(n // 4), n % 4 * 2 + c, s_hi[:, c, :], s_lo[:, c, :],
                                 c == 0, c == 1)
                last.then_inc(out_ready[bank], 1)
            outputs_and_norm("ple_gate", "ple", u_hi, u_lo, u_ready, 32)

        @block.scalar
        def _(act):
            af = nc.scalar.activation

            def split(u, slot):
                if isinstance(u, int):
                    act.wait_ge(landed[slot], 16 * (u // RING + 1))
                else:
                    act.wait_ge(landed[slot], (u - slot) * (16 // RING) + 16)
                af(w_hi[:, slot, :], raw[:, slot, :], ACT.Copy).then_inc(hi_done, 1)

            def ahead(turn, j):
                if isinstance(turn.unit(j), int) and turn.unit(j) + 3 >= SLOTS:
                    return
                if not isinstance(turn.unit(j), int) or turn.unit(j) > 0:
                    ended(act, turn, j - 1)
                split(turn.unit(j + 3), turn.slot(j + 3))

            def ready(turn, bank, m):
                act.wait_ge(out_ready[bank], turn.out(bank, m) + 1)

            def square(q, c, src, wait_all=False):
                if not isinstance(q, int) or q >= 2:
                    act.wait_ge(sq_used, q if wait_all else q - 1)
                return af(sq[:, c % 2, :], src, ACT.Square).then_inc(sq_ready, 1)

            def stat_root(k):
                act.wait_ge(var_ready, k + 1)
                af(tiny[:, 4:8], tiny[:, 0:4], ACT.Sqrt).then_inc(sd_ready, 1)

            def round_u(n0):
                for c in range(C8):
                    act.wait_ge(n_ready, n0 + c + 1)
                    af(u_hi[:, c, :], sq[:, c % 2, :], ACT.Copy).then_inc(u_hi_ready, 1)

            def outputs(turn_name, stat):
                q, k = STATS[stat]
                for i in range(2):
                    turn = Turn(turn_name, i)
                    for j in range(4):
                        ahead(turn, j)
                        ready(turn, j % 2, j // 2)
                        c = 4 * i + j
                        square(q + c, c, ps[j % 2][:])
                        af(y_u[:, c, :], ps[j % 2][:], ACT.Copy).then_inc(out_free[j % 2], 1)
                stat_root(k)

            for c in range(C8):
                if c % 2 == 0:
                    act.wait_ge(x_landed[c // 2], 16)
                square(c, c, xs[:, c, :])
            split(0, 0)
            stat_root(0)
            act.wait_ge(sem("dtw_landed"), 16)
            af(dt_hi, dt_raw[:], ACT.Copy).then_inc(sem("dtw_hi"), 1)
            split(1, 1)
            split(2, 2)
            round_u(0)

            def att_in(turn):
                ahead(turn, 0)
                ready(turn, 0, 0)
                af(k_t[:], ps[0][:], ACT.Copy).then_inc(out_free[0], 1)
                ahead(turn, 1)
                ready(turn, 1, 0)
                af(q_t[:], ps[1][:], ACT.Copy, scale=-float(HEAD) ** -0.5).then_inc(out_free[1], 1)
                ahead(turn, 2)
                ready(turn, 0, 1)
                af(v_t[:], ps[0][:], ACT.Copy).then_inc(out_free[0], 1)

            def attention(i):
                def p_copy(b):
                    act.wait_ge(sem("turned"), i * 8 + b + 1)
                    if b >= 2:
                        act.wait_ge(sem("attended"), i * 8 + (b - 1))
                    n = b % QB + 1
                    af(p_t[:, b % 2, 0:n, :].rearrange("p k t -> p (k t)"), ps[2 + 4 * (b % 2)][:, 0:n * P],
                       ACT.Copy).then_inc(sem("p_t_ready"), 1)

                for b in range(8):
                    n = (b % QB + 1) * P
                    act.wait_ge(sem("logits_done"), i * 8 + b + 1)
                    af(logits[:, b % 4, 0:n], logits[:, b % 4, 0:n], ACT.Exp, scale=-1.0,
                       bias=tiny[:, 8 + b:9 + b], accum_out=tiny[:, 16 + b:17 + b])\
                        .then_inc(sem("exp_done"), 1)
                    if b >= 2:
                        p_copy(b - 2)
                p_copy(6)
                p_copy(7)
                act.wait_ge(sem("attended"), i * 8 + 8)
                af(s_hi[:, 0, :], ps[7][:], ACT.Copy).then_inc(sem("att_hi"), 1)

            att_in(Turn("att_first"))
            attention(0)
            act.wait_ge(sem("dt_abs"), 1)
            af(hd[:, 4, :], hd[:, 3, :], ACT.Exp, scale=-1.0).then_inc(sem("dt_exp"), 1)
            af(hd[:, 7, 0:S_HEADS], v("a_log", 0, S_HEADS), ACT.Exp).then_inc(sem("dt_exp"), 1)
            with act.Fori(1, PAIRS) as i:
                turn = Turn("attend", i, 1)
                att_in(turn)
                ahead(turn, 3)
                attention(i)
            ahead(Turn("att_last"), 0)
            act.wait_ge(sem("dt_to_end"), 1)
            af(hd[:, 5, :], hd[:, 5, :], ACT.Exp).then_inc(sem("dt_exp"), 1)
            act.wait_ge(sem("acs_turned"), 1)
            af(acs_h[:], ps[3][0:S_HEADS, :], ACT.Copy).then_inc(sem("acs_ready"), 1)
            act.wait_ge(sem("acs_ready"), 1)
            act.dma_start(acs_dram, acs_h[:]).then_inc(sem("acs_stored"), 16)

            q0, k0 = STATS["ssm"]
            acs_rows = acs_dram.rearrange("(g h) t -> g h t", h=HPG)

            def to_cat(turn, j):
                ahead(turn, j)
                ready(turn, j % 2, j // 2)
                af(cat[:, j, 3:T + 3], ps[j % 2][:], ACT.Copy).then_inc(out_free[j % 2], 1)

            def z_tanh(turn, j):
                ahead(turn, 4 + j)
                ready(turn, j, 2)
                af(zz[:, j, :], ps[j][:], ACT.Tanh, scale=0.5).then_inc(sem("z_tanh"), 1)

            def tanh_conv(g, j):
                act.wait_ge(sem("conv4_done"), g * 4 + (j + 1))
                if j >= 2:
                    act.wait_ge(sem("silu_done"), g * 4 + (j - 1))
                af(th[:, j % 2, :], post[:, j, :], ACT.Tanh, scale=0.5).then_inc(sem("tanh_done"), 1)

            def to_gate(turn, j):
                ahead(turn, j)
                ready(turn, j % 2, j // 2)
                if turn.slots == 4 and not isinstance(turn.i, int):
                    act.wait_ge(sem("mixed"), turn.i * 2 + (j // 2 + 1))
                    col = turn.i * 2 + (2 + 8 * (j % 2) + j // 2)
                    bias_half = half[:, bass.ds(col, 1)]
                else:
                    bias_half = half[:, 8 * (j % 2) + j // 2:8 * (j % 2) + j // 2 + 1]
                af(gate[:, j, :], ps[j % 2][:], ACT.Tanh, scale=0.5, bias=bias_half).then_inc(out_free[j % 2], 1)

            def load_decays(g):
                act.dma_start(bc[:], acs_rows[g].partition_broadcast(P)).then_inc(sem("bc_landed"), 16)

            def decays_of_head(i, h):
                act.wait_ge(sem("differences"), i * 4 + (h + 1))
                af(decay[:, h, :], decay[:, h, :], ACT.Exp).then_inc(sem("decay_exp"), 1)
                if h == 0:
                    act.wait_ge(sem("ends_done"), i + 1)
                af(bc[:, h, :], bc[:, h, :], ACT.Exp).then_inc(sem("bc_exp"), 1)

            def y_square(i, j):
                act.wait_ge(sem("y_gated"), i * 2 + (j + 1))
                square(i * 2 + (q0 + j), j, y_g[:, j, :])

            def y_high(i):
                for j in range(2):
                    act.wait_ge(sem("y_normed"), i * 2 + (j + 1))
                    af(s_hi[:, j, :], y_g[:, j, :], ACT.Copy).then_inc(sem("ssm_hi"), 1)

            def group_start(i):
                act.wait_ge(sem("bc_landed"), i * 16 + 16)
                af(tiny[:, 24:40].rearrange("p (h c) -> p h c", h=HPG), bc[:, :, P - 1:T:P], ACT.Exp)\
                    .then_inc(sem("ends_done"), 1)
                act.wait_ge(sem("b_turned"), i + 1)
                af(b_tok[:].rearrange("p c n -> p (c n)"), ps[4][:], ACT.Copy).then_inc(sem("b_tok_ready"), 1)

            def first_state(i):
                act.wait_ge(sem("state_sums"), i + 1)
                af(states[:, 0, :], ps[2][:, 0:256], ACT.Copy).then_inc(sem("state0"), 1)

            turn = Turn("ssm_first")
            to_cat(turn, 0)
            act.wait_ge(sem("acs_stored"), 16)
            act.wait_ge(sem("heads_ready"), 1)
            load_decays(0)
            for j in range(1, 4):
                to_cat(turn, j)
                tanh_conv(0, j - 1)
            z_tanh(turn, 0)
            tanh_conv(0, 3)
            z_tanh(turn, 1)
            with act.Fori(0, GROUPS - 1) as i:
                turn = Turn("ssm", i)
                group_start(i)
                decays_of_head(i, 0)
                decays_of_head(i, 1)
                to_cat(turn, 0)
                decays_of_head(i, 2)
                decays_of_head(i, 3)
                first_state(i)
                to_cat(turn, 1)
                y_square(i, 0)
                tanh_conv(i + 1, 0)
                to_cat(turn, 2)
                y_square(i, 1)
                load_decays(i + 1)
                to_cat(turn, 3)
                tanh_conv(i + 1, 1)
                stat_root(i + k0)
                z_tanh(turn, 0)
                y_high(i)
                tanh_conv(i + 1, 2)
                z_tanh(turn, 1)
                tanh_conv(i + 1, 3)
                ahead(turn, 6)
                ahead(turn, 7)
            i, turn = GROUPS - 1, Turn("gates_first")
            group_start(i)
            decays_of_head(i, 0)
            decays_of_head(i, 1)
            to_gate(turn, 0)
            decays_of_head(i, 2)
            decays_of_head(i, 3)
            first_state(i)
            to_gate(turn, 1)
            y_square(i, 0)
            to_gate(turn, 2)
            y_square(i, 1)
            stat_root(i + k0)
            y_high(i)
            to_gate(turn, 3)
            turn = Turn("ssm_last")
            ahead(turn, 0)
            ahead(turn, 1)

            def mixed_high(c):
                for n in range(2):
                    act.wait_ge(sem("mixed"), c + (n + 1))
                    af(v_hi[:, c + n, :], tmp[:, n, :], ACT.Copy).then_inc(sem("mixed_hi"), 1)

            with act.Fori(0, 3) as i:
                turn = Turn("gates", i)
                mixed_high(i * 2)
                for j in range(4):
                    to_gate(turn, j)
            mixed_high(6)

            outputs("mix_out", "post1")

            def squares_and_scaled(name, first_x, n0):
                q, _ = STATS[name]

                def round_scaled(c):
                    act.wait_ge(n_ready, n0 + c + 1)
                    af(u_hi[:, c, :], tmp[:, c % 2, :], ACT.Copy).then_inc(u_hi_ready, 1)

                for c in range(C8):
                    act.wait_ge(x_ready, first_x + c + 1)
                    square(q + c, c, xs[:, c, :])
                    if c:
                        round_scaled(c - 1)
                round_scaled(C8 - 1)

            squares_and_scaled("fpre1", 0, 8)
            act.wait_ge(u_ready, 16)
            act.dma_start(rt[:], ret_tables).then_inc(sem("rt_landed"), 16)
            act.dma_start(p_raw[:], p).then_inc(sem("p_landed"), 16)

            def ffn_up(turn):
                def round_hidden(j):
                    freed(act, turn, j % 2, j // 2)
                    af(v_hi[:, j, :], tmp[:, j % 2, :], ACT.Copy).then_inc(sem("hidden_hi"), 1)

                for j in range(8):
                    ahead(turn, j)
                    ready(turn, j % 2, j // 2)
                    if j >= 2:
                        act.wait_ge(sem("hidden_ready"), turn.i * 8 + (j - 1))
                    af(tmp[:, j % 2, :], ps[j % 2][:], ACT.Relu).then_inc(sem("relu_done"), 1)
                    if j:
                        round_hidden(j - 1)
                round_hidden(7)

            with act.Fori(0, 3) as i:
                turn = Turn("ffn", i)
                ffn_up(turn)
                for j in range(8):
                    ahead(turn, 8 + j)
            turn = Turn("ffn", 3)
            ffn_up(turn)
            q, k = STATS["fpost1"]
            for j in range(8):
                ahead(turn, 8 + j)
                if j >= 1:
                    freed(act, turn, (j - 1) % 2, 4 + (j - 1) // 2)
                    square(q + j - 1, j - 1, ffn_acc[:, j - 1, :])
            act.wait_ge(sem("p_landed"), 16)
            af(s_hi[:], p_raw[:], ACT.Copy).then_inc(sem("p_hi"), 1)
            freed(act, turn, 1, 7)
            square(q + 7, 7, ffn_acc[:, 7, :])
            stat_root(k)
            squares_and_scaled("pre2", 8, 16)
            stat_root(STATS["pre2"][1])

            turn = Turn("glu")
            for n in range(4):
                ahead(turn, 2 * n)
                ready(turn, 0, n)
                af(glu[:, 2 * n, :], ps[0][:], ACT.Copy, scale=0.5).then_inc(out_free[0], 1)
                ahead(turn, 2 * n + 1)
                freed(act, turn, 1, n)
                af(glu[:, 2 * n + 1, :], glu[:, 2 * n + 1, :], ACT.Tanh, scale=0.5).then_inc(sem("glu_tanh"), 1)

            q0, k0 = STATS["retain"]

            def retain_in(turn, j, dst):
                ahead(turn, j)
                ready(turn, j % 2, j // 2)
                if not isinstance(turn.i, int):
                    if j < 2:
                        act.wait_ge(sem("rotated"), turn.i * 2)
                    else:
                        act.wait_ge(sem("r_v_turned"), turn.i)
                af(dst[:], ps[j % 2][:], ACT.Copy).then_inc(out_free[j % 2], 1)

            def retain_gate(turn):
                freed(act, turn, 1, 1)
                af(r_g[:, 0, :], r_g[:, 1, :], ACT.Tanh, scale=0.5).then_inc(sem("r_g_tanh"), 1)

            def values_by_token(head):
                act.wait_ge(sem("r_v_turned"), head + 1)
                af(r_vtok[:].rearrange("p k t -> p (k t)"), ps[6][:], ACT.Copy).then_inc(sem("r_vtok_ready"), 1)

            def retained_root(head):
                act.wait_ge(sem("retained"), head + 1)
                square(head + q0, 0, ps[7][:], wait_all=True)
                stat_root(head + k0)

            def retained_high(head):
                act.wait_ge(sem("ret_normed"), head + 1)
                af(v_hi[:, head + 4, :], r_o[:], ACT.Copy).then_inc(sem("ret_hi"), 1)

            turn = Turn("retain")
            for j, dst in enumerate((r_q, r_k, r_v)):
                retain_in(turn, j, dst)
            ahead(turn, 3)
            retain_gate(turn)
            with act.Fori(1, R_HEADS) as i:
                turn = Turn("retain", i)
                values_by_token(i - 1)
                for j, dst in enumerate((r_q, r_k, r_v)):
                    retain_in(turn, j, dst)
                retained_root(i - 1)
                ahead(turn, 3)
                retained_high(i - 1)
                retain_gate(turn)
            values_by_token(R_HEADS - 1)
            q0, _ = STATS["ln"]
            for c in range(4):
                act.wait_ge(sem("centred"), c + 1)
                if c == 0:
                    act.wait_ge(sq_used, q0)
                square(q0 + c, c, cv[:, c, :])
            act.wait_ge(sem("ln_var"), 1)
            af(tiny[:, 4:8], tiny[:, 0:4], ACT.Sqrt).then_inc(sem("ln_sd"), 1)
            q, k = STATS["retain_last"]
            act.wait_ge(sem("retained"), R_HEADS)
            square(q, 0, ps[7][:], wait_all=True)
            stat_root(k)
            for c in range(4):
                act.wait_ge(sem("ln_scaled"), c + 1)
                if c >= 2:
                    act.wait_ge(sem("conv_silu"), c - 1)
                af(sq[:, c % 2, :], cv[:, c, :], ACT.Tanh).then_inc(sem("ln_tanh"), 1)
                if c:
                    act.wait_ge(sem("conv_silu"), c)
                    af(v_hi[:, c - 1, :], cv[:, c - 1, :], ACT.Copy).then_inc(sem("conv_hi"), 1)
            act.wait_ge(sem("conv_silu"), 4)
            af(v_hi[:, 3, :], cv[:, 3, :], ACT.Copy).then_inc(sem("conv_hi"), 1)
            retained_high(R_HEADS - 1)

            outputs("mix2_out", "post2")
            squares_and_scaled("fpre2", 16, 24)
            stat_root(STATS["fpre2"][1])

            with act.Fori(0, H2 // 2) as i:
                turn = Turn("swiglu", i)
                for n in range(2):
                    ahead(turn, 2 * n)
                    freed(act, turn, 0, n)
                    af(sq[:, 1, :], sq[:, 0, :], ACT.Tanh, scale=0.5).then_inc(sem("gate2_tanh"), 1)
                    ahead(turn, 2 * n + 1)
                    act.wait_ge(sem("hidden2_made"), i * 2 + n + 1)
                    af(h_hi[:, i * 2 + n, :], h_tmp[:], ACT.Copy).then_inc(sem("hidden2_hi"), 1)
            q, k = STATS["fpost2"]
            for i in range(2):
                turn = Turn("down2", i)
                for n in range(4):
                    for s in range(3):
                        ahead(turn, 3 * n + s)
                    ready(turn, n % 2, n // 2)
                    c = 4 * i + n
                    square(q + c, c, ps[n % 2][:])
                    af(y_u[:, c, :], ps[n % 2][:], ACT.Copy).then_inc(out_free[n % 2], 1)
            stat_root(k)
            turn = Turn("ple_proj")
            for n in range(C8):
                if n in (1, 5):
                    ahead(turn, n // 4)
                ready(turn, n % 2, n // 2)
                af(pj[:, n, :], ps[n % 2][:], ACT.Copy).then_inc(out_free[n % 2], 1)
            ahead(turn, 2)
            ahead(turn, 3)
            for c in range(C8):
                act.wait_ge(x_ready, 24 + c + 1)
                af(u_hi[:, c, :], xs[:, c, :], ACT.Copy).then_inc(u_hi_ready, 1)
            q, k = STATS["ple"]
            for i in range(2):
                turn = Turn("ple_gate", i)
                for j in range(4):
                    ahead(turn, j)
                    ready(turn, j % 2, j // 2)
                    c = 4 * i + j
                    if c >= 2:
                        act.wait_ge(sem("e_ready"), c - 1)
                    af(ple_tanh[:, c % 2, :], ps[j % 2][:], ACT.Tanh, scale=0.5).then_inc(out_free[j % 2], 1)
                    if c:
                        act.wait_ge(sem("e_ready"), c)
                        square(q + c - 1, c - 1, pj[:, c - 1, :])
            act.wait_ge(sem("e_ready"), 8)
            square(q + 7, 7, pj[:, 7, :])
            stat_root(k)

        @block.vector
        def _(dve):
            tt, ts, stt = nc.vector.tensor_tensor, nc.vector.tensor_scalar, nc.vector.scalar_tensor_tensor

            def ready(turn, bank, m):
                dve.wait_ge(out_ready[bank], turn.out(bank, m) + 1)

            def means(at, width, eps):
                for t in range(QB):
                    last = nc.vector.tensor_tensor_reduce(
                        out=diag[:, t * P:(t + 1) * P], in0=ms[:, t * P:(t + 1) * P], in1=ident,
                        scale=1.0 / width, scalar=eps, op0=ALU.mult, op1=ALU.add,
                        accum_out=tiny[:, at + t:at + t + 1])
                return last

            def sum_squares(q, c):
                if c == 0:
                    return
                dve.wait_ge(sq_ready, q + (c + 1))
                if c == 1:
                    tt(diag[:], sq[:, 0, :], sq[:, 1, :], ALU.add).then_inc(sq_used, 2)
                else:
                    dve.wait_ge(sq_used, q + c)
                    tt(diag[:], diag[:], sq[:, c % 2, :], ALU.add).then_inc(sq_used, 1)

            def factors(width, eps, q, k, var_sem, sd_sem, diag_sem, summed=None, input_var=None):
                if summed is None:
                    dve.wait_ge(sq_used, q)
                else:
                    dve.wait_ge(sem("summed"), summed + 1)
                nc.vector.memset(tiny[:, 60:61], 0.0)
                if input_var is None:
                    means(0, width, eps).then_inc(var_sem, 1)
                else:
                    means(0, width, 0.0)
                    tt(tiny[:, 52:56], input_var, input_var, ALU.mult)
                    dve.drain()
                    stt(out=tiny[:, 0:4], in0=tiny[:, 52:56], scalar=eps, in1=tiny[:, 0:4],
                        op0=ALU.mult, op1=ALU.add).then_inc(var_sem, 1)
                dve.wait_ge(sd_sem, k + 1)
                nc.vector.reciprocal(tiny[:, 40:44], tiny[:, 4:8])
                dve.drain()
                tt(tiny[:, 52:56], tiny[:, 40:44], tiny[:, 40:44], ALU.mult)
                dve.drain()
                tt(tiny[:, 52:56], tiny[:, 52:56], tiny[:, 0:4], ALU.mult)
                dve.drain()
                ts(tiny[:, 52:56], tiny[:, 52:56], -0.5, 1.5, ALU.mult, ALU.add)
                dve.drain()
                tt(tiny[:, 40:44], tiny[:, 40:44], tiny[:, 52:56], ALU.mult)
                dve.drain()
                for t in range(QB):
                    last = ts(diag[:, t * P:(t + 1) * P], ident, tiny[:, 40 + t:41 + t], None, ALU.mult)
                last.then_inc(diag_sem, 1)

            def stat(name, chunks=C8, i=0, width=D, eps=EPS, input_var=None):
                q, k = STATS[name]
                factors(width, eps, i * chunks + (q + chunks), i + k, var_ready, sd_ready, diag_ready,
                        i + SUMMED[name] if name in SUMMED else None, input_var)
                dve.wait_ge(rb_ready, i + k + 1)

            def pre_norm(name, n0):
                stat(name)

                def rest(c):
                    dve.wait_ge(u_hi_ready, n0 + c + 1)
                    tt(u_lo[:, c, :], sq[:, c % 2, :], u_hi[:, c, :].bitcast(F32), ALU.subtract)\
                        .then_inc(u_ready, 1)

                for c in range(C8):
                    if c >= 2:
                        dve.wait_ge(u_ready, n0 + c - 1)
                    stt(out=sq[:, c % 2, :], in0=xs[:, c, :], scalar=v(name, c), in1=rb[:], op0=ALU.mult,
                        op1=ALU.mult).then_inc(n_ready, 1)
                    if c:
                        rest(c - 1)
                rest(C8 - 1)

            def post_norm(name, y, eps=EPS, done=x_ready, after=None, input_var=None, behind=lambda c: None,
                          skip=()):
                if after:
                    for c in range(C8):
                        sum_squares(STATS[name][0], c)
                    dve.wait_ge(out_free[0], OUT0[after][0] + 1)
                    dve.wait_ge(out_free[1], OUT0[after][1] + 1)
                stat(name, eps=eps, input_var=input_var)
                first = ("post1", "fpost1", "post2", "fpost2", "ple").index(name) * C8

                def add(c):
                    dve.wait_ge(sem("y_scaled"), first + c + 1)
                    tt(xs[:, c, :], xs[:, c, :], y[:, c, :], ALU.add).then_inc(done, 1)

                for c in range(C8):
                    stt(out=y[:, c, :], in0=y[:, c, :], scalar=v(name, c), in1=rb[:], op0=ALU.mult, op1=ALU.mult)\
                        .then_inc(sem("y_scaled"), 1)
                    if c and (c - 1) not in skip:
                        add(c - 1)
                        behind(c - 1)
                if C8 - 1 not in skip:
                    add(C8 - 1)
                    behind(C8 - 1)

            nc.vector.memset(tiny[:], 0.0).then_inc(out_free[0], 1)
            nc.vector.memset(half[:], 0.0).then_inc(out_free[1], 1)
            for c in range(C8):
                sum_squares(STATS["pre1"][0], c)
            dve.wait_ge(sem("const_landed"), 32)
            dve.drain()
            ts(half[:, 0:16], v("gate_b", 0, 16), 0.5, None, ALU.mult)
            ts(half[:, 16:32], v("d_skip", 0, 16), 0.5, None, ALU.mult)
            for landed_x in x_landed:
                dve.wait_ge(landed_x, 16)
            pre_norm("pre1", 0)
            dve.wait_ge(sem("dtw_hi"), 1)
            tt(dt_lo, dt_raw[:], dt_hi.bitcast(F32), ALU.subtract).then_inc(sem("dtw_ready"), 1)
            nc.vector.memset(att_acc[:], 0.0)
            nc.vector.memset(ssm_acc[:], 0.0)
            dve.wait_ge(sem("dist_landed"), 16)

            def by_chunk(row):
                return row.unsqueeze(1).broadcast_to([P, QB, S_HEADS])

            def heads(k):
                return hd[:, k, :].rearrange("p (c h) -> p c h", c=QB)

            def biases(columns):
                for h in range(2):
                    stt(out=bias[:, h, :], in0=dist[:, 0:T], scalar=columns[h], in1=dist[:, T:2 * T],
                        op0=ALU.mult, op1=ALU.add)
                dve.drain()

            def attention(i, between):
                def logit(b):
                    h, qb = divmod(b, QB)
                    n = (qb + 1) * P
                    if b >= 4:
                        dve.wait_ge(sem("turned"), i * 8 + (b - 3))
                    dve.wait_ge(sem("scores_ready"), i * 8 + b + 1)
                    nc.vector.memset(tiny[:, 44 + b:45 + b], 0.0)
                    nc.vector.tensor_tensor_reduce(
                        out=logits[:, b % 4, 0:n], in0=ps[3 + b % 3][:, 0:n], in1=bias[:, h, T - n:T],
                        scale=1.0, scalar=3e38, op0=ALU.add, op1=ALU.min,
                        accum_out=tiny[:, 8 + b:9 + b]).then_inc(sem("logits_done"), 1)

                def normal(b):
                    n = (b % QB + 1) * P
                    dve.wait_ge(sem("exp_done"), i * 8 + b + 1)
                    nc.vector.reciprocal(tiny[:, 44 + b:45 + b], tiny[:, 16 + b:17 + b])
                    dve.drain()
                    ts(logits[:, b % 4, 0:n], logits[:, b % 4, 0:n], tiny[:, 44 + b:45 + b], None, ALU.mult)\
                        .then_inc(sem("probs_ready"), 1)

                for b in range(8):
                    logit(b)
                    if b == 1:
                        dve.wait_ge(sem("v_turned"), i + 1)
                        nc.vector.tensor_copy(v_tok[:].rearrange("p k t -> p (k t)"), ps[6][:])\
                            .then_inc(sem("v_tok_ready"), 1)
                    if b >= 1:
                        normal(b - 1)
                        between(b - 1)
                normal(7)
                between(7)
                dve.wait_ge(sem("att_hi"), i + 1)
                tt(s_lo[:, 0, :], ps[7][:], s_hi[:, 0, :].bitcast(F32), ALU.subtract).then_inc(sem("att_split"), 1)

            def add_output(acc, turn, n, m0, m1):
                bank = n % 2
                ready(turn, bank, (m0, m1)[bank] + n // 2)
                tt(acc[:, n, :], acc[:, n, :], ps[bank][:], ALU.add).then_inc(out_free[bank], 1)

            biases([slopes[:, h:h + 1] for h in range(2)])
            dve.wait_ge(sem("dt_logits"), 1)
            tt(heads(0), ps[7][:, 0:P].rearrange("p (c h) -> p c h", c=QB), by_chunk(v("dt_bias", 0, S_HEADS)),
               ALU.add).then_inc(sem("dt_read"), 1)
            attention(0, lambda b: None)
            ts(hd[:, 1, :], hd[:, 0, :], 0.0, None, ALU.min)
            ts(hd[:, 2, :], hd[:, 0, :], 0.0, None, ALU.max)
            dve.drain()
            tt(hd[:, 3, :], hd[:, 2, :], hd[:, 1, :], ALU.subtract).then_inc(sem("dt_abs"), 1)
            dve.wait_ge(sem("dt_exp"), 2)
            ts(hd[:, 1, :], hd[:, 4, :], 2.0, None, ALU.add)
            dve.drain()
            nc.vector.reciprocal(hd[:, 5, :], hd[:, 1, :])
            dve.drain()
            tt(hd[:, 1, :], hd[:, 4, :], hd[:, 5, :], ALU.mult)
            dve.drain()
            tt(hd[:, 5, :], hd[:, 1, :], hd[:, 1, :], ALU.mult)
            dve.drain()
            ts(hd[:, 0, :], hd[:, 5, :], 1.0 / 17, None, ALU.mult)
            for n in (15, 13, 11, 9, 7, 5, 3):
                dve.drain()
                stt(out=hd[:, 0, :], in0=hd[:, 0, :], scalar=1.0 / n, in1=hd[:, 5, :], op0=ALU.add, op1=ALU.mult)
            dve.drain()
            stt(out=hd[:, 0, :], in0=hd[:, 0, :], scalar=1.0, in1=hd[:, 1, :], op0=ALU.add, op1=ALU.mult)
            dve.drain()
            stt(out=hd[:, 3, :], in0=hd[:, 0, :], scalar=2.0, in1=hd[:, 2, :], op0=ALU.mult, op1=ALU.add)
            dve.drain()
            stt(out=heads(4), in0=heads(3), scalar=-1.0, in1=by_chunk(hd[:, 7, 0:S_HEADS]),
                op0=ALU.mult, op1=ALU.mult).then_inc(sem("la_ready"), 1)
            ts(heads_t[:, 0, :, :], heads(3), 0.125, None, ALU.mult)

            with dve.Fori(1, PAIRS) as i:
                turn = Turn("attend", i, 1)
                dve.drain()
                biases([slopes[:, bass.ds(i * 2 + h, 1)] for h in range(2)])
                attention(i, lambda b: add_output(att_acc, turn, b, 2, 1))
            nc.vector.memset(cat[:, :, 0:3], 0.0)
            dve.wait_ge(sem("acs_sum"), 2)
            nc.vector.tensor_copy(heads_t[:, 1, :, :], ps[4][:, 0:P].rearrange("p (c h) -> p c h", c=QB))\
                .then_inc(sem("acs_tok"), 1)
            dve.wait_ge(sem("acs_tok"), 1)
            tt(heads(5), ps[5][:, 0:P].rearrange("p (c h) -> p c h", c=QB), heads_t[:, 1, :, :], ALU.subtract)\
                .then_inc(sem("dt_to_end"), 1)
            turn = Turn("att_last")
            for n in range(C8):
                add_output(att_acc, turn, n, 0, 0)
            dve.wait_ge(sem("dt_exp"), 3)
            tt(heads_t[:, 2, :, :], heads(5), heads_t[:, 0, :, :], ALU.mult).then_inc(sem("heads_ready"), 1)
            dve.drain()

            q0, k0 = STATS["ssm"]
            cw = VEC["conv4"]

            def silu(g, j):
                dve.wait_ge(sem("tanh_done"), g * 4 + (j + 1))
                stt(out=post[:, j, :], in0=th[:, j % 2, :], scalar=1.0, in1=post[:, j, :],
                    op0=ALU.add, op1=ALU.mult).then_inc(sem("silu_done"), 1)

            def conv4(turn, g, j):
                freed(dve, turn, j % 2, j // 2)

                def weight(t):
                    col = g * (4 * (CONV4 + 1)) + (cw + j * (CONV4 + 1) + t)
                    return vec[:, col:col + 1] if isinstance(g, int) else vec[:, bass.ds(col, 1)]

                ts(post[:, j, :], cat[:, j, 0:T], weight(0), weight(CONV4), ALU.mult, ALU.add)
                for t in range(1, CONV4):
                    dve.drain()
                    last = stt(out=post[:, j, :], in0=cat[:, j, t:t + T], scalar=weight(t), in1=post[:, j, :],
                               op0=ALU.mult, op1=ALU.add)
                last.then_inc(sem("conv4_done"), 1)

            def z_silu(g, j):
                dve.wait_ge(sem("z_tanh"), g * 2 + (j + 1))
                stt(out=zz[:, j, :], in0=zz[:, j, :], scalar=1.0, in1=ps[j][:], op0=ALU.add, op1=ALU.mult)\
                    .then_inc(out_free[j], 1)

            def group_inputs(i):
                def per_head(n, j):
                    at = i * HPG + 2 * j
                    cols = slice(at, at + 2) if isinstance(i, int) else bass.ds(at, 2)
                    return heads_t[:, n, :, cols].unsqueeze(3).broadcast_to([P, QB, 2, HEAD])

                dve.wait_ge(sem("bc_landed"), i * 16 + 16)
                for h in range(HPG):
                    for c in range(QB):
                        w = slice(c * P, (c + 1) * P)
                        at = i * HPG + h
                        own = heads_t[:, 1, c, at:at + 1] if isinstance(i, int) else heads_t[:, 1, c, bass.ds(at, 1)]
                        last = ts(decay[:, h, w], bc[:, h, w], own, 0.0, ALU.subtract, ALU.min)
                    last.then_inc(sem("differences"), 1)
                for j in range(2):
                    dve.wait_ge(sem("x_turned"), i * 2 + (j + 1))
                    src = ps[2 + j][:].rearrange("p (c h f) -> p c h f", c=QB, h=2)
                    cols = slice(j * P, (j + 1) * P)
                    tt(xw[:, :, cols].rearrange("p c (h f) -> p c h f", h=2), src, per_head(2, j), ALU.mult)
                    tt(xd[:, :, cols].rearrange("p c (h f) -> p c h f", h=2), src, per_head(0, j), ALU.mult)\
                        .then_inc(sem("xw_ready"), 1)
                dve.wait_ge(sem("bc_product"), i + 1)
                tt(gm[:], ps[5][:].rearrange("p (c t) -> p c t", c=QB), tri.unsqueeze(1).broadcast_to([P, QB, P]),
                   ALU.mult)
                dve.drain()
                for h in range(HPG):
                    dve.wait_ge(sem("decay_exp"), i * 4 + (h + 1))
                    tt(decay[:, h, :], decay[:, h, :], gm[:].rearrange("p c t -> p (c t)"), ALU.mult)\
                        .then_inc(sem("kernel_ready"), 1)
                    dve.wait_ge(sem("bc_exp"), i * 4 + (h + 1))
                    tt(bc[:, h, :], bc[:, h, :], post[:, 3, :], ALU.mult).then_inc(sem("c_decayed"), 1)
                for c in range(1, 3):
                    dve.drain()
                    if c == 1:
                        dve.wait_ge(sem("state0"), i + 1)
                    for h in range(HPG):
                        cols = slice(h * HEAD, (h + 1) * HEAD)
                        at = c % 2 * 256 + h * HEAD
                        last = stt(out=states[:, c, cols], in0=states[:, c - 1, cols],
                                   scalar=tiny[:, 24 + 4 * h + c:25 + 4 * h + c], in1=ps[2 + c // 2][:, at:at + HEAD],
                                   op0=ALU.mult, op1=ALU.add)
                last.then_inc(sem("states_ready"), 1)

            def y_gate(i, j):
                dve.wait_ge(sem("y_done"), i * 4 + (2 * j + 2))
                at = i * 2 + (16 + j)
                skip = half[:, at:at + 1] if isinstance(i, int) else half[:, bass.ds(at, 1)]
                stt(out=y_g[:, j, :], in0=post[:, j, :], scalar=skip, in1=ps[6 + j][:], op0=ALU.mult, op1=ALU.add)
                dve.drain()
                tt(y_g[:, j, :], y_g[:, j, :], zz[:, j, :], ALU.mult).then_inc(sem("y_gated"), 1)

            def y_sum(i):
                sum_squares(i * 2 + q0, 1)

            def y_norm(i):
                stat("ssm", 2, i, width=2 * P, eps=4 * EPS)
                for j in range(2):
                    at = i * 2 + (VEC["ssm_norm"] + j)
                    scale = vec[:, at:at + 1] if isinstance(i, int) else vec[:, bass.ds(at, 1)]
                    stt(out=y_g[:, j, :], in0=y_g[:, j, :], scalar=scale, in1=rb[:],
                        op0=ALU.mult, op1=ALU.mult).then_inc(sem("y_normed"), 1)

            def y_rest(i):
                for j in range(2):
                    dve.wait_ge(sem("ssm_hi"), i * 2 + (j + 1))
                    tt(s_lo[:, j, :], y_g[:, j, :], s_hi[:, j, :].bitcast(F32), ALU.subtract)\
                        .then_inc(sem("ssm_split"), 1)

            turn = Turn("ssm_first")
            for j in range(4):
                conv4(turn, 0, j)
                if j:
                    silu(0, j - 1)
            silu(0, 3)
            z_silu(0, 0)
            z_silu(0, 1)
            with dve.Fori(0, GROUPS - 1) as i:
                turn = Turn("ssm", i)
                group_inputs(i)
                y_gate(i, 0)
                dve.drain()
                conv4(turn, i + 1, 0)
                y_gate(i, 1)
                dve.drain()
                conv4(turn, i + 1, 1)
                y_sum(i)
                silu(i + 1, 0)
                conv4(turn, i + 1, 2)
                silu(i + 1, 1)
                y_norm(i)
                z_silu(i + 1, 0)
                y_rest(i)
                conv4(turn, i + 1, 3)
                z_silu(i + 1, 1)
                silu(i + 1, 2)
                silu(i + 1, 3)
                for n in range(C8):
                    add_output(ssm_acc, turn, n, 3, 3)
                dve.drain()
            group_inputs(GROUPS - 1)
            y_gate(GROUPS - 1, 0)
            y_gate(GROUPS - 1, 1)
            y_sum(GROUPS - 1)
            y_norm(GROUPS - 1)
            y_rest(GROUPS - 1)
            turn = Turn("ssm_last")
            for n in range(C8):
                add_output(ssm_acc, turn, n, 0, 0)

            def mix(c):
                dve.drain()
                for n in range(2):
                    for j, acc in enumerate((att_acc, ssm_acc)):
                        stt(out=gate[:, 2 * n + j, :], in0=gate[:, 2 * n + j, :], scalar=1.0, in1=acc[:, c + n, :],
                            op0=ALU.add, op1=ALU.mult)
                dve.drain()
                for n in range(2):
                    tt(tmp[:, n, :], gate[:, 2 * n, :], gate[:, 2 * n + 1, :], ALU.add).then_inc(sem("mixed"), 1)
                for n in range(2):
                    dve.wait_ge(sem("mixed_hi"), c + (n + 1))
                    tt(v_lo[:, c + n, :], tmp[:, n, :], v_hi[:, c + n, :].bitcast(F32), ALU.subtract)\
                        .then_inc(sem("mixed_ready"), 1)

            freed(dve, Turn("gates_first"), 0, 1)
            freed(dve, Turn("gates_first"), 1, 1)
            with dve.Fori(0, 3) as i:
                turn = Turn("gates", i)
                mix(i * 2)
                freed(dve, turn, 0, 1)
                freed(dve, turn, 1, 1)
            mix(6)
            dve.drain()

            def scaling(name, first_x, n0):
                def scale(c):
                    dve.wait_ge(x_ready, first_x + c + 1)
                    if c >= 2:
                        dve.wait_ge(u_ready, n0 + c - 1)
                    ts(tmp[:, c % 2, :], xs[:, c, :], v(name, c), None, ALU.mult).then_inc(n_ready, 1)

                def rest(c):
                    dve.wait_ge(u_hi_ready, n0 + c + 1)
                    tt(u_lo[:, c, :], tmp[:, c % 2, :], u_hi[:, c, :].bitcast(F32), ALU.subtract)\
                        .then_inc(u_ready, 1)

                def behind(c):
                    if 1 <= c:
                        scale(c - 1)
                    if 2 <= c:
                        rest(c - 2)
                    if c == C8 - 1:
                        scale(c)
                        rest(c - 1)
                        rest(c)
                return behind

            def keep_scale(name, dst):
                stat(name)
                nc.vector.tensor_copy(dst[:], rb[:])
                dve.drain()

            nc.vector.memset(ffn_acc[:], 0.0)
            post_norm("post1", y_u, eps=4 * EPS, after="ffn", behind=scaling("fpre1", 0, 8))
            dve.wait_ge(sq_used, STATS["fpre1"][0] + C8)
            nc.vector.memset(tiny[:, 60:61], 0.0)
            means(56, D, EPS)
            dve.drain()

            def ffn_turn(i, added=lambda j: None):
                turn = Turn("ffn", i)

                def rest_hidden(j):
                    dve.wait_ge(sem("hidden_hi"), i * 8 + j + 1)
                    tt(v_lo[:, j, :], tmp[:, j % 2, :], v_hi[:, j, :].bitcast(F32), ALU.subtract)\
                        .then_inc(sem("hidden_ready"), 1)

                for j in range(8):
                    dve.wait_ge(sem("relu_done"), i * 8 + j + 1)
                    stt(out=tmp[:, j % 2, :], in0=ps[j % 2][:], scalar=0.0, in1=tmp[:, j % 2, :],
                        op0=ALU.max, op1=ALU.mult).then_inc(out_free[j % 2], 1)
                    if j:
                        rest_hidden(j - 1)
                rest_hidden(7)
                dve.drain()
                for j in range(8):
                    ready(turn, j % 2, 4 + j // 2)
                    tt(ffn_acc[:, j, :], ffn_acc[:, j, :], ps[j % 2][:], ALU.add).then_inc(out_free[j % 2], 1)
                    added(j)

            with dve.Fori(0, 3) as i:
                ffn_turn(i)
            ffn_turn(3, lambda j: sum_squares(STATS["fpost1"][0], j - 1) if j else None)
            sum_squares(STATS["fpost1"][0], 7)
            dve.wait_ge(sem("p_hi"), 1)
            tt(s_lo[:], p_raw[:], s_hi[:].bitcast(F32), ALU.subtract).then_inc(sem("p_split"), 1)
            dve.drain()
            post_norm("fpost1", ffn_acc, input_var=tiny[:, 56:60], behind=scaling("pre2", 8, 16))
            keep_scale("pre2", x_scale)
            nc.vector.tensor_copy(tiny[:, 56:60], tiny[:, 40:44])

            nc.vector.memset(cat31[:, :, 0:CONV31 - 1], 0.0)

            def glu_scale(n):
                ready(Turn("glu"), 1, n)
                tt(glu[:, 2 * n + 1, :], ps[1][:], x_scale[:], ALU.mult).then_inc(out_free[1], 1)

            def glu_product(n):
                freed(dve, Turn("glu"), 0, n)
                dve.wait_ge(sem("glu_tanh"), n + 1)
                stt(out=glu[:, 2 * n, :], in0=glu[:, 2 * n + 1, :], scalar=1.0, in1=glu[:, 2 * n, :],
                    op0=ALU.add, op1=ALU.mult)
                dve.drain()
                tt(cat31[:, n, CONV31 - 1:], glu[:, 2 * n, :], x_scale[:], ALU.mult)

            EARLY = range(0, CONV31 // 2, 2)
            LATE = [t for pair in zip(range(1, CONV31, 2), range(EARLY[-1] + 2, CONV31, 2)) for t in pair]
            LATE += [t for t in range(1, CONV31, 2) if t not in LATE]

            def tap(i, t):
                at = i * (CONV31 + 1) + (VEC["conv31"] + t)
                w = vec[:, at:at + 1] if isinstance(i, int) else vec[:, bass.ds(at, 1)]
                acc = cv_odd[:] if t % 2 else cv[:, i, :]
                if t == 0:
                    return ts(acc, cat31[:, i, 0:T], w, vec[:, at + CONV31:at + CONV31 + 1], ALU.mult, ALU.add)
                if t == 1:
                    return ts(acc, cat31[:, i, 1:T + 1], w, None, ALU.mult)
                return stt(out=acc, in0=cat31[:, i, t:t + T], scalar=w, in1=acc, op0=ALU.mult, op1=ALU.add)

            def early_taps(chunks, before):
                for n, t in enumerate(EARLY):
                    for k, c in enumerate(chunks):
                        if n:
                            dve.wait_ge(sem("early_tap_done"), before + (n - 1) * len(chunks) + k + 1)
                        tap(c, t).then_inc(sem("early_tap_done"), 1)

            def late_taps(i, first, end):
                for n in range(first, end):
                    same = [m for m in range(n) if LATE[m] % 2 == LATE[n] % 2]
                    if same:
                        dve.wait_ge(sem("late_tap_done"), i * len(LATE) + (same[-1] + 1))
                    elif LATE[n] % 2 == 0:
                        dve.wait_ge(sem("early_tap_done"), len(EARLY) * (1 if isinstance(i, int) else 4))
                    elif not isinstance(i, int):
                        dve.wait_ge(sem("conv_done"), i)
                    tap(i, LATE[n]).then_inc(sem("late_tap_done"), 1)

            def conv_sum(i):
                dve.wait_ge(sem("late_tap_done"), i * len(LATE) + len(LATE))
                tt(cv[:, i, :], cv[:, i, :], cv_odd[:], ALU.add).then_inc(sem("conv_done"), 1)

            glu_scale(0)
            glu_product(0)
            dve.drain()
            early_taps([0], 0)
            glu_scale(1)
            late_taps(0, 0, 2)
            glu_product(1)
            late_taps(0, 2, 12)
            glu_scale(2)
            late_taps(0, 12, 14)
            glu_product(2)
            late_taps(0, 14, len(LATE))
            glu_scale(3)
            conv_sum(0)
            glu_product(3)
            dve.drain()
            dve.wait_ge(sem("rt_landed"), 16)
            for k in range(2):
                tt(rt[:, k, :], rt[:, k, :], x_scale[:], ALU.mult)
            dve.drain()

            def rotate(i):
                for j, (src, dst) in enumerate(((r_q, rot_q), (r_k, rot_k))):
                    dve.wait_ge(sem("swapped"), i * 2 + (j + 1))
                    tt(dst[:], src[:], rt[:, 0, :], ALU.mult)
                    tt(rot_s[:, j, :], ps[4 + j][:], rt[:, 1, :], ALU.mult)
                    dve.drain()
                    tt(dst[:], dst[:], rot_s[:, j, :], ALU.add).then_inc(sem("rotated"), 1)

            def decayed(i):
                for kb in range(QB):
                    n = T - kb * P
                    dve.wait_ge(sem("r_scores"), i * 4 + (kb + 1))
                    stt(out=r_s[:, S_OFF[kb]:S_OFF[kb] + n], in0=ps[4 + kb % 2][:, 0:n],
                        scalar=tiny[:, 56 + kb:57 + kb], in1=rt[:, i + 2, 0:n], op0=ALU.mult, op1=ALU.mult)\
                        .then_inc(sem("decayed"), 1)

            def ret_gate(turn):
                ready(turn, 1, 1)
                tt(r_g[:, 1, :], ps[1][:], x_scale[:], ALU.mult).then_inc(out_free[1], 1)

            def ret_factors(turn):
                dve.wait_ge(sem("r_g_tanh"), turn.i + 1)
                stt(out=r_g[:, 0, :], in0=r_g[:, 0, :], scalar=1.0, in1=r_g[:, 1, :], op0=ALU.add, op1=ALU.mult)
                dve.drain()
                q, k = STATS["retain_last"] if isinstance(turn.i, int) else (turn.i + n for n in STATS["retain"])
                factors(P, EPS, q + 1, k, var_ready, sd_ready, diag_ready)

            def ret_norm(i):
                dve.drain()
                dve.wait_ge(rb_ready, i + (STATS["retain"][1] + 1))
                stt(out=r_g[:, 0, :], in0=r_g[:, 0, :], scalar=0.5, in1=rb[:], op0=ALU.mult, op1=ALU.mult)
                dve.drain()
                tt(r_o[:], r_g[:, 0, :], ps[7][:], ALU.mult).then_inc(sem("ret_normed"), 1)
                dve.wait_ge(sem("ret_hi"), i + 1)
                tt(v_lo[:, i + 4, :], r_o[:], v_hi[:, i + 4, :].bitcast(F32), ALU.subtract)\
                    .then_inc(sem("ret_split"), 1)
                dve.drain()

            early_taps([1, 2, 3], len(EARLY))
            ret_gate(Turn("retain"))
            with dve.Fori(1, R_HEADS) as i:
                rotate(i - 1)
                late_taps(i, 0, 3)
                decayed(i - 1)
                late_taps(i, 3, 22)
                ret_factors(Turn("retain", i - 1))
                late_taps(i, 22, len(LATE))
                conv_sum(i)
                ret_norm(i - 1)
                ret_gate(Turn("retain", i))
            rotate(R_HEADS - 1)
            dve.wait_ge(sem("mean_sum"), 1)
            means(40, D_CONV, 0.0)
            dve.drain()
            for t in range(QB):
                last = ts(diag[:, t * P:(t + 1) * P], ident, tiny[:, 40 + t:41 + t], None, ALU.mult)
            last.then_inc(sem("mean_diag"), 1)
            decayed(R_HEADS - 1)
            dve.wait_ge(sem("mean_ready"), 1)
            for c in range(4):
                tt(cv[:, c, :], cv[:, c, :], rb[:], ALU.subtract).then_inc(sem("centred"), 1)
            factors(D_CONV, EPS, STATS["ln"][0] + 4, 0, sem("ln_var"), sem("ln_sd"), sem("ln_diag"))
            dve.wait_ge(sem("ln_ready"), 1)

            def conv_rest(c):
                dve.wait_ge(sem("conv_hi"), c + 1)
                tt(v_lo[:, c, :], cv[:, c, :], v_hi[:, c, :].bitcast(F32), ALU.subtract).then_inc(sem("y2_ready"), 1)

            for c in range(4):
                stt(out=cv[:, c, :], in0=cv[:, c, :], scalar=v("ln_w", c), in1=rb[:], op0=ALU.mult, op1=ALU.mult)
                dve.drain()
                ts(cv[:, c, :], cv[:, c, :], v("ln_b", c), 0.5, ALU.add, ALU.mult).then_inc(sem("ln_scaled"), 1)
            ret_factors(Turn("retain", R_HEADS - 1))
            for c in range(4):
                dve.wait_ge(sem("ln_tanh"), c + 1)
                stt(out=cv[:, c, :], in0=sq[:, c % 2, :], scalar=1.0, in1=cv[:, c, :], op0=ALU.add, op1=ALU.mult)\
                    .then_inc(sem("conv_silu"), 1)
                if c:
                    conv_rest(c - 1)
            conv_rest(3)
            ret_norm(R_HEADS - 1)
            nc.vector.memset(tiny[:, 60:61], 0.0).then_inc(sem("y2_ready"), 4)

            post_norm("post2", y_u, after="swiglu", behind=scaling("fpre2", 16, 24))
            keep_scale("fpre2", h_scale)

            with dve.Fori(0, H2 // 2) as i:
                turn = Turn("swiglu", i)
                for n in range(2):
                    ready(turn, 0, n)
                    tt(sq[:, 0, :], ps[0][:], h_scale[:], ALU.mult).then_inc(out_free[0], 1)
                    dve.wait_ge(sem("gate2_tanh"), i * 2 + n + 1)
                    stt(out=sq[:, 1, :], in0=sq[:, 1, :], scalar=1.0, in1=sq[:, 0, :], op0=ALU.add, op1=ALU.mult)
                    dve.drain()
                    ready(turn, 1, n)
                    tt(sq[:, 1, :], sq[:, 1, :], ps[1][:], ALU.mult).then_inc(out_free[1], 1)
                    dve.drain()
                    stt(out=h_tmp[:], in0=sq[:, 1, :], scalar=0.5, in1=h_scale[:], op0=ALU.mult, op1=ALU.mult)\
                        .then_inc(sem("hidden2_made"), 1)
                    dve.wait_ge(sem("hidden2_hi"), i * 2 + n + 1)
                    tt(h_lo[:, i * 2 + n, :], h_tmp[:], h_hi[:, i * 2 + n, :].bitcast(F32), ALU.subtract)\
                        .then_inc(sem("hidden2_ready"), 1)
                    dve.drain()
            post_norm("fpost2", y_u, after="ple_proj")
            for c in range(C8):
                dve.wait_ge(u_hi_ready, 32 + c + 1)
                tt(u_lo[:, c, :], xs[:, c, :], u_hi[:, c, :].bitcast(F32), ALU.subtract).then_inc(u_ready, 1)
            for c in range(C8):
                freed(dve, Turn("ple_gate", c // 4), c % 2, c % 4 // 2)
                stt(out=pj[:, c, :], in0=ple_tanh[:, c % 2, :], scalar=1.0, in1=pj[:, c, :], op0=ALU.add, op1=ALU.mult)\
                    .then_inc(sem("e_ready"), 1)
                if c:
                    sum_squares(STATS["ple"][0], c - 1)
            sum_squares(STATS["ple"][0], 7)
            post_norm("ple", pj, eps=4 * EPS, done=sem("result_ready"),
                      skip=range(1, C8, 2))


def weight_stream(w):
    w_in, w_att, w_ssm, w_out = w["w_in"][0], w["w_att_proj"][0], w["w_ssm_proj"][0], w["w_out"][0]
    up, down = w["w_up"][0], w["w_down"][0]
    w_in2, w_out2 = w["w_in_2"][0], w["w_out_2"][0]
    gate2, up2, down2 = w["w_ffn_gate_2"][0], w["w_ffn_up_2"][0], w["w_ffn_down_2"][0]
    q0, k0, v0 = 0, ATT_W, 2 * ATT_W
    z0 = 3 * ATT_W
    x0 = z0 + S_INNER
    b0 = x0 + S_INNER
    c0 = b0 + GROUPS * S_STATE
    dt0 = c0 + GROUPS * S_STATE
    g0 = dt0 + S_HEADS
    stream = np.zeros((SLOTS, P, TILES * P), np.float32)
    n = [0]

    def slot(tiles):
        for t, tile in enumerate(tiles):
            stream[n[0], :, t * P:(t + 1) * P] = tile
        n[0] += 1

    def columns(m, c, k0=0, k1=TILES):
        slot([m[k * P:(k + 1) * P, c:c + P] for k in range(k0, k1)])

    def att_in(i):
        for at in (k0, q0, v0):
            columns(w_in, at + i * P)

    def att_out(i):
        slot([w_att[i * P:(i + 1) * P, c * P:(c + 1) * P] for c in range(C8)])

    def group_in(g):
        for at in (x0 + g * 256, x0 + g * 256 + P, b0 + g * P, c0 + g * P, z0 + g * 256, z0 + g * 256 + P):
            columns(w_in, at)

    def group_out(g):
        for m in range(2):
            slot([w_ssm[(2 * g + k) * P:(2 * g + k + 1) * P, c * P:(c + 1) * P]
                  for c in range(4 * m, 4 * m + 4) for k in range(2)])

    def gates(c):
        columns(w_in, g0 + c * P)
        columns(w_in, g0 + D + c * P)

    att_in(0)
    for i in range(1, PAIRS):
        att_in(i)
        att_out(i - 1)
    att_out(PAIRS - 1)
    group_in(0)
    for g in range(GROUPS - 1):
        group_in(g + 1)
        group_out(g)
    gates(0)
    gates(1)
    group_out(GROUPS - 1)
    for c in range(2, C8):
        gates(c)
    for c in range(C8):
        columns(w_out, c * P)
    for i in range(4):
        for c in range(8):
            columns(up, (8 * i + c) * P)
        for c in range(C8):
            columns(down, c * P, 8 * i, 8 * i + 8)
    for c in range(4):
        columns(w_in2, c * P)
        columns(w_in2, D_CONV + c * P)
    for h in range(R_HEADS):
        for part in range(4):
            columns(w_in2, 2 * D_CONV + part * 512 + h * P)
    for c in range(C8):
        columns(w_out2, c * P)
    for c in range(H2):
        columns(gate2, c * P)
        columns(up2, c * P)
    for c in range(C8):
        for s in range(3):
            columns(down2, c * P, 8 * s, min(H2, 8 * s + 8))
    proj = w["w_ple_proj_2"][0]
    for m in range(2):
        slot([proj[k * P:(k + 1) * P, c * P:(c + 1) * P] for c in range(4 * m, 4 * m + 4) for k in range(2)])
    n[0] += 2
    for c in range(C8):
        columns(w["w_ple_gate_2"][0], c * P)
    assert n[0] == SLOTS
    w_dt = w_in[:, dt0:dt0 + S_HEADS].reshape(TILES, P, S_HEADS).transpose(1, 0, 2)
    return stream, np.ascontiguousarray(w_dt.reshape(P, TILES * S_HEADS))



def feature_vectors(w):
    vec = np.zeros((P, NVEC), np.float32)

    def put(name, a, at=0):
        a = a.reshape(-1, P).T
        vec[:, VEC[name] + at:VEC[name] + at + a.shape[1]] = a

    for name, key in (("pre1", "norm_mix_pre_w"), ("post1", "norm_mix_post_w"), ("fpre1", "norm_ffn_pre_w"),
                      ("fpost1", "norm_ffn_post_w"), ("gate_b", "b_gate"), ("ssm_norm", "ssm_norm_w"),
                      ("pre2", "mix_pre_norm_2"), ("post2", "mix_post_norm_2"), ("fpre2", "ffn_pre_norm_2"),
                      ("fpost2", "ffn_post_norm_2"), ("ple", "ple_post_norm_2"),
                      ("ln_w", "conv_ln_w_2"), ("ln_b", "conv_ln_b_2")):
        put(name, w[key][0])
    put("d_skip", np.repeat(w["d_skip"][0], HEAD))
    taps = np.concatenate([w["conv_w"][0], w["conv_b"]])
    for g in range(GROUPS):
        for j, c in enumerate((2 * g, 2 * g + 1, 16 + g, 24 + g)):
            vec[:, VEC["conv4"] + (4 * g + j) * 5:VEC["conv4"] + (4 * g + j + 1) * 5] = taps[:, c * P:(c + 1) * P].T
    taps = np.concatenate([w["conv_dw_w_2"][0], w["conv_dw_b_2"]])
    for c in range(4):
        vec[:, VEC["conv31"] + c * 32:VEC["conv31"] + (c + 1) * 32] = taps[:, c * P:(c + 1) * P].T
    for name in ("dt_bias", "a_log"):
        vec[:, VEC[name]:VEC[name] + S_HEADS] = w[name]
    return vec


def shape_constants():
    i = np.arange(P)
    cst = np.zeros((P, 4 * P + N_HEADS), np.float32)
    cst[:, 0:P] = np.eye(P)
    cst[:, P:2 * P] = 1.0
    cst[:, 2 * P:3 * P] = i[:, None] <= i[None, :]
    cst[i, 3 * P + (i + 64) % P] = 1.0
    small = 2 ** int(np.floor(np.log2(N_HEADS)))

    def powers(m):
        return [2.0 ** (-8.0 / m * (k + 1)) for k in range(m)]

    cst[:, 4 * P:] = np.array(powers(small) + powers(2 * small)[0::2][:N_HEADS - small], np.float32)
    d = i[:, None] - np.arange(T)[None, :] + (T - P)
    times = (d <= 128).astype(int) + (d % 4 == 0) + (d % 16 == 0)
    seen = (d >= 0) & (times > 0)
    tables = np.zeros((P, 2 * T), np.float32)
    tables[:, 0:T] = np.where(seen, d, 0)
    tables[:, T:] = np.where(seen, -np.log(np.maximum(times, 1)), MASKED)
    f = np.float32(10000.0) ** (-np.arange(64, dtype=np.float32) / np.float32(64))
    ang = np.arange(T, dtype=np.float32)[None, :] * np.concatenate([f, f])[:, None].astype(np.float32)
    ret = np.zeros((P, 6, T), np.float32)
    ret[:, 0] = np.cos(ang)
    ret[:, 1] = np.sin(ang) * np.where(i < 64, -1.0, 1.0)[:, None]
    rel = np.arange(T)[None, :] - i[:, None]
    for h in range(R_HEADS):
        log_g = np.log(np.float32(1.0 - 2.0 ** (-5.0 - h)))
        ret[:, 2 + h] = np.where(rel >= 0, np.exp(np.float64(log_g) * np.maximum(rel, 0)), 0.0) * 128.0 ** -0.5
    return cst, tables, ret


def kernel(**inputs):
    from concourse import bacc
    from concourse.bass_utils import run_bass_kernel_spmd

    w = {k: np.asarray(a) for k, a in inputs.items()}
    stream, w_dt = weight_stream(w)
    cst, att_tables, ret_tables = shape_constants()

    def by_feature(a):
        return np.ascontiguousarray(a.T.reshape(-1, P, a.shape[0]).transpose(1, 0, 2))

    arrays = {
        "weights": stream, "w_dt": w_dt, "x": by_feature(w["x"][0]), "p": by_feature(w["p_2"][0, 0]),
        "vectors": feature_vectors(w), "constants": cst, "att_tables": att_tables, "ret_tables": ret_tables,
    }
    nc = bacc.Bacc("TRN2", target_bir_lowering=False, num_devices=1)
    aps = [nc.dram_tensor(k, a.shape, F32, kind="ExternalInput").ap() for k, a in arrays.items()]
    acs = nc.dram_tensor("acs", (S_HEADS, T), F32, kind="Internal").ap()
    out = nc.dram_tensor("out", (P, C8, T), F32, kind="ExternalOutput").ap()
    block_program(nc, *aps, acs, out)
    r = run_bass_kernel_spmd(nc, [arrays], core_ids=[0])
    y = np.asarray(r.results[0]["out"])
    return np.ascontiguousarray(y.transpose(1, 0, 2).reshape(D, T).T)[None]
```
